# Optimizing a Trainium2 kernel written in Bass

```python
import math
import jax
import jax.numpy as jnp
from jax import lax
import numpy as np

D_MODEL = 1024
BATCH = 1
SEQ = 256
DEPTH = 1

D_SSD = D_MODEL
SSD_HEAD_DIM = 64
N_SSD_HEADS = D_SSD // SSD_HEAD_DIM
N_GROUPS = 2
HEADS_PER_GROUP = N_SSD_HEADS // N_GROUPS
D_STATE = 128
SSD_CONV = 4
CHUNK = 128
D_XBC = D_SSD + 2 * N_GROUPS * D_STATE
D_SC = D_MODEL
SC_GROUP_DIM = 64
N_SC_GROUPS = D_SC // SC_GROUP_DIM
SC_CONV = 3
D_MIX = D_SSD + D_SC
PROJ_SPLITS = (D_SSD, D_SSD + D_XBC, D_SSD + D_XBC + N_SSD_HEADS,
               D_SSD + D_XBC + N_SSD_HEADS + D_SC, D_SSD + D_XBC + N_SSD_HEADS + 2 * D_SC)
PROJ_DIM = D_SSD + D_XBC + N_SSD_HEADS + 3 * D_SC
N_EXPERTS = 32
TOP_K = 4
EXPERT_FF = D_MODEL
SWIGLU_LIMIT = 7.0
SWIGLU_ALPHA = 1.702
EXPERT_BLOCK = 256
EPS = 1e-5

kernel_name = 'hybrid_ssd_shortconv_moe'

def rms_norm(x, w):
    xf = x.astype(jnp.float32)
    y = xf * lax.rsqrt(jnp.mean(xf * xf, axis=-1, keepdims=True) + EPS)
    return (y * w.astype(jnp.float32)).astype(x.dtype)

def gated_group_rms_norm(y, z, w, n_groups):
    g = (y * jax.nn.silu(z)).astype(jnp.float32)
    shp = g.shape
    g = g.reshape(*shp[:-1], n_groups, shp[-1] // n_groups)
    g = g * lax.rsqrt(jnp.mean(g * g, axis=-1, keepdims=True) + EPS)
    return (g.reshape(shp) * w.astype(jnp.float32)).astype(y.dtype)

def causal_depthwise_conv(u, w):
    k, c = w.shape
    return lax.conv_general_dilated(
        u, w[:, None, :], window_strides=(1,), padding=[(k - 1, 0)],
        dimension_numbers=('NWC', 'WIO', 'NWC'), feature_group_count=c)

def ssd_chunked_scan(xdt, adt, bm, cm):
    b, s = xdt.shape[:2]
    nc = s // CHUNK

    def to_chunks(t):
        return jnp.moveaxis(t.reshape(b, nc, CHUNK, *t.shape[2:]), 1, 0)

    causal = jnp.tril(jnp.ones((CHUNK, CHUNK), dtype=bool))[None, :, :, None, None]

    def step(state, inp):
        xc, ac, bc, cc = inp
        acum = jnp.cumsum(ac, axis=1)
        seg = acum[:, :, None] - acum[:, None]
        decay_in = jnp.exp(jnp.where(causal, seg, -jnp.inf))
        cb = jnp.einsum('bign,bjgn->bijg', cc, bc)
        y_intra = jnp.einsum('bijg,bijge,bjgep->bigep', cb, decay_in, xc)
        y_inter = jnp.einsum('bign,bgepn->bigep', cc, state) * jnp.exp(acum)[..., None]
        decay_out = jnp.exp(acum[:, -1:] - acum)
        new_state = (state * jnp.exp(acum[:, -1])[..., None, None]
                     + jnp.einsum('bjgn,bjge,bjgep->bgepn', bc, decay_out, xc))
        return new_state, y_intra + y_inter

    state0 = jnp.zeros((b, N_GROUPS, HEADS_PER_GROUP, SSD_HEAD_DIM, D_STATE), jnp.float32)
    _, y = lax.scan(step, state0, (to_chunks(xdt), to_chunks(adt), to_chunks(bm), to_chunks(cm)))
    return jnp.moveaxis(y, 0, 1).reshape(b, s, N_GROUPS, HEADS_PER_GROUP, SSD_HEAD_DIM)

def mixer_block(xn, w_in, ssd_conv_w, ssd_conv_b, dt_bias, a_log, d_skip, ssd_norm_w,
                sc_conv_w, sc_norm_w, w_out):
    b, s, _ = xn.shape
    proj = xn @ w_in
    z, xbc, dt_raw, g_b, g_c, u = jnp.split(proj, PROJ_SPLITS, axis=-1)
    xbc = jax.nn.silu(causal_depthwise_conv(xbc, ssd_conv_w) + ssd_conv_b)
    xs, bs, cs = jnp.split(xbc, [D_SSD, D_SSD + N_GROUPS * D_STATE], axis=-1)
    dt = jax.nn.softplus(dt_raw.astype(jnp.float32) + dt_bias.astype(jnp.float32))
    a = -jnp.exp(a_log.astype(jnp.float32))
    xs_h = xs.astype(jnp.float32).reshape(b, s, N_GROUPS, HEADS_PER_GROUP, SSD_HEAD_DIM)
    dt_h = dt.reshape(b, s, N_GROUPS, HEADS_PER_GROUP)
    y = ssd_chunked_scan(
        xs_h * dt_h[..., None],
        dt_h * a.reshape(N_GROUPS, HEADS_PER_GROUP),
        bs.astype(jnp.float32).reshape(b, s, N_GROUPS, D_STATE),
        cs.astype(jnp.float32).reshape(b, s, N_GROUPS, D_STATE))
    y = y + d_skip.astype(jnp.float32).reshape(N_GROUPS, HEADS_PER_GROUP)[..., None] * xs_h
    y_ssd = gated_group_rms_norm(y.reshape(b, s, D_SSD).astype(xn.dtype), z, ssd_norm_w, N_GROUPS)
    v = causal_depthwise_conv(g_c * u, sc_conv_w)
    y_sc = rms_norm(g_b * v, sc_norm_w)
    return jnp.concatenate([y_ssd, y_sc], axis=-1) @ w_out

def moe_block(xn, w_router, b_router, w_gate_up, b_gate_up, w_down, b_down):
    b, s, d = xn.shape
    t = b * s
    xf = xn.reshape(t, d)
    logits = (xf @ w_router + b_router).astype(jnp.float32)
    top_logit, top_idx = lax.top_k(logits, TOP_K)
    gates = jax.nn.softmax(top_logit, axis=-1)
    n_assign = t * TOP_K
    flat_e = top_idx.reshape(n_assign).astype(jnp.int32)
    flat_tok = jnp.arange(n_assign, dtype=jnp.int32) // TOP_K
    flat_g = gates.reshape(n_assign)
    order = jnp.argsort(flat_e)
    se = flat_e[order]
    counts = jnp.bincount(flat_e, length=N_EXPERTS).astype(jnp.int32)
    starts = jnp.cumsum(counts) - counts
    pcounts = (counts + EXPERT_BLOCK - 1) // EXPERT_BLOCK * EXPERT_BLOCK
    pends = jnp.cumsum(pcounts)
    pstarts = pends - pcounts
    dest = pstarts[se] + jnp.arange(n_assign, dtype=jnp.int32) - starts[se]
    n_rows = n_assign + N_EXPERTS * EXPERT_BLOCK
    n_blocks = n_rows // EXPERT_BLOCK
    row_tok = jnp.zeros((n_rows,), jnp.int32).at[dest].set(flat_tok[order])
    row_gate = jnp.zeros((n_rows,), jnp.float32).at[dest].set(flat_g[order])
    block_start = jnp.arange(n_blocks, dtype=jnp.int32) * EXPERT_BLOCK
    blk_e = jnp.minimum(jnp.searchsorted(pends, block_start, side='right'), N_EXPERTS - 1)

    def expert_block(args):
        tok, g, e = args
        xb = xf[tok]
        gu = xb @ w_gate_up[e] + b_gate_up[e]
        gate, up = gu[:, :EXPERT_FF], gu[:, EXPERT_FF:]
        gate = jnp.minimum(gate, SWIGLU_LIMIT)
        up = jnp.clip(up, -SWIGLU_LIMIT, SWIGLU_LIMIT)
        hid = (up + 1.0) * (gate * jax.nn.sigmoid(SWIGLU_ALPHA * gate))
        out = hid @ w_down[e] + b_down[e]
        return (out * g[:, None]).astype(xf.dtype)

    outs = lax.map(expert_block, (row_tok.reshape(n_blocks, EXPERT_BLOCK),
                                  row_gate.reshape(n_blocks, EXPERT_BLOCK), blk_e))
    y = jnp.zeros_like(xf).at[row_tok].add(outs.reshape(n_rows, d))
    return y.reshape(b, s, d)

def setup_inputs(seed: int = 0) -> dict:
    key = jax.random.key(seed)
    ks = jax.random.split(key, 20)
    L, D, E, F = DEPTH, D_MODEL, N_EXPERTS, EXPERT_FF
    nrm = jax.random.normal
    x = nrm(ks[0], (BATCH, SEQ, D), jnp.float32)
    norm1_w = 1.0 + 0.02 * nrm(ks[1], (L, D), jnp.float32)
    col_scale = jnp.ones((PROJ_DIM,), jnp.float32).at[PROJ_SPLITS[1]:PROJ_SPLITS[2]].set(0.1)
    w_in = nrm(ks[2], (L, D, PROJ_DIM), jnp.float32) * (D ** -0.5) * col_scale
    ssd_conv_w = nrm(ks[3], (L, SSD_CONV, D_XBC), jnp.float32) * (SSD_CONV ** -0.5)
    ssd_conv_b = 0.02 * nrm(ks[4], (L, D_XBC), jnp.float32)
    dt0 = jnp.exp(jax.random.uniform(ks[5], (L, N_SSD_HEADS), jnp.float32,
                                     math.log(1e-3), math.log(1e-1)))
    dt_bias = dt0 + jnp.log(-jnp.expm1(-dt0))
    a_log = jnp.log(jax.random.uniform(ks[6], (L, N_SSD_HEADS), jnp.float32, 1.0, 16.0))
    d_skip = 1.0 + 0.1 * nrm(ks[7], (L, N_SSD_HEADS), jnp.float32)
    ssd_norm_w = 1.0 + 0.02 * nrm(ks[8], (L, D_SSD), jnp.float32)
    sc_conv_w = nrm(ks[9], (L, SC_CONV, D_SC), jnp.float32) * (SC_CONV ** -0.5)
    sc_norm_w = 1.0 + 0.02 * nrm(ks[10], (L, D_SC), jnp.float32)
    w_out = nrm(ks[11], (L, D_MIX, D), jnp.float32) * (D_MIX ** -0.5)
    norm2_w = 1.0 + 0.02 * nrm(ks[12], (L, D), jnp.float32)
    w_router = nrm(ks[13], (L, D, E), jnp.float32) * (D ** -0.5)
    b_router = 0.01 * nrm(ks[14], (L, E), jnp.float32)
    w_gate_up = nrm(ks[15], (L, E, D, 2 * F), jnp.float32) * (D ** -0.5)
    b_gate_up = 0.01 * nrm(ks[16], (L, E, 2 * F), jnp.float32)
    w_down = nrm(ks[17], (L, E, F, D), jnp.float32) * (F ** -0.5)
    b_down = 0.01 * nrm(ks[18], (L, E, D), jnp.float32)
    final_norm_w = 1.0 + 0.02 * nrm(ks[19], (D,), jnp.float32)
    return {'x': x, 'norm1_w': norm1_w, 'w_in': w_in, 'ssd_conv_w': ssd_conv_w,
            'ssd_conv_b': ssd_conv_b, 'dt_bias': dt_bias, 'a_log': a_log, 'd_skip': d_skip,
            'ssd_norm_w': ssd_norm_w, 'sc_conv_w': sc_conv_w, 'sc_norm_w': sc_norm_w,
            'w_out': w_out, 'norm2_w': norm2_w, 'w_router': w_router, 'b_router': b_router,
            'w_gate_up': w_gate_up, 'b_gate_up': b_gate_up, 'w_down': w_down, 'b_down': b_down,
            'final_norm_w': final_norm_w}

def reference(x, norm1_w, w_in, ssd_conv_w, ssd_conv_b, dt_bias, a_log, d_skip, ssd_norm_w,
              sc_conv_w, sc_norm_w, w_out, norm2_w, w_router, b_router, w_gate_up, b_gate_up,
              w_down, b_down, final_norm_w):
    h = x
    for l in range(DEPTH):
        xn = rms_norm(h, norm1_w[l])
        h = h + mixer_block(xn, w_in[l], ssd_conv_w[l], ssd_conv_b[l], dt_bias[l], a_log[l],
                            d_skip[l], ssd_norm_w[l], sc_conv_w[l], sc_norm_w[l], w_out[l])
        xn = rms_norm(h, norm2_w[l])
        h = h + moe_block(xn, w_router[l], b_router[l], w_gate_up[l], b_gate_up[l],
                          w_down[l], b_down[l])
    return rms_norm(h, final_norm_w)


_drawn_inputs = setup_inputs


def setup_inputs(seed=0):
    import zlib

    import numpy as np

    out = dict(_drawn_inputs(seed))
    spreads = {}
    factors = {'b_router': 3.384, 'b_gate_up': 8.0, 'b_down': 8.0, 'final_norm_w': 2.843}
    for name, (base, spread) in spreads.items():
        noise = np.random.default_rng([zlib.crc32(name.encode()), seed]).standard_normal(out[name].shape)
        drawn = base * np.exp(spread * noise) if base else spread * noise
        out[name] = jnp.asarray(drawn.astype(out[name].dtype))
    for name, factor in factors.items():
        out[name] = (out[name] * factor).astype(out[name].dtype)
    return out
```

```python
import concourse.bass as bass
from concourse import mybir
from contextlib import ExitStack

F32 = mybir.dt.float32
I32 = mybir.dt.int32
U32 = mybir.dt.uint32
ALU = mybir.AluOpType
ACT = mybir.ActivationFunctionType
AX = mybir.AxisListType
ds = bass.ds

P = 128
D = 1024
T = 256
TT = T // P
KD = D // P
HEADS = 16
HDIM = D // HEADS
GROUPS = 2
NSTATE = 128
XBC = D + 2 * GROUPS * NSTATE
XT = XBC // P
SSD_TAPS = 4
SC_TAPS = 3
E = 32
TOPK = 4
FF = 1024
EPS = 1e-5
LIMIT = 7.0
SW_ALPHA = 1.702

C_Z, C_XBC = 0, D
C_DT = C_XBC + XBC
C_GB = C_DT + HEADS
C_GC = C_GB + D
C_U = C_GC + D

BLK = 256
A_BLOCKS = XBC // BLK
B_TURNS = D // BLK
WSLOTS = 4

SLOTS = 64
ROUNDS = T // SLOTS
PAIRS = E // 2
RING = 8
CHUNKS = 12
EPAD = E + 2

R_DS = 0
R_N1 = R_DS + KD
R_CW = R_N1 + KD
R_CB = R_CW + SSD_TAPS * XT
R_SCW = R_CB + XT
R_SN = R_SCW + SC_TAPS * KD
R_SCN = R_SN + KD
ROWS = R_SCN + KD


def spread(ap, axis, n):
    shape = list(ap.shape)
    index = [slice(None)] * len(shape)
    index.insert(axis, None)
    shape.insert(axis, n)
    return ap[tuple(index)].broadcast_to(shape)


class Chain:

    def __init__(self, eng, sem):
        self.eng, self.sem, self.n, self.base = eng, sem, 0, 0

    def turn(self, turn, steps):
        self.base, self.n = turn * steps, 0

    def step(self, ins):
        self.n += 1
        ins.then_inc(self.sem, 1)
        self.eng.wait_ge(self.sem, self.base + self.n)


def hybrid_layer(nc, x, norm1_w, w_in, ssd_conv_w, ssd_conv_b, dt_bias, a_log, d_skip, ssd_norm_w,
                 sc_conv_w, sc_norm_w, w_out, norm2_w, w_router, b_router, w_gate_up, b_gate_up,
                 w_down, b_down, final_norm_w, out):
    acum_dram = nc.dram_tensor("acum_scratch", (TT, HEADS, P), F32).ap()

    with ExitStack() as ctx:
        def sb(name, shape, dt=F32):
            return ctx.enter_context(nc.sbuf_tensor(name, shape, dt))

        def sem(name):
            return ctx.enter_context(nc.semaphore(name))

        ring = sb("ring", [P, RING, 4096])
        work = sb("work", [P, 17664])
        ident = sb("ident", [P, P])
        upto = sb("upto", [P, P])
        after = sb("after", [P, P])
        before = sb("before", [P, P])
        ones = sb("ones", [P, P])
        iota = sb("iota", [P, T])
        chan = sb("chan", [P, ROWS])
        small = sb("small", [P, 640])

        used = [0]

        def part(n):
            a = small[:, used[0]:used[0] + n]
            used[0] += n
            return a

        dtb_row = part(HEADS)
        a_row = part(HEADS)
        dt_x = part(TT * HEADS)
        dt_s = part(TT * HEADS)
        dt_y = part(TT * HEADS)
        dtv = part(TT * HEADS)
        adt = part(TT * HEADS)
        acum_j = part(TT * HEADS)
        decay_out = part(HEADS)
        sumsq = part(TT)
        rstd = part(TT)
        mix_ms = part(3 * TT)
        mix_rstd = part(3 * TT)
        br_row = part(E)
        top8 = part(TT * 8)
        negmax = part(TT)
        topi_f = part(TT * 8)
        gsum = part(TT)
        cnt = part(8)
        skip2 = part(2)
        posm = part(TT * EPAD)
        gates = part(TT * EPAD)
        topi = sb("topi", [P, TT, 8], U32)
        overflow = sb("overflow", [P, 1], I32)

        flat = ring[:, :, :].rearrange("p s n -> p (s n)")
        at = [0]

        def scratch(n):
            a = flat[:, at[0]:at[0] + n]
            at[0] += n
            return a

        xn = scratch(TT * D).rearrange("p (t d) -> p t d", t=TT)
        xnT = scratch(KD * T).rearrange("p (k t) -> p k t", k=KD)
        bcT = scratch(4 * T).rearrange("p (n t) -> p n t", n=4)
        zs = scratch(KD * T).rearrange("p (n t) -> p n t", n=KD)
        xdt = scratch(TT * D).rearrange("p (c d) -> p c d", c=TT)
        mt = scratch(TT * HEADS * P).rearrange("p (c e i) -> p c e i", c=TT, e=HEADS)
        cs = scratch(HEADS * P).rearrange("p (e i) -> p e i", e=HEADS)
        xdd = scratch(D)
        btok = scratch(GROUPS * NSTATE)
        state = scratch(D)
        cbt = scratch(TT * GROUPS * P).rearrange("p (c g i) -> p c g i", c=TT, g=GROUPS)
        sig = scratch(2 * T)
        gcs = scratch(2 * T)
        prod = scratch(2 * T)
        conv = scratch(2 * T)
        sq_sc = scratch(KD * T).rearrange("p (n t) -> p n t", n=KD)
        sq_ssd = scratch(KD * T).rearrange("p (n t) -> p n t", n=KD)
        wdt = scratch(KD * HEADS).rearrange("p (k n) -> p k n", k=KD)
        rows = scratch(P)
        acumT = scratch(TT * P)

        wblk = work[:, 0:8192].rearrange("p (s n) -> p s n", s=WSLOTS)
        h = work[:, 8192:10240].rearrange("p (t d) -> p t d", t=TT)
        gsc = work[:, 10240:12288].rearrange("p (n t) -> p n t", n=KD)
        xs = work[:, 12288:14336].rearrange("p (n t) -> p n t", n=KD)
        bgu = work[:, 14336:16384]
        bdn = work[:, 16384:17408]
        wr = work[:, 17408:17664].rearrange("p (k n) -> p k n", k=KD)
        x2 = work[:, 0:2048].rearrange("p (t d) -> p t d", t=TT)
        xsel = work[:, 2048:3072].rearrange("p (k j) -> p k j", k=KD)
        gate = work[:, 3072:4096]
        up = work[:, 4096:5120]
        hid = work[:, 5120:6144]
        hidT = work[:, 6144:7168].rearrange("p (f j) -> p f j", f=KD)
        oute = work[:, 7168:8192]
        x2T = work[:, 3072:5120].rearrange("p (k t) -> p k t", k=KD)
        norm_row = work[:, 10240:11264]
        sel = work[:, 11264:11520].rearrange("p (t j) -> p t j", t=TT)
        selg = work[:, 11520:11776].rearrange("p (t j) -> p t j", t=TT)
        gT = work[:, 11776:12032].rearrange("p (t j) -> p t j", t=TT)
        sele = work[:, 12032:12160]
        mask = work[:, 12288:12288 + TT * E].rearrange("p (t e) -> p t e", t=TT)
        logit = work[:, 12352:12352 + TT * E].rearrange("p (t e) -> p t e", t=TT)
        gatesT = work[:, 12416:12416 + T]
        h_sq = work[:, 13312:14336]

        posm3 = posm.rearrange("p (t e) -> p t e", t=TT)
        gates3 = gates.rearrange("p (t e) -> p t e", t=TT)

        ps = ctx.enter_context(nc.psum_tensor("ps", [P, 8, 512], F32))

        consts_made = sem("consts_made")
        x_loaded = sem("x_loaded")
        rows_loaded = sem("rows_loaded")
        wdt_loaded = sem("wdt_loaded")
        dt_rows_loaded = sem("dt_rows_loaded")
        wblk_full = [sem(f"wblk_full{s}") for s in range(WSLOTS)]
        acum_stored = sem("acum_stored")
        acum_spread = [sem("acum_spread_mt"), sem("acum_spread_cs")]
        moe_params = sem("moe_params")
        norm_row_loaded = sem("norm_row_loaded")
        final_row_loaded = sem("final_row_loaded")
        ring_full = [sem(f"ring_full{s}") for s in range(RING)]
        out_stored = sem("out_stored")
        act_step = sem("act_step")
        dve_step = sem("dve_step")
        pool_step = sem("pool_step")
        sumsq_ready = sem("sumsq_ready")
        meansq_ready = sem("meansq_ready")
        root_ready = sem("root_ready")
        rstd_ready = sem("rstd_ready")
        xn_ready = sem("xn_ready")
        skip_ready = sem("skip_ready")
        chan_ps = sem("chan_ps")
        chan_ready = sem("chan_ready")
        xT_ps = sem("xT_ps")
        xT_dve = sem("xT_dve")
        xT_act = sem("xT_act")
        dt_ps = sem("dt_ps")
        dtx_ready = sem("dtx_ready")
        dt_exp = sem("dt_exp")
        adt_ready = sem("adt_ready")
        acum_ps = sem("acum_ps")
        acumT_ready = sem("acumT_ready")
        decay_ready = sem("decay_ready")
        blk_done = sem("blk_done")
        zs_ready = sem("zs_ready")
        prod_ready = sem("prod_ready")
        conv_tap = sem("conv_tap")
        conv_sum = sem("conv_sum")
        conv_sig = sem("conv_sig")
        xbc_ready = sem("xbc_ready")
        xs_tok_ps = sem("xs_tok_ps")
        xdt_ready = sem("xdt_ready")
        cb_ps = sem("cb_ps")
        cb_taken = sem("cb_taken")
        seg_ready = sem("seg_ready")
        seg_exp = sem("seg_exp")
        cs_exp = sem("cs_exp")
        mt_ready = sem("mt_ready")
        xdd_ready = sem("xdd_ready")
        btok_ready = sem("btok_ready")
        state_ps = sem("state_ps")
        state_ready = sem("state_ready")
        z_sig = sem("z_sig")
        gc_ready = sem("gc_ready")
        sc_ready = sem("sc_ready")
        sc_scaled = sem("sc_scaled")
        y_ps = sem("y_ps")
        g_ready = sem("g_ready")
        g_scaled = sem("g_scaled")
        ms_ps = sem("ms_ps")
        ms_ready = sem("ms_ready")
        ms_root = sem("ms_root")
        mix_ps = sem("mix_ps")
        mix_taken = sem("mix_taken")
        x2_ready = sem("x2_ready")
        x2T_ps = sem("x2T_ps")
        x2T_dve = sem("x2T_dve")
        x2T_act = sem("x2T_act")
        logit_ps = sem("logit_ps")
        max_ready = sem("max_ready")
        exp_ready = sem("exp_ready")
        mask_ready = sem("mask_ready")
        pos_ps = sem("pos_ps")
        route_ready = sem("route_ready")
        gatesT_ps = sem("gatesT_ps")
        gatesT_ready = sem("gatesT_ready")
        seed_ps = sem("seed_ps")
        seed_taken = sem("seed_taken")
        dve_moe = sem("dve_moe")
        sel_ready = sem("sel_ready")
        sele_ready = sem("sele_ready")
        selg_ready = sem("selg_ready")
        gather_ps = sem("gather_ps")
        xsel_ready = sem("xsel_ready")
        chunk_done = sem("chunk_done")
        gate_ready = sem("gate_ready")
        gate_sig = sem("gate_sig")
        hid_ready = sem("hid_ready")
        hidT_ps = sem("hidT_ps")
        hidT_ready = sem("hidT_ready")
        gT_ps = sem("gT_ps")
        gT_ready = sem("gT_ready")
        oute_ready = sem("oute_ready")
        add_ps = sem("add_ps")
        last_sq = sem("last_sq")
        last_ms = sem("last_ms")
        last_root = sem("last_root")
        out_ready = sem("out_ready")

        CONSTS = 6
        ROW_LOADS = 7
        LAST = A_BLOCKS + 4 * B_TURNS
        OUT_BLOCKS = 8
        OUT_ROWS = [D + 256 * i for i in range(4)] + [256 * i for i in range(4)]

        block = ctx.enter_context(nc.Block())

        def flag_set(eng):
            return eng.value_load(overflow[0:1, 0:1], min_val=0, max_val=1) > 0

        @block.sync
        def _(sp):
            def w_in_block(slot, col):
                return sp.dma_start(wblk[:, slot, :].rearrange("p (k n) -> p k n", k=KD),
                                    w_in[:, ds(col, BLK)].rearrange("(k p) n -> p k n", p=P))

            sp.dma_start(h, x.rearrange("(t p) d -> p t d", p=P)).then_inc(x_loaded, 16)
            for b in range(A_BLOCKS):
                if b >= WSLOTS:
                    sp.wait_ge(blk_done, b - WSLOTS + 1)
                w_in_block(b % WSLOTS, C_XBC + BLK * b).then_inc(wblk_full[b % WSLOTS], 16)
            with sp.Fori(0, B_TURNS) as q:
                for j, col in enumerate((C_Z, C_GC, C_U, C_GB)):
                    b = A_BLOCKS + j
                    sp.wait_ge(blk_done, q * 4 + (b - WSLOTS + 1))
                    w_in_block(b % WSLOTS, q * BLK + col).then_inc(wblk_full[b % WSLOTS], 16)
            for i in range(OUT_BLOCKS):
                b = LAST + i
                if i < 7:
                    sp.wait_ge(blk_done, b - WSLOTS + 1)
                else:
                    sp.wait_ge(mix_ps, 4)
                sp.dma_start(wblk[:, b % WSLOTS, :].rearrange("p (k n) -> p k n", k=2),
                             w_out[OUT_ROWS[i]:OUT_ROWS[i] + 2 * P, :].rearrange("(k p) n -> p k n", p=P))\
                    .then_inc(wblk_full[b % WSLOTS], 16)

            def load_chunk(pair, c):
                e = (pair + c // CHUNKS) * 2 + c % 2
                step = c % CHUNKS // 2
                slot = c % RING
                if step < 4:
                    src = w_gate_up[ds(e, 1), step * 256:step * 256 + 256, :]
                    sp.dma_start(ring[:, slot, :].rearrange("p (k n) -> p k n", k=2),
                                 src.rearrange("o (k p) n -> p (o k) n", p=P)).then_inc(ring_full[slot], 16)
                else:
                    step -= 4
                    src = w_down[ds(e, 1), step * 512:step * 512 + 512, :]
                    sp.dma_start(ring[:, slot, :].rearrange("p (k n) -> p k n", k=4),
                                 src.rearrange("o (k p) n -> p (o k) n", p=P)).then_inc(ring_full[slot], 16)

            def load_pass(rnd, first):
                done = rnd * (PAIRS * CHUNKS)
                for c in range(RING):
                    if not first:
                        sp.wait_ge(chunk_done, done + (c - RING + 1))
                    load_chunk(0, c)
                with sp.Fori(0, PAIRS // 2 - 1) as t:
                    for c in range(RING, RING + 2 * CHUNKS):
                        sp.wait_ge(chunk_done, done + t * (2 * CHUNKS) + (c - RING + 1))
                        load_chunk(t * 2, c)
                t = PAIRS // 2 - 1
                for c in range(RING, 2 * CHUNKS):
                    sp.wait_ge(chunk_done, done + (t * 2 * CHUNKS + c - RING + 1))
                    load_chunk(t * 2, c)

            sp.wait_ge(ms_ps, 2)
            load_pass(0, True)
            sp.wait_ge(route_ready, 3)
            with sp.If(flag_set(sp)):
                with sp.Fori(1, ROUNDS) as rnd:
                    load_pass(rnd, False)
            for t in range(TT):
                sp.wait_ge(out_ready, t + 1)
                sp.dma_start(out[t * P:(t + 1) * P, :], h[:, t, :]).then_inc(out_stored, 16)
            sp.wait_ge(out_stored, 16 * TT)

        @block.gpsimd
        def _(pool):
            chain = Chain(pool, pool_step)
            for tile, value in ((ident, 0.0), (upto, 1.0), (after, 1.0), (before, 1.0), (ones, 1.0)):
                chain.step(pool.memset(tile[:, :], value))
            for tile, how, fill, sign in ((ident, ALU.not_equal, 1.0, 1), (upto, ALU.is_ge, 0.0, 1),
                                          (after, ALU.is_gt, 0.0, -1), (before, ALU.is_gt, 0.0, 1)):
                pool.affine_select(out=tile[:, :], in_=tile[:, :], compare_op=how, fill=fill, base=0,
                                   pattern=[[sign, P]], channel_multiplier=-sign).then_inc(consts_made, 1)
            pool.iota(iota[:, :], pattern=[[1, T]], base=0, channel_multiplier=0,
                      allow_small_or_imprecise_dtypes=True).then_inc(consts_made, 1)
            pool.memset(cnt[:, 0:1], 0.0).then_inc(consts_made, 1)
            pool.wait_ge(acumT_ready, 1)
            pool.dma_start(acum_dram.rearrange("c e i -> e c i"),
                           acumT[0:HEADS, :].rearrange("e (c i) -> e c i", c=TT)).then_inc(acum_stored, 16)
            pool.wait_ge(acum_stored, 16)
            pool.dma_start(mt.rearrange("p c e i -> p (c e i)"),
                           acum_dram.rearrange("c e i -> (c e i)").partition_broadcast(P))\
                .then_inc(acum_spread[0], 16)
            pool.dma_start(cs.rearrange("p e i -> p (e i)"),
                           acum_dram[1].rearrange("e i -> (e i)").partition_broadcast(P))\
                .then_inc(acum_spread[1], 16)
            pool.wait_ge(xdt_ready, 2)
            pool.wait_ge(decay_ready, 1)
            pool.tensor_tensor(xdd.rearrange("p (e n) -> p e n", e=HEADS),
                               xdt[:, 0, :].rearrange("p (e n) -> p e n", e=HEADS),
                               spread(decay_out, 2, HDIM), ALU.mult).then_inc(xdd_ready, 1)
            pool.wait_ge(x2_ready, 2)
            pool.dma_start(norm_row, final_norm_w.partition_broadcast(P)).then_inc(final_row_loaded, 16)

        @block.scalar
        def _(act):
            chain = Chain(act, act_step)

            for at_row, src in ((R_N1, norm1_w.rearrange("(n p) -> n p", p=P)),
                                (R_CW, ssd_conv_w.rearrange("w (n p) -> (w n) p", p=P)),
                                (R_CB, ssd_conv_b.rearrange("(n p) -> n p", p=P)),
                                (R_SCW, sc_conv_w.rearrange("w (n p) -> (w n) p", p=P)),
                                (R_SN, ssd_norm_w.rearrange("(n p) -> n p", p=P)),
                                (R_SCN, sc_norm_w.rearrange("(n p) -> n p", p=P))):
                act.dma_start(rows[at_row:at_row + src.shape[0], :], src).then_inc(rows_loaded, 16)
            act.dma_start(skip2[0:KD, :], d_skip.rearrange("(q a) -> q a", a=2)).then_inc(rows_loaded, 16)
            act.dma_start(wdt, w_in[:, C_DT:C_DT + HEADS].rearrange("(k p) n -> p k n", p=P))\
                .then_inc(wdt_loaded, 16)
            act.dma_start(dtb_row, dt_bias.partition_broadcast(P)).then_inc(dt_rows_loaded, 16)
            act.dma_start(a_row, a_log.partition_broadcast(P)).then_inc(dt_rows_loaded, 16)
            act.dma_start(wr, w_router.rearrange("(k p) n -> p k n", p=P)).then_inc(moe_params, 16)
            act.dma_start(br_row, b_router.partition_broadcast(P)).then_inc(moe_params, 16)
            act.dma_start(bdn[0:E, :], b_down).then_inc(moe_params, 16)
            act.dma_start(bgu[0:E, :], b_gate_up).then_inc(moe_params, 16)

            act.wait_ge(x_loaded, 16)
            for t in range(TT):
                ins = act.activation(xn[:, t, :], h[:, t, :], ACT.Square, accum_out=sumsq[:, t:t + 1])
            ins.then_inc(sumsq_ready, 1)
            act.wait_ge(meansq_ready, 1)
            act.activation(rstd, sumsq, ACT.Sqrt).then_inc(root_ready, 1)
            act.wait_ge(rstd_ready, 1)
            act.activation(xn[:, 1, :], h[:, 1, :], ACT.Copy, scale=rstd[:, 1:2]).then_inc(xn_ready, 1)

            act.wait_ge(chan_ready, 1)
            for k in range(KD // 2, KD):
                act.wait_ge(xT_ps, k // 2 + 1)
                act.activation(xnT[:, k, :], ps[:, 4 + k // 2, (k % 2) * T:(k % 2) * T + T], ACT.Copy,
                               scale=chan[:, R_N1 + k:R_N1 + k + 1]).then_inc(xT_act, 1)

            act.wait_ge(dt_rows_loaded, 32)
            chain.step(act.activation(a_row, a_row, ACT.Exp))
            act.wait_ge(dtx_ready, 1)
            act.activation(dt_s, dt_x, ACT.Exp, scale=-1.0).then_inc(dt_exp, 1)

            def conv_block(b):
                for s in range(2):
                    n = 2 * b + s
                    dst = xs[:, n, :] if n < KD else bcT[:, n - KD, :]
                    act.wait_ge(blk_done, b + 1)
                    act.activation(dst, ps[:, b % 4, s * T:s * T + T], ACT.Identity,
                                   scale=chan[:, R_CW + 3 * XT + n:R_CW + 3 * XT + n + 1],
                                   bias=chan[:, R_CB + n:R_CB + n + 1]).then_inc(conv_tap, 1)
                act.wait_ge(conv_sum, b + 1)
                src = xs[:, 2 * b:2 * b + 2, :] if b < 4 else bcT[:, 2 * b - KD:2 * b - KD + 2, :]
                if b > 0:
                    act.wait_ge(xbc_ready, b)
                act.activation(sig.rearrange("p (n t) -> p n t", n=2), src, ACT.Sigmoid).then_inc(conv_sig, 1)

            for b in range(A_BLOCKS):
                conv_block(b)
            act.wait_ge(acumT_ready, 1)
            act.activation(decay_out, ps[:, 5, 32:48], ACT.Exp).then_inc(decay_ready, 1)

            def b_turn(q, bank0):
                act.wait_ge(blk_done, q * 4 + (A_BLOCKS + 1))
                act.wait_ge(zs_ready, q)
                act.activation(sig, ps[:, bank0 % 4, :], ACT.Sigmoid).then_inc(z_sig, 1)
                act.wait_ge(blk_done, q * 4 + (A_BLOCKS + 2))
                act.wait_ge(prod_ready, q)
                act.activation(gcs, ps[:, (bank0 + 1) % 4, :], ACT.Copy).then_inc(gc_ready, 1)
                act.wait_ge(sc_ready, q + 1)
                for s in range(2):
                    act.activation(sq_sc[:, ds(q * 2 + s, 1), :], gsc[:, ds(q * 2 + s, 1), :],
                                   ACT.Square).then_inc(sc_scaled, 1)
                act.wait_ge(sc_scaled, q * 4 + 2)
                for s in range(2):
                    act.activation(gsc[:, ds(q * 2 + s, 1), :], gsc[:, ds(q * 2 + s, 1), :], ACT.Copy,
                                   scale=chan[:, ds(q * 2 + (R_SCN + s), 1)]).then_inc(sc_scaled, 1)

            act.wait_ge(xbc_ready, A_BLOCKS)
            b_turn(0, A_BLOCKS)
            act.wait_ge(cb_ps, 2)
            act.activation(btok, ps[:, 5, 0:GROUPS * NSTATE], ACT.Copy).then_inc(btok_ready, 1)
            for c in range(TT):
                act.wait_ge(seg_ready, c + 1)
                act.activation(mt[:, c], mt[:, c], ACT.Exp).then_inc(seg_exp, 1)
            act.wait_ge(acum_spread[1], 16)
            act.activation(cs, cs, ACT.Exp).then_inc(cs_exp, 1)
            with act.Fori(1, B_TURNS) as q:
                b_turn(q, A_BLOCKS)
            act.wait_ge(state_ps, 1)
            act.activation(state, ps[:, 6:8, :].rearrange("p b n -> p (b n)"), ACT.Copy)\
                .then_inc(state_ready, 1)

            for q in range(KD):
                act.wait_ge(g_ready, q // 2 + 1)
                chain.step(act.activation(sq_ssd[:, q, :], xs[:, q, :], ACT.Square))
                act.activation(xs[:, q, :], xs[:, q, :], ACT.Copy,
                               scale=chan[:, R_SN + q:R_SN + q + 1]).then_inc(g_scaled, 1)
            act.wait_ge(ms_ready, 1)
            act.activation(mix_rstd[:, 0:TT], mix_ms[:, 0:TT], ACT.Sqrt).then_inc(ms_root, 1)
            act.wait_ge(ms_ready, 2)
            act.activation(mix_rstd[:, TT:3 * TT], mix_ms[:, TT:3 * TT], ACT.Sqrt).then_inc(ms_root, 1)

            act.wait_ge(mix_taken, 4)
            act.dma_start(norm_row, norm2_w.partition_broadcast(P)).then_inc(norm_row_loaded, 16)
            act.wait_ge(mix_taken, 12)
            for t in range(TT):
                act.activation(h_sq, h[:, t, :], ACT.Square, accum_out=sumsq[:, t:t + 1])\
                    .then_inc(sumsq_ready, 1)
                act.wait_ge(sumsq_ready, 2 + t)
            act.wait_ge(meansq_ready, 2)
            act.activation(rstd, sumsq, ACT.Sqrt).then_inc(root_ready, 1)
            for k in range(KD // 2, KD):
                act.wait_ge(x2T_ps, k // 2 + 1)
                act.activation(x2T[:, k, :], ps[:, k // 2, (k % 2) * T:(k % 2) * T + T], ACT.Copy)\
                    .then_inc(x2T_act, 1)
            act.wait_ge(max_ready, 1)
            for t in range(TT):
                act.activation(gates3[:, t, 0:E], logit[:, t, :], ACT.Exp, bias=negmax[:, t:t + 1])\
                    .then_inc(exp_ready, 1)
            act.wait_ge(gatesT_ps, 1)
            act.activation(gatesT[0:E, :], ps[0:E, 5, 0:T], ACT.Copy).then_inc(gatesT_ready, 1)

            def take_gathered(g, i):
                act.wait_ge(gather_ps, g + 1)
                act.activation(xsel, ps[:, 4:6, :].rearrange("p b (k j) -> p (b k) j", j=P), ACT.Copy)\
                    .then_inc(xsel_ready, 1)

            def item(i, g):
                for n in range(2):
                    half = slice(n * 512, n * 512 + 512)
                    act.wait_ge(gate_ready, i * 2 + (n + 1))
                    act.activation(hid[:, half], gate[:, half], ACT.Sigmoid, scale=SW_ALPHA)\
                        .then_inc(gate_sig, 1)
                take_gathered(g + 1, i)
                for n in range(2):
                    act.wait_ge(hidT_ps, i * 2 + (n + 1))
                    act.activation(hidT[:, n * 4:n * 4 + 4, :], ps[:, n, :].rearrange("p (f j) -> p f j", j=P),
                                   ACT.Copy).then_inc(hidT_ready, 1)
                act.wait_ge(gT_ps, i + 1)
                act.activation(gT, ps[:, 2, 0:T].rearrange("p (t j) -> p t j", t=TT), ACT.Copy)\
                    .then_inc(gT_ready, 1)
                act.wait_ge(chunk_done, i * CHUNKS + CHUNKS)
                for n in range(2):
                    act.activation(oute[:, n * 512:n * 512 + 512], ps[:, 6 + n, :], ACT.Copy)\
                        .then_inc(oute_ready, 1)

            def expert_pass(rnd):
                take_gathered(rnd * (PAIRS + 1), None)
                with act.Fori(0, PAIRS) as p:
                    item(rnd * PAIRS + p, rnd * (PAIRS + 1) + p)

            expert_pass(0)
            act.wait_ge(route_ready, 3)
            with act.If(flag_set(act)):
                with act.Fori(1, ROUNDS) as rnd:
                    expert_pass(rnd)

            for t in range(TT):
                if t == 0:
                    act.wait_ge(last_ms, 1)
                act.activation(x2[:, t, :], h[:, t, :], ACT.Square, accum_out=sumsq[:, t:t + 1])\
                    .then_inc(last_sq, 1)
            act.wait_ge(last_ms, 2)
            act.activation(rstd, sumsq, ACT.Sqrt).then_inc(last_root, 1)

        @block.vector
        def _(dve):
            chain = Chain(dve, dve_step)

            def sent(ins, sem_, value):
                ins.then_inc(sem_, 1)
                dve.wait_ge(sem_, value)

            dve.wait_ge(rows_loaded, 16 * ROW_LOADS)
            sent(dve.tensor_copy(rows[R_DS:R_DS + KD, :].rearrange("q (a n) -> q a n", a=2),
                                 spread(skip2[0:KD, :], 2, HDIM)), skip_ready, 1)
            dve.wait_ge(sumsq_ready, 1)
            sent(dve.tensor_scalar(sumsq, sumsq, 1.0 / D, EPS, ALU.mult, ALU.add), meansq_ready, 1)
            dve.wait_ge(root_ready, 1)
            sent(dve.reciprocal(rstd, rstd), rstd_ready, 1)
            dve.tensor_scalar(xn[:, 0, :], h[:, 0, :], rstd[:, 0:1], None, ALU.mult).then_inc(xn_ready, 1)
            dve.wait_ge(chan_ps, 1)
            sent(dve.tensor_copy(chan[:, :], ps[:, 0, 0:ROWS]), chan_ready, 1)
            for b in range(2):
                dve.wait_ge(xT_ps, b + 1)
                dve.tensor_tensor(xnT[:, 2 * b:2 * b + 2, :], ps[:, 4 + b, :].rearrange("p (k t) -> p k t", k=2),
                                  spread(chan[:, R_N1 + 2 * b:R_N1 + 2 * b + 2], 2, T), ALU.mult)\
                    .then_inc(xT_dve, 1)

            dve.wait_ge(dt_ps, 1)
            dve.wait_ge(dt_rows_loaded, 32)
            chain.step(dve.tensor_tensor(dt_y.rearrange("p (c e) -> p c e", c=TT),
                                         ps[:, 4, 0:TT * HEADS].rearrange("p (c e) -> p c e", c=TT),
                                         spread(dtb_row, 1, TT), ALU.add))
            chain.step(dve.tensor_scalar(dt_x, dt_y, -1.0, None, ALU.mult))
            sent(dve.tensor_tensor(dt_x, dt_x, dt_y, ALU.max), dtx_ready, 1)
            chain.step(dve.tensor_scalar(dt_y, dt_y, 0.0, None, ALU.max))
            dve.wait_ge(dt_exp, 1)
            chain.step(dve.tensor_scalar(dt_x, dt_s, 2.0, None, ALU.add))
            chain.step(dve.reciprocal(dt_x, dt_x))
            chain.step(dve.tensor_tensor(dt_s, dt_s, dt_x, ALU.mult))
            chain.step(dve.tensor_tensor(dt_x, dt_s, dt_s, ALU.mult))
            terms = list(range(15, 1, -2))
            chain.step(dve.tensor_scalar(dtv, dt_x, 2.0 / 17, None, ALU.mult))
            for n in terms:
                chain.step(dve.scalar_tensor_tensor(out=dtv, in0=dtv, scalar=2.0 / n, in1=dt_x,
                                                    op0=ALU.add, op1=ALU.mult))
            chain.step(dve.scalar_tensor_tensor(out=dtv, in0=dtv, scalar=2.0, in1=dt_s,
                                                op0=ALU.add, op1=ALU.mult))
            chain.step(dve.tensor_tensor(dtv, dtv, dt_y, ALU.add))
            dve.wait_ge(act_step, 1)
            sent(dve.scalar_tensor_tensor(out=adt.rearrange("p (c e) -> p c e", c=TT),
                                          in0=dtv.rearrange("p (c e) -> p c e", c=TT), scalar=-1.0,
                                          in1=spread(a_row, 1, TT), op0=ALU.mult, op1=ALU.mult), adt_ready, 1)

            def conv_block(b):
                for s in range(2):
                    n = 2 * b + s
                    dst = xs[:, n, :] if n < KD else bcT[:, n - KD, :]
                    src = ps[:, b % 4, s * T:s * T + T]
                    dve.wait_ge(conv_tap, 2 * b + 2)
                    for back in range(1, SSD_TAPS):
                        tap = SSD_TAPS - 1 - back
                        ins = dve.scalar_tensor_tensor(
                            out=dst[:, back:], in0=src[:, :T - back],
                            scalar=chan[:, R_CW + tap * XT + n:R_CW + tap * XT + n + 1],
                            in1=dst[:, back:], op0=ALU.mult, op1=ALU.add)
                        if s == 1 and back == SSD_TAPS - 1:
                            sent(ins, conv_sum, b + 1)
                        else:
                            chain.step(ins)
                dst = xs[:, 2 * b:2 * b + 2, :] if b < 4 else bcT[:, 2 * b - KD:2 * b - KD + 2, :]
                dve.wait_ge(conv_sig, b + 1)
                sent(dve.tensor_tensor(dst, dst, sig.rearrange("p (n t) -> p n t", n=2), ALU.mult),
                     xbc_ready, b + 1)

            for b in range(3):
                conv_block(b)
            dve.wait_ge(acum_ps, 1)
            chain.step(dve.tensor_copy(acum_j, ps[:, 5, 0:TT * HEADS]))
            sent(dve.tensor_copy(acumT[0:HEADS, :], ps[0:HEADS, 5, 64:64 + T]), acumT_ready, 1)
            for b in range(3, A_BLOCKS):
                conv_block(b)

            def b_turn(q, bank0):
                two = ds(q * 2, 2)
                dve.wait_ge(z_sig, q + 1)
                sent(dve.tensor_tensor(zs[:, two, :], ps[:, bank0 % 4, :].rearrange("p (n t) -> p n t", n=2),
                                       sig.rearrange("p (n t) -> p n t", n=2), ALU.mult), zs_ready, q + 1)
                dve.wait_ge(gc_ready, q + 1)
                dve.wait_ge(blk_done, q * 4 + (A_BLOCKS + 3))
                sent(dve.tensor_tensor(prod, ps[:, (bank0 + 2) % 4, :], gcs, ALU.mult), prod_ready, q + 1)
                for s in range(2):
                    src, dst = prod[:, s * T:s * T + T], conv[:, s * T:s * T + T]
                    chain.step(dve.tensor_scalar(dst, src, chan[:, ds(q * 2 + (R_SCW + 2 * KD + s), 1)], None, ALU.mult))
                    for back in range(1, SC_TAPS):
                        tap = SC_TAPS - 1 - back
                        chain.step(dve.scalar_tensor_tensor(
                            out=dst[:, back:], in0=src[:, :T - back],
                            scalar=chan[:, ds(q * 2 + (R_SCW + tap * KD + s), 1)],
                            in1=dst[:, back:], op0=ALU.mult, op1=ALU.add))
                dve.wait_ge(blk_done, q * 4 + (A_BLOCKS + 4))
                sent(dve.tensor_tensor(gsc[:, two, :], ps[:, (bank0 + 3) % 4, :].rearrange("p (n t) -> p n t", n=2),
                                       conv.rearrange("p (n t) -> p n t", n=2), ALU.mult), sc_ready, q + 1)

            b_turn(0, A_BLOCKS)
            for c in range(TT):
                for n in range(2):
                    dve.wait_ge(xs_tok_ps, 2 * c + n + 1)
                    heads = slice(c * HEADS + 8 * n, c * HEADS + 8 * n + 8)
                    sent(dve.tensor_tensor(xdt[:, c, n * 512:n * 512 + 512].rearrange("p (e d) -> p e d", e=8),
                                           ps[:, 4 + 2 * c + n, :].rearrange("p (e d) -> p e d", e=8),
                                           spread(dtv[:, heads], 2, HDIM), ALU.mult), xdt_ready, 2 * c + n + 1)
            for c in range(TT):
                dve.wait_ge(acum_spread[0], 16)
                chain.step(dve.tensor_tensor(mt[:, c], mt[:, c],
                                             spread(acum_j[:, c * HEADS:c * HEADS + HEADS], 2, P), ALU.subtract))
                sent(dve.tensor_scalar(mt[:, c], mt[:, c], 0.0, None, ALU.min), seg_ready, c + 1)
            dve.wait_ge(cb_ps, 1)
            sent(dve.tensor_tensor(cbt.rearrange("p c g i -> p (c g) i"),
                                   ps[:, 4, :].rearrange("p (n i) -> p n i", i=P),
                                   spread(upto[:, :], 1, TT * GROUPS), ALU.mult), cb_taken, 1)
            n = 0
            for c in range(TT):
                dve.wait_ge(seg_exp, c + 1)
                for g in range(GROUPS):
                    n += 1
                    sent(dve.tensor_tensor(mt[:, c, 8 * g:8 * g + 8, :], mt[:, c, 8 * g:8 * g + 8, :],
                                           spread(cbt[:, c, g, :], 1, 8), ALU.mult), mt_ready, n)
            dve.wait_ge(cs_exp, 1)
            for g in range(GROUPS):
                n += 1
                sent(dve.tensor_tensor(cs[:, 8 * g:8 * g + 8, :], cs[:, 8 * g:8 * g + 8, :],
                                       spread(bcT[:, 2 + g, P:2 * P], 1, 8), ALU.mult), mt_ready, n)
            before_loop = chain.n
            TURN_STEPS = 2 * SC_TAPS
            with dve.Fori(1, B_TURNS) as q:
                chain.turn(q, TURN_STEPS)
                chain.base = chain.base + (before_loop - TURN_STEPS)
                b_turn(q, A_BLOCKS)
                assert chain.n == TURN_STEPS
            chain.base, chain.n = before_loop + TURN_STEPS * (B_TURNS - 1), 0

            dve.wait_ge(ms_ps, 1)
            sent(dve.tensor_scalar(mix_ms[:, 0:TT], ps[:, 0, 0:TT], 1.0 / D, EPS, ALU.mult, ALU.add), ms_ready, 1)
            for b in range(4):
                dve.wait_ge(y_ps, b + 1)
                for s in range(2):
                    n = 2 * b + s
                    chain.step(dve.scalar_tensor_tensor(
                        out=xs[:, n, :], in0=xs[:, n, :], scalar=chan[:, R_DS + n:R_DS + n + 1],
                        in1=ps[:, 4 + b, s * T:s * T + T], op0=ALU.mult, op1=ALU.add))
                sent(dve.tensor_tensor(xs[:, 2 * b:2 * b + 2, :], xs[:, 2 * b:2 * b + 2, :],
                                       zs[:, 2 * b:2 * b + 2, :], ALU.mult), g_ready, b + 1)
            dve.wait_ge(ms_root, 1)
            chain.step(dve.reciprocal(mix_rstd[:, 0:TT], mix_rstd[:, 0:TT]))

            def add_group(g, bank0):
                for n in range(4):
                    t, half = divmod(3 - n, 2)
                    dve.wait_ge(mix_ps, 4 * g + n + 1)
                    cols = slice(half * 512, half * 512 + 512)
                    sent(dve.scalar_tensor_tensor(out=h[:, t, cols], in0=ps[:, bank0 + 3 - n, :],
                                                  scalar=mix_rstd[:, 2 * g + t:2 * g + t + 1],
                                                  in1=h[:, t, cols], op0=ALU.mult, op1=ALU.add),
                         mix_taken, 4 * g + n + 1)

            dve.wait_ge(ms_ps, 2)
            sent(dve.tensor_scalar(mix_ms[:, TT:3 * TT], ps[:, 4, 0:2 * TT], 1.0 / 512, EPS, ALU.mult, ALU.add),
                 ms_ready, 2)
            add_group(0, 0)
            dve.wait_ge(ms_root, 2)
            chain.step(dve.reciprocal(mix_rstd[:, TT:3 * TT], mix_rstd[:, TT:3 * TT]))
            add_group(1, 4)
            add_group(2, 0)

            dve.wait_ge(sumsq_ready, 3)
            sent(dve.tensor_scalar(sumsq, sumsq, 1.0 / D, EPS, ALU.mult, ALU.add), meansq_ready, 2)
            dve.wait_ge(root_ready, 2)
            sent(dve.reciprocal(rstd, rstd), rstd_ready, 2)
            dve.wait_ge(norm_row_loaded, 16)
            for t in range(TT):
                sent(dve.scalar_tensor_tensor(out=x2[:, t, :], in0=h[:, t, :], scalar=rstd[:, t:t + 1],
                                              in1=norm_row, op0=ALU.mult, op1=ALU.mult), x2_ready, t + 1)
            for b in range(2):
                dve.wait_ge(x2T_ps, b + 1)
                dve.tensor_copy(x2T[:, 2 * b:2 * b + 2, :], ps[:, b, :].rearrange("p (k t) -> p k t", k=2))\
                    .then_inc(x2T_dve, 1)

            dve.wait_ge(moe_params, 64)
            dve.wait_ge(logit_ps, 1)
            chain.step(dve.tensor_tensor(logit, ps[:, 4, 0:TT * E].rearrange("p (t e) -> p t e", t=TT),
                                         spread(br_row, 1, TT), ALU.add))
            for t in range(TT):
                chain.step(dve.max(top8[:, 8 * t:8 * t + 8], logit[:, t, :]))
            sent(dve.tensor_scalar(negmax.rearrange("p (t o) -> p t o", o=1),
                                   top8.rearrange("p (t n) -> p t n", n=8)[:, :, 0:1], -1.0, None, ALU.mult),
                 max_ready, 1)
            for t in range(TT):
                chain.step(dve.max_index(topi[:, t, :], top8[:, 8 * t:8 * t + 8], logit[:, t, :]))
            chain.step(dve.tensor_copy(topi_f, topi[:, :, :].rearrange("p t n -> p (t n)")))
            for t in range(TT):
                chain.step(dve.tensor_scalar(mask[:, t, :], iota[:, 0:E], topi_f[:, 8 * t:8 * t + 1], None,
                                             ALU.is_equal))
                for n in range(1, TOPK):
                    ins = dve.scalar_tensor_tensor(out=mask[:, t, :], in0=iota[:, 0:E],
                                                   scalar=topi_f[:, 8 * t + n:8 * t + n + 1],
                                                   in1=mask[:, t, :], op0=ALU.is_equal, op1=ALU.add)
                    if n == TOPK - 1:
                        sent(ins, mask_ready, t + 1)
                    else:
                        chain.step(ins)
            dve.wait_ge(exp_ready, 2)
            chain.step(dve.memset(gates3[:, :, E:EPAD], 0.0))
            chain.step(dve.tensor_tensor(gates3[:, :, 0:E], gates3[:, :, 0:E], mask, ALU.mult))
            chain.step(dve.tensor_reduce(gsum, gates3[:, :, 0:E], AX.X, ALU.add))
            chain.step(dve.reciprocal(gsum, gsum))
            sent(dve.tensor_tensor(gates3[:, :, 0:E], gates3[:, :, 0:E], spread(gsum, 2, E), ALU.mult),
                 route_ready, 1)
            dve.wait_ge(pos_ps, 1)
            chain.step(dve.memset(posm3[:, :, E:EPAD], -1.0))
            chain.step(dve.scalar_tensor_tensor(out=posm3[:, :, 0:E],
                                                in0=ps[:, 6, 0:TT * E].rearrange("p (t e) -> p t e", t=TT),
                                                scalar=1.0, in1=mask, op0=ALU.add, op1=ALU.mult))
            sent(dve.tensor_scalar(posm3[:, :, 0:E], posm3[:, :, 0:E], -1.0, None, ALU.add), route_ready, 2)
            chain.step(dve.tensor_reduce(cnt[:, 1:2], ps[:, 6, TT * E:TT * E + E], AX.X, ALU.max))
            sent(dve.tensor_scalar(overflow[:, :], cnt[:, 1:2], float(SLOTS), None, ALU.is_gt), route_ready, 3)

            moe = Chain(dve, dve_moe)
            ITEM_STEPS = 8
            quad = "p t (a j) -> p t a j"

            def build_sel(g, p, rnd):
                if not isinstance(g, int):
                    dve.wait_ge(gather_ps, g)
                slots = iota[:, ds(rnd * SLOTS, SLOTS)]
                sent(dve.tensor_tensor(sel.rearrange(quad, a=2), spread(spread(slots, 1, 2), 1, TT),
                                       spread(posm3[:, :, ds(p * 2, 2)], 3, SLOTS), ALU.is_equal),
                     sel_ready, g + 1)

            def build_sele(g, p):
                dve.tensor_copy(sele[0:E, :].rearrange("p (a j) -> p a j", a=2),
                                spread(ident[0:E, ds(p * 2, 2)], 2, SLOTS)).then_inc(sele_ready, 1)

            def item(i, g, p, rnd):
                moe.turn(i, ITEM_STEPS)
                build_sel(g + 1, p + 1, rnd)
                slots = iota[:, ds(rnd * SLOTS, SLOTS)]
                moe.step(dve.tensor_tensor(selg.rearrange(quad, a=2), spread(spread(slots, 1, 2), 1, TT),
                                           spread(posm3[:, :, ds(p * 2, 2)], 3, SLOTS), ALU.is_equal))
                sent(dve.tensor_tensor(selg.rearrange(quad, a=2), selg.rearrange(quad, a=2),
                                       spread(gates3[:, :, ds(p * 2, 2)], 3, SLOTS), ALU.mult),
                     selg_ready, i + 1)
                dve.wait_ge(chunk_done, i * CHUNKS + 8)
                for n in range(2):
                    sent(dve.tensor_scalar(gate[:, n * 512:n * 512 + 512], ps[:, n, :], LIMIT, None, ALU.min),
                         gate_ready, i * 2 + (n + 1))
                moe.step(dve.tensor_scalar(up, ps[:, 2:4, :].rearrange("p b n -> p (b n)"), LIMIT, -LIMIT,
                                           ALU.min, ALU.max))
                for n in range(2):
                    half = slice(n * 512, n * 512 + 512)
                    dve.wait_ge(gate_sig, i * 2 + (n + 1))
                    moe.step(dve.tensor_tensor(gate[:, half], gate[:, half], hid[:, half], ALU.mult))
                    sent(dve.scalar_tensor_tensor(out=hid[:, half], in0=up[:, half], scalar=1.0,
                                                  in1=gate[:, half], op0=ALU.add, op1=ALU.mult),
                         hid_ready, i * 2 + (n + 1))
                build_sele(g + 1, p + 1)
                for n in range(4):
                    half, t = divmod(n, 2)
                    cols = slice(half * 512, half * 512 + 512)
                    dve.wait_ge(add_ps, i * 4 + (n + 1))
                    moe.step(dve.tensor_tensor(h[:, t, cols], h[:, t, cols], ps[:, [6, 7, 4, 5][n], :], ALU.add))
                assert moe.n == ITEM_STEPS

            def expert_pass(rnd):
                g = rnd * (PAIRS + 1)
                build_sel(g, 0, rnd)
                build_sele(g, 0)
                with dve.Fori(0, PAIRS) as p:
                    item(rnd * PAIRS + p, g + p, p, rnd)

            for n in range(4):
                t, half = divmod(n, 2)
                cols = slice(half * 512, half * 512 + 512)
                dve.wait_ge(seed_ps, n + 1)
                sent(dve.tensor_tensor(h[:, t, cols], h[:, t, cols], ps[:, n, :], ALU.add), seed_taken, n + 1)
            expert_pass(0)
            with dve.If(flag_set(dve)):
                with dve.Fori(1, ROUNDS) as rnd:
                    expert_pass(rnd)

            sent(dve.memset(cnt[:, 3:4], 0.0), last_ms, 1)
            dve.wait_ge(last_sq, 2)
            sent(dve.tensor_scalar(sumsq, sumsq, 1.0 / D, EPS, ALU.mult, ALU.add), last_ms, 2)
            dve.wait_ge(last_root, 1)
            sent(dve.reciprocal(rstd, rstd), rstd_ready, 3)
            dve.wait_ge(final_row_loaded, 16)
            for t in range(TT):
                dve.scalar_tensor_tensor(out=h[:, t, :], in0=h[:, t, :], scalar=rstd[:, t:t + 1],
                                         in1=norm_row, op0=ALU.mult, op1=ALU.mult).then_inc(out_ready, 1)

        @block.tensor
        def _(pe):
            pe.wait_ge(consts_made, CONSTS)
            pe.wait_ge(rows_loaded, 16 * ROW_LOADS)
            pe.wait_ge(skip_ready, 1)
            pe.transpose(ps[:, 0, 0:ROWS], rows[0:ROWS, :], ident[0:ROWS, 0:ROWS]).then_inc(chan_ps, 1)
            pe.wait_ge(xn_ready, 2)
            for k in range(KD):
                for t in range(TT):
                    mm = pe.transpose(ps[:, 4 + k // 2, (k % 2) * T + t * P:(k % 2) * T + t * P + P],
                                      xn[:, t, k * P:k * P + P], ident[:, :])
                if k % 2:
                    mm.then_inc(xT_ps, 1)
            pe.wait_ge(xT_dve, 2)
            pe.wait_ge(xT_act, 4)
            pe.wait_ge(wdt_loaded, 16)
            for t in range(TT):
                for k in range(KD):
                    mm = pe.matmul(ps[:, 4, t * HEADS:t * HEADS + HEADS], xnT[:, k, t * P:t * P + P],
                                   wdt[:, k, :], start=(k == 0), stop=(k == KD - 1))
            mm.then_inc(dt_ps, 1)

            def w_in_block(slot, use, bank):
                pe.wait_ge(wblk_full[slot], use * 16 + 16)
                w = wblk[:, slot, :].rearrange("p (k n) -> p k n", k=KD)
                for s in range(2):
                    for k in range(KD):
                        mm = pe.matmul(ps[:, bank, s * T:s * T + T], w[:, k, s * P:s * P + P], xnT[:, k, :],
                                       start=(k == 0), stop=(k == KD - 1))
                mm.then_inc(blk_done, 1)

            for b in range(A_BLOCKS):
                if b >= 4:
                    pe.wait_ge(conv_sum, b - 3)
                w_in_block(b % WSLOTS, b // WSLOTS, b % 4)
                if b == 1:
                    pe.wait_ge(adt_ready, 1)
                    pe.matmul(ps[:, 5, 0:TT * HEADS], upto[:, :], adt, start=True, stop=True)
                    pe.matmul(ps[:, 5, 32:48], after[:, :], adt[:, 0:HEADS], start=True, stop=True)
                    for c in range(TT):
                        mm = pe.matmul(ps[0:HEADS, 5, 64 + c * P:64 + c * P + P],
                                       adt[:, c * HEADS:c * HEADS + HEADS], upto[:, :], start=True, stop=True)
                    mm.then_inc(acum_ps, 1)

            def b_turn(q):
                for j in range(4):
                    b = A_BLOCKS + j
                    if isinstance(q, int):
                        pe.wait_ge(conv_sum, b - 3)
                    else:
                        pe.wait_ge((zs_ready, gc_ready, prod_ready, sc_ready)[j], q)
                    w_in_block(b % WSLOTS, q + b // WSLOTS, b % 4)

            b_turn(0)
            pe.wait_ge(acumT_ready, 1)
            pe.wait_ge(decay_ready, 1)
            pe.wait_ge(xbc_ready, A_BLOCKS)
            for c in range(TT):
                for k in range(KD):
                    mm = pe.transpose(ps[:, 4 + 2 * c + k // 4, (k % 4) * P:(k % 4) * P + P],
                                      xs[:, k, c * P:c * P + P], ident[:, :])
                    if k % 4 == 3:
                        mm.then_inc(xs_tok_ps, 1)
            pe.wait_ge(xdt_ready, 1)
            for c in range(TT):
                for g in range(GROUPS):
                    mm = pe.matmul(ps[:, 4, (c * GROUPS + g) * P:(c * GROUPS + g) * P + P],
                                   bcT[:, g, c * P:c * P + P], bcT[:, 2 + g, c * P:c * P + P],
                                   start=True, stop=True)
            mm.then_inc(cb_ps, 1)
            pe.wait_ge(xdt_ready, 2)
            for g in range(GROUPS):
                mm = pe.transpose(ps[:, 5, g * NSTATE:g * NSTATE + NSTATE], bcT[:, g, 0:P], ident[:, :])
            mm.then_inc(cb_ps, 1)
            with pe.Fori(1, B_TURNS) as q:
                b_turn(q)

            pe.wait_ge(xdd_ready, 1)
            pe.wait_ge(btok_ready, 1)
            pe.wait_ge(xdt_ready, 4)
            for g in range(GROUPS):
                mm = pe.matmul(ps[:, 6 + g, :], btok[:, g * NSTATE:g * NSTATE + NSTATE],
                               xdd[:, g * 512:g * 512 + 512], start=True, stop=True)
            mm.then_inc(state_ps, 1)
            pe.wait_ge(sc_scaled, 4 * B_TURNS)
            for t in range(TT):
                for k in range(KD):
                    mm = pe.matmul(ps[:, 0, t:t + 1], sq_sc[:, k, t * P:t * P + P], ones[:, 0:1],
                                   start=(k == 0), stop=(k == KD - 1))
            mm.then_inc(ms_ps, 1)
            pe.wait_ge(cb_taken, 1)
            pe.wait_ge(mt_ready, 6)
            for q in range(KD):
                if q == 0:
                    pe.wait_ge(state_ready, 1)
                for s in range(2):
                    e = 2 * q + s
                    cols = slice(e * HDIM, e * HDIM + HDIM)
                    bank, at_col = 4 + q // 2, (q % 2) * T
                    rows_ = slice(s * HDIM, s * HDIM + HDIM)
                    pe.matmul(ps[rows_, bank, at_col:at_col + P], xdt[:, 0, cols], mt[:, 0, e, :],
                              start=True, stop=True)
                    pe.matmul(ps[rows_, bank, at_col + P:at_col + T], xdt[:, 1, cols], mt[:, 1, e, :],
                              start=True, stop=False)
                    mm = pe.matmul(ps[rows_, bank, at_col + P:at_col + T], state[:, cols], cs[:, e, :],
                                   start=False, stop=True)
                if q % 2:
                    mm.then_inc(y_ps, 1)

            def out_group(g, blocks, src, tile0, bank0):
                for n, i in enumerate(blocks):
                    b = LAST + i
                    pe.wait_ge(wblk_full[b % WSLOTS], 16 * (b // WSLOTS + 1))
                    w = wblk[:, b % WSLOTS, :].rearrange("p (k n) -> p k n", k=2)
                    for kk in range(2):
                        k = tile0 + 2 * n + kk
                        final = n == len(blocks) - 1 and kk == 1
                        for r in range(4):
                            t, half = divmod(3 - r, 2)
                            mm = pe.matmul(ps[:, bank0 + 3 - r, :], src[:, k, t * P:t * P + P],
                                           w[:, kk, half * 512:half * 512 + 512],
                                           start=(n == 0 and kk == 0), stop=final)
                            if final and r < 3:
                                mm.then_inc(mix_ps, 1)
                    if final:
                        mm.then_inc(mix_ps, 1)
                    else:
                        mm.then_inc(blk_done, 1)

            pe.wait_ge(sc_ready, B_TURNS)
            pe.wait_ge(ms_ready, 1)
            out_group(0, range(0, 4), gsc, 0, 0)
            pe.wait_ge(g_scaled, KD)
            for g in range(2):
                for t in range(TT):
                    for k in range(4):
                        mm = pe.matmul(ps[:, 4, 2 * g + t:2 * g + t + 1], sq_ssd[:, 4 * g + k, t * P:t * P + P],
                                       ones[:, 0:1], start=(k == 0), stop=(k == 3))
            mm.then_inc(ms_ps, 1)
            pe.wait_ge(ms_ready, 2)
            out_group(1, range(4, 6), xs, 0, 4)
            pe.wait_ge(mix_taken, 4)
            out_group(2, range(6, 8), xs, 4, 0)

            pe.wait_ge(mix_taken, 12)
            pe.wait_ge(x2_ready, 2)
            for k in range(KD):
                for t in range(TT):
                    mm = pe.transpose(ps[:, k // 2, (k % 2) * T + t * P:(k % 2) * T + t * P + P],
                                      x2[:, t, k * P:k * P + P], ident[:, :])
                if k % 2:
                    mm.then_inc(x2T_ps, 1)
            pe.wait_ge(moe_params, 64)
            pe.wait_ge(x2T_dve, 2)
            pe.wait_ge(x2T_act, 4)
            for t in range(TT):
                for k in range(KD):
                    mm = pe.matmul(ps[:, 4, t * E:t * E + E], x2T[:, k, t * P:t * P + P], wr[:, k, :],
                                   start=(k == 0), stop=(k == KD - 1))
            mm.then_inc(logit_ps, 1)
            pe.wait_ge(mask_ready, 2)
            pe.matmul(ps[:, 6, 0:E], before[:, :], mask[:, 0, :], start=True, stop=True)
            pe.matmul(ps[:, 6, E:2 * E], before[:, :], mask[:, 1, :], start=True, stop=False)
            pe.matmul(ps[:, 6, E:2 * E], ones[:, :], mask[:, 0, :], start=False, stop=True)
            pe.matmul(ps[:, 6, 2 * E:3 * E], ones[:, :], mask[:, 0, :], start=True, stop=False)
            pe.matmul(ps[:, 6, 2 * E:3 * E], ones[:, :], mask[:, 1, :], start=False, stop=True)\
                .then_inc(pos_ps, 1)
            pe.wait_ge(route_ready, 1)
            for t in range(TT):
                mm = pe.transpose(ps[0:E, 5, t * P:t * P + P], gates3[:, t, 0:E], ident[:, :])
            mm.then_inc(gatesT_ps, 1)
            pe.wait_ge(gatesT_ready, 1)
            for n in range(4):
                t, half = divmod(n, 2)
                pe.matmul(ps[:, n, :], gatesT[0:E, t * P:t * P + P], bdn[0:E, half * 512:half * 512 + 512],
                          start=True, stop=True).then_inc(seed_ps, 1)

            def gather(g):
                pe.wait_ge(sel_ready, g + 1)
                for k in range(KD):
                    for t in range(TT):
                        mm = pe.matmul(ps[:, 4 + k // 4, (k % 4) * P:(k % 4) * P + P],
                                       x2[:, t, k * P:k * P + P], sel[:, t, :], start=(t == 0), stop=(t == TT - 1))
                mm.then_inc(gather_ps, 1)

            def halves(bank, lhs, w, first, last):
                for a in range(2):
                    mm = pe.matmul(ps[a * 64:a * 64 + 64, bank, :], lhs[:, a * 64:a * 64 + 64], w[a],
                                   start=first, stop=last, skip_group_check=True)
                    yield mm

            def item(i, g, t, u):
                pe.wait_ge(sele_ready, g + 1)
                for n in range(4):
                    pe.matmul(ps[:, n, :], sele[0:E, :], bgu[0:E, n * 512:n * 512 + 512], start=True,
                              stop=False, skip_group_check=True)
                pe.wait_ge(xsel_ready, g + 1)

                def chunk_pair(step):
                    c = u * CHUNKS + 2 * step
                    slots_ = []
                    for a in range(2):
                        pe.wait_ge(ring_full[(c + a) % RING], t * 48 + 16 * ((c + a) // RING + 1))
                        slots_.append(ring[:, (c + a) % RING, :])
                    return slots_

                for step in range(4):
                    w = [s.rearrange("p (k n) -> p k n", k=2) for s in chunk_pair(step)]
                    for kk in range(2):
                        k = 2 * step + kk
                        for n in range(4):
                            for mm in halves(n, xsel[:, k, :], [v[:, kk, n * 512:n * 512 + 512] for v in w],
                                             False, k == KD - 1):
                                if kk == 1 and n == 3:
                                    mm.then_inc(chunk_done, 1)
                gather(g + 1)
                for n in range(2):
                    pe.wait_ge(hid_ready, i * 2 + (n + 1))
                    for f in range(4):
                        mm = pe.transpose(ps[:, n, f * P:f * P + P], hid[:, (4 * n + f) * P:(4 * n + f) * P + P],
                                          ident[:, :])
                    mm.then_inc(hidT_ps, 1)
                pe.wait_ge(selg_ready, i + 1)
                for tt in range(TT):
                    mm = pe.transpose(ps[:, 2, tt * P:tt * P + P], selg[:, tt, :], ident[:, :])
                mm.then_inc(gT_ps, 1)
                for step in range(2):
                    w = [s.rearrange("p (k n) -> p k n", k=4) for s in chunk_pair(4 + step)]
                    pe.wait_ge(hidT_ready, i * 2 + (step + 1))
                    for kk in range(4):
                        f = 4 * step + kk
                        for n in range(2):
                            for mm in halves(6 + n, hidT[:, f, :], [v[:, kk, n * 512:n * 512 + 512] for v in w],
                                             f == 0, f == KD - 1):
                                if kk == 3 and n == 1:
                                    mm.then_inc(chunk_done, 1)
                pe.wait_ge(gT_ready, i + 1)
                for n in range(4):
                    half, tt = divmod(n, 2)
                    if tt == 0:
                        pe.wait_ge(oute_ready, i * 2 + 2)
                        if half:
                            pe.wait_ge(xsel_ready, g + 2)
                    pe.matmul(ps[:, [6, 7, 4, 5][n], :], gT[:, tt, :], oute[:, half * 512:half * 512 + 512],
                              start=True, stop=True).then_inc(add_ps, 1)

            def expert_pass(rnd):
                g0, i0, t0 = rnd * (PAIRS + 1), rnd * PAIRS, rnd * (PAIRS // 2)
                gather(g0)
                with pe.Fori(0, PAIRS // 2) as t:
                    for u in range(2):
                        item(i0 + t * 2 + u, g0 + t * 2 + u, t0 + t, u)

            pe.wait_ge(seed_taken, 4)
            expert_pass(0)
            with pe.If(flag_set(pe)):
                with pe.Fori(1, ROUNDS) as rnd:
                    expert_pass(rnd)


_INS = ['x', 'norm1_w', 'w_in', 'ssd_conv_w', 'ssd_conv_b', 'dt_bias', 'a_log', 'd_skip', 'ssd_norm_w',
        'sc_conv_w', 'sc_norm_w', 'w_out', 'norm2_w', 'w_router', 'b_router', 'w_gate_up', 'b_gate_up',
        'w_down', 'b_down', 'final_norm_w']


def kernel(**inputs):
    import numpy as _np
    import concourse.bacc as _bacc
    from concourse import mybir as _mybir
    from concourse.bass_utils import run_bass_kernel_spmd as _run

    nc = _bacc.Bacc("TRN2", target_bir_lowering=False, num_devices=1)
    arrays, args = {}, []
    for name in _INS:
        a = _np.ascontiguousarray(inputs[name])
        if name != 'final_norm_w':
            a = a.reshape(a.shape[1:])
        arrays[f"in_{name}"] = a
        args.append(nc.dram_tensor(f"in_{name}", a.shape, _mybir.dt.from_np(a.dtype), kind="ExternalInput").ap())
    out = nc.dram_tensor("out", (256, 1024), _mybir.dt.float32, kind="ExternalOutput").ap()
    hybrid_layer(nc, *args, out)
    r = _run(nc, [arrays], core_ids=[0])
    return r.results[0]["out"].reshape(1, 256, 1024)
```

```python
import concourse.bass as bass
from concourse import mybir
from contextlib import ExitStack

F32 = mybir.dt.float32
I32 = mybir.dt.int32
U32 = mybir.dt.uint32
ALU = mybir.AluOpType
ACT = mybir.ActivationFunctionType
AX = mybir.AxisListType
ds = bass.ds

P = 128
D = 1024
T = 256
TT = T // P
KD = D // P
HEADS = 16
HDIM = D // HEADS
GROUPS = 2
NSTATE = 128
XBC = D + 2 * GROUPS * NSTATE
XT = XBC // P
SSD_TAPS = 4
SC_TAPS = 3
E = 32
TOPK = 4
FF = 1024
EPS = 1e-5
LIMIT = 7.0
SW_ALPHA = 1.702

C_Z, C_XBC = 0, D
C_DT = C_XBC + XBC
C_GB = C_DT + HEADS
C_GC = C_GB + D
C_U = C_GC + D

BLK = 256
A_BLOCKS = XBC // BLK
B_TURNS = D // BLK
WSLOTS = 4

SLOTS = 64
ROUNDS = T // SLOTS
PAIRS = E // 2
RING = 8
CHUNKS = 12
EPAD = E + 2

R_DS = 0
R_N1 = R_DS + KD
R_CW = R_N1 + KD
R_CB = R_CW + SSD_TAPS * XT
R_SCW = R_CB + XT
R_SN = R_SCW + SC_TAPS * KD
R_SCN = R_SN + KD
R_N2 = R_SCN + KD
ROWS = R_N2 + KD


def spread(ap, axis, n):
    shape = list(ap.shape)
    index = [slice(None)] * len(shape)
    index.insert(axis, None)
    shape.insert(axis, n)
    return ap[tuple(index)].broadcast_to(shape)


class Chain:

    def __init__(self, eng, sem):
        self.eng, self.sem, self.n, self.base = eng, sem, 0, 0

    def turn(self, turn, steps):
        self.base, self.n = turn * steps, 0

    def step(self, ins):
        self.n += 1
        ins.then_inc(self.sem, 1)
        self.eng.wait_ge(self.sem, self.base + self.n)


def hybrid_layer(nc, x, norm1_w, w_in, ssd_conv_w, ssd_conv_b, dt_bias, a_log, d_skip, ssd_norm_w,
                 sc_conv_w, sc_norm_w, w_out, norm2_w, w_router, b_router, w_gate_up, b_gate_up,
                 w_down, b_down, final_norm_w, out):
    acum_dram = nc.dram_tensor("acum_scratch", (TT, HEADS, P), F32).ap()

    with ExitStack() as ctx:
        def sb(name, shape, dt=F32):
            return ctx.enter_context(nc.sbuf_tensor(name, shape, dt))

        def sem(name):
            return ctx.enter_context(nc.semaphore(name))

        ring = sb("ring", [P, RING, 4096])
        work = sb("work", [P, 17664])
        ident = sb("ident", [P, P])
        upto = sb("upto", [P, P])
        after = sb("after", [P, P])
        before = sb("before", [P, P])
        ones = sb("ones", [P, P])
        iota = sb("iota", [P, T])
        chan = sb("chan", [P, ROWS])
        small = sb("small", [P, 640])

        used = [0]

        def part(n):
            a = small[:, used[0]:used[0] + n]
            used[0] += n
            return a

        dtb_row = part(HEADS)
        a_row = part(HEADS)
        dt_x = part(TT * HEADS)
        dt_s = part(TT * HEADS)
        dt_y = part(TT * HEADS)
        dtv = part(TT * HEADS)
        adt = part(TT * HEADS)
        acum_j = part(TT * HEADS)
        decay_out = part(HEADS)
        sumsq = part(TT)
        sumsq2 = part(2 * TT)
        rstd = part(TT)
        power = part(3 * TT)
        mix_ms = part(3 * TT)
        mix_rstd = part(3 * TT)
        br_row = part(E)
        top8 = part(TT * 8)
        negmax = part(TT)
        topi_f = part(TT * 8)
        gsum = part(TT)
        cnt = part(8)
        skip2 = part(2)
        posm = part(TT * EPAD)
        gates = part(TT * EPAD)
        topi = sb("topi", [P, TT, 8], U32)
        overflow = sb("overflow", [P, 1], I32)

        flat = ring[:, :, :].rearrange("p s n -> p (s n)")
        at = [0]

        def scratch(n):
            a = flat[:, at[0]:at[0] + n]
            at[0] += n
            return a

        xn = scratch(TT * D).rearrange("p (t d) -> p t d", t=TT)
        xnT = scratch(KD * T).rearrange("p (k t) -> p k t", k=KD)
        bcT = scratch(4 * T).rearrange("p (n t) -> p n t", n=4)
        zs = scratch(KD * T).rearrange("p (n t) -> p n t", n=KD)
        xdt = scratch(TT * D).rearrange("p (c d) -> p c d", c=TT)
        mt = scratch(TT * HEADS * P).rearrange("p (c e i) -> p c e i", c=TT, e=HEADS)
        cs = scratch(HEADS * P).rearrange("p (e i) -> p e i", e=HEADS)
        xdd = scratch(D)
        btok = scratch(GROUPS * NSTATE)
        state = scratch(D)
        cbt = scratch(TT * GROUPS * P).rearrange("p (c g i) -> p c g i", c=TT, g=GROUPS)
        sig = scratch(2 * T)
        gcs = scratch(2 * T)
        prod = scratch(2 * T)
        conv = scratch(2 * T)
        sq_sc = scratch(KD * T).rearrange("p (n t) -> p n t", n=KD)
        sq_ssd = scratch(KD * T).rearrange("p (n t) -> p n t", n=KD)
        wdt = scratch(KD * HEADS).rearrange("p (k n) -> p k n", k=KD)
        rows = scratch(P)
        acumT = scratch(TT * P)

        wblk = work[:, 0:8192].rearrange("p (s n) -> p s n", s=WSLOTS)
        h = work[:, 8192:10240].rearrange("p (t d) -> p t d", t=TT)
        gsc = work[:, 10240:12288].rearrange("p (n t) -> p n t", n=KD)
        xs = work[:, 12288:14336].rearrange("p (n t) -> p n t", n=KD)
        bgu = work[:, 14336:16384]
        bdn = work[:, 16384:17408]
        wr = work[:, 17408:17664].rearrange("p (k n) -> p k n", k=KD)
        xsel = work[:, 0:1024].rearrange("p (k j) -> p k j", k=KD)
        gate = work[:, 1024:2048]
        up = work[:, 2048:3072]
        hid = work[:, 3072:4096]
        x2 = work[:, 4096:6144].rearrange("p (t d) -> p t d", t=TT)
        hidT = work[:, 6144:7168].rearrange("p (f j) -> p f j", f=KD)
        oute = work[:, 7168:8192]
        hT = work[:, 6144:8192].rearrange("p (t k j) -> p t k j", t=TT, k=KD)
        final_row = work[:, 10240:11264]
        sel = work[:, 11264:11520].rearrange("p (t j) -> p t j", t=TT)
        selg = work[:, 11520:11776].rearrange("p (t j) -> p t j", t=TT)
        gT = work[:, 11776:12032].rearrange("p (t j) -> p t j", t=TT)
        sele = work[:, 12032:12160]
        mask = work[:, 12288:12288 + TT * E].rearrange("p (t e) -> p t e", t=TT)
        logit = work[:, 12352:12352 + TT * E].rearrange("p (t e) -> p t e", t=TT)
        hot = work[:, 12416:12416 + TOPK * E].rearrange("p (n e) -> p n e", n=TOPK)

        posm3 = posm.rearrange("p (t e) -> p t e", t=TT)
        gates3 = gates.rearrange("p (t e) -> p t e", t=TT)

        ps = ctx.enter_context(nc.psum_tensor("ps", [P, 8, 512], F32))

        consts_made = sem("consts_made")
        x_loaded = [sem(f"x_loaded{t}") for t in range(TT)]
        rows_loaded = sem("rows_loaded")
        wdt_loaded = sem("wdt_loaded")
        dt_rows_loaded = sem("dt_rows_loaded")
        wblk_full = [sem(f"wblk_full{s}") for s in range(WSLOTS)]
        acum_stored = sem("acum_stored")
        acum_spread = [sem("acum_spread_mt"), sem("acum_spread_cs")]
        moe_params = sem("moe_params")
        final_row_loaded = sem("final_row_loaded")
        ring_full = [sem(f"ring_full{s}") for s in range(RING)]
        out_stored = sem("out_stored")
        act_step = sem("act_step")
        dve_step = sem("dve_step")
        pool_step = sem("pool_step")
        sumsq_ready = sem("sumsq_ready")
        rstd_ready = sem("rstd_ready")
        xn_ready = sem("xn_ready")
        skip_ready = sem("skip_ready")
        chan_ps = sem("chan_ps")
        chan_ready = sem("chan_ready")
        xT_ps = sem("xT_ps")
        xT_dve = sem("xT_dve")
        xT_act = sem("xT_act")
        dt_ps = sem("dt_ps")
        dtx_ready = sem("dtx_ready")
        dt_exp = sem("dt_exp")
        adt_ready = sem("adt_ready")
        acum_ps = sem("acum_ps")
        acumT_ready = sem("acumT_ready")
        decay_ready = sem("decay_ready")
        blk_done = sem("blk_done")
        zs_ready = sem("zs_ready")
        prod_ready = sem("prod_ready")
        conv_tap = sem("conv_tap")
        conv_sum = sem("conv_sum")
        conv_sig = sem("conv_sig")
        xbc_ready = sem("xbc_ready")
        xs_tok_ps = sem("xs_tok_ps")
        xdt_ready = sem("xdt_ready")
        cb_ps = sem("cb_ps")
        cb_taken = sem("cb_taken")
        seg_ready = sem("seg_ready")
        seg_exp = sem("seg_exp")
        cs_exp = sem("cs_exp")
        mt_ready = sem("mt_ready")
        xdd_ready = sem("xdd_ready")
        btok_ready = sem("btok_ready")
        state_ps = sem("state_ps")
        state_ready = sem("state_ready")
        z_sig = sem("z_sig")
        gc_ready = sem("gc_ready")
        sc_ready = sem("sc_ready")
        sc_scaled = sem("sc_scaled")
        y_ps = sem("y_ps")
        g_ready = sem("g_ready")
        g_scaled = sem("g_scaled")
        ms_ps = sem("ms_ps")
        ms_ready = sem("ms_ready")
        mix_rstd_ready = sem("mix_rstd_ready")
        mix_ps = sem("mix_ps")
        mix_taken = sem("mix_taken")
        wr_ready = sem("wr_ready")
        sumsq2_ready = sem("sumsq2_ready")
        rstd2_ready = sem("rstd2_ready")
        x2_ready = sem("x2_ready")
        hT_ps = sem("hT_ps")
        hT_dve = sem("hT_dve")
        hT_act = sem("hT_act")
        logit_ps = sem("logit_ps")
        max_ready = sem("max_ready")
        exp_ready = sem("exp_ready")
        mask_ready = sem("mask_ready")
        pos_ps = sem("pos_ps")
        slots_ready = sem("slots_ready")
        route_ready = sem("route_ready")
        dve_moe = sem("dve_moe")
        sel_ready = sem("sel_ready")
        sele_ready = sem("sele_ready")
        selg_ready = sem("selg_ready")
        gather_ps = sem("gather_ps")
        xsel_ready = sem("xsel_ready")
        chunk_done = sem("chunk_done")
        gate_ready = sem("gate_ready")
        gate_sig = sem("gate_sig")
        hid_ready = sem("hid_ready")
        hidT_ps = sem("hidT_ps")
        hidT_ready = sem("hidT_ready")
        gT_ps = sem("gT_ps")
        gT_ready = sem("gT_ready")
        oute_ready = sem("oute_ready")
        add_ps = sem("add_ps")
        moe_added = sem("moe_added")
        last_sq = sem("last_sq")
        last_rstd = sem("last_rstd")
        out_ready = sem("out_ready")

        CONSTS = 7
        ROW_LOADS = 8
        LAST = A_BLOCKS + 4 * B_TURNS
        OUT_BLOCKS = 8
        OUT_ROWS = [D + 256 * i for i in range(4)] + [256 * i for i in range(4)]

        block = ctx.enter_context(nc.Block())

        def flag_set(eng):
            return eng.value_load(overflow[0:1, 0:1], min_val=0, max_val=1) > 0

        @block.sync
        def _(sp):
            def w_in_block(slot, col):
                return sp.dma_start(wblk[:, slot, :].rearrange("p (k n) -> p k n", k=KD),
                                    w_in[:, ds(col, BLK)].rearrange("(k p) n -> p k n", p=P))

            for t in range(TT):
                sp.dma_start(h[:, t, :], x[t * P:(t + 1) * P, :]).then_inc(x_loaded[t], 16)
            for at_row, src in ((R_N1, norm1_w.rearrange("(n p) -> n p", p=P)),
                                (R_CW, ssd_conv_w.rearrange("w (n p) -> (w n) p", p=P)),
                                (R_CB, ssd_conv_b.rearrange("(n p) -> n p", p=P)),
                                (R_SCW, sc_conv_w.rearrange("w (n p) -> (w n) p", p=P)),
                                (R_SN, ssd_norm_w.rearrange("(n p) -> n p", p=P)),
                                (R_SCN, sc_norm_w.rearrange("(n p) -> n p", p=P)),
                                (R_N2, norm2_w.rearrange("(n p) -> n p", p=P))):
                sp.dma_start(rows[at_row:at_row + src.shape[0], :], src).then_inc(rows_loaded, 16)
            sp.dma_start(skip2[0:KD, :], d_skip.rearrange("(q a) -> q a", a=2)).then_inc(rows_loaded, 16)
            for b in range(A_BLOCKS):
                if b >= WSLOTS:
                    sp.wait_ge(blk_done, b - WSLOTS + 1)
                w_in_block(b % WSLOTS, C_XBC + BLK * b).then_inc(wblk_full[b % WSLOTS], 16)
            with sp.Fori(0, B_TURNS) as q:
                for j, col in enumerate((C_Z, C_GC, C_U, C_GB)):
                    b = A_BLOCKS + j
                    sp.wait_ge(blk_done, q * 4 + (b - WSLOTS + 1))
                    w_in_block(b % WSLOTS, q * BLK + col).then_inc(wblk_full[b % WSLOTS], 16)
            for i in range(OUT_BLOCKS):
                b = LAST + i
                if i < 7:
                    sp.wait_ge(blk_done, b - WSLOTS + 1)
                else:
                    sp.wait_ge(mix_ps, 4)
                sp.dma_start(wblk[:, b % WSLOTS, :].rearrange("p (k n) -> p k n", k=2),
                             w_out[OUT_ROWS[i]:OUT_ROWS[i] + 2 * P, :].rearrange("(k p) n -> p k n", p=P))\
                    .then_inc(wblk_full[b % WSLOTS], 16)

            def load_chunk(pair, c):
                e = (pair + c // CHUNKS) * 2 + c % 2
                step = c % CHUNKS // 2
                slot = c % RING
                if step < 4:
                    src = w_gate_up[ds(e, 1), step * 256:step * 256 + 256, :]
                    sp.dma_start(ring[:, slot, :].rearrange("p (k n) -> p k n", k=2),
                                 src.rearrange("o (k p) n -> p (o k) n", p=P)).then_inc(ring_full[slot], 16)
                else:
                    step -= 4
                    src = w_down[ds(e, 1), step * 512:step * 512 + 512, :]
                    sp.dma_start(ring[:, slot, :].rearrange("p (k n) -> p k n", k=4),
                                 src.rearrange("o (k p) n -> p (o k) n", p=P)).then_inc(ring_full[slot], 16)

            def load_pass(rnd, first):
                done = rnd * (PAIRS * CHUNKS)
                for c in range(RING):
                    if not first:
                        sp.wait_ge(chunk_done, done + (c - RING + 1))
                    load_chunk(0, c)
                with sp.Fori(0, PAIRS // 2 - 1) as t:
                    for c in range(RING, RING + 2 * CHUNKS):
                        sp.wait_ge(chunk_done, done + t * (2 * CHUNKS) + (c - RING + 1))
                        load_chunk(t * 2, c)
                t = PAIRS // 2 - 1
                for c in range(RING, 2 * CHUNKS):
                    sp.wait_ge(chunk_done, done + (t * 2 * CHUNKS + c - RING + 1))
                    load_chunk(t * 2, c)

            sp.wait_ge(ms_ps, 2)
            load_pass(0, True)
            sp.wait_ge(route_ready, 1)
            with sp.If(flag_set(sp)):
                with sp.Fori(1, ROUNDS) as rnd:
                    load_pass(rnd, False)
            for t in range(TT):
                sp.wait_ge(out_ready, t + 1)
                sp.dma_start(out[t * P:(t + 1) * P, :], h[:, t, :]).then_inc(out_stored, 16)
            sp.wait_ge(out_stored, 16 * TT)

        @block.gpsimd
        def _(pool):
            chain = Chain(pool, pool_step)
            for tile, value in ((ident, 0.0), (upto, 1.0), (after, 1.0), (before, 1.0), (ones, 1.0)):
                chain.step(pool.memset(tile[:, :], value))
            pool.memset(power, -0.5).then_inc(consts_made, 1)
            for tile, how, fill, sign in ((ident, ALU.not_equal, 1.0, 1), (upto, ALU.is_ge, 0.0, 1),
                                          (after, ALU.is_gt, 0.0, -1), (before, ALU.is_gt, 0.0, 1)):
                pool.affine_select(out=tile[:, :], in_=tile[:, :], compare_op=how, fill=fill, base=0,
                                   pattern=[[sign, P]], channel_multiplier=-sign).then_inc(consts_made, 1)
            pool.iota(iota[:, :], pattern=[[1, T]], base=0, channel_multiplier=0,
                      allow_small_or_imprecise_dtypes=True).then_inc(consts_made, 1)
            pool.memset(cnt[:, 0:1], 0.0).then_inc(consts_made, 1)

            def root(dst, sums, n, scale):
                chain.step(pool.tensor_scalar(dst, sums, scale, EPS, ALU.mult, ALU.add))
                return pool.tensor_tensor(dst, dst, power[:, 0:n], ALU.pow)

            pool.wait_ge(consts_made, CONSTS)
            for t in range(TT):
                pool.wait_ge(sumsq_ready, t + 1)
                root(rstd[:, t:t + 1], sumsq[:, t:t + 1], 1, 1.0 / D).then_inc(rstd_ready, 1)
            pool.wait_ge(acumT_ready, 1)
            pool.dma_start(acum_dram.rearrange("c e i -> e c i"),
                           acumT[0:HEADS, :].rearrange("e (c i) -> e c i", c=TT)).then_inc(acum_stored, 16)
            pool.wait_ge(acum_stored, 16)
            pool.dma_start(mt.rearrange("p c e i -> p (c e i)"),
                           acum_dram.rearrange("c e i -> (c e i)").partition_broadcast(P))\
                .then_inc(acum_spread[0], 16)
            pool.dma_start(cs.rearrange("p e i -> p (e i)"),
                           acum_dram[1].rearrange("e i -> (e i)").partition_broadcast(P))\
                .then_inc(acum_spread[1], 16)
            pool.wait_ge(xdt_ready, 2)
            pool.wait_ge(decay_ready, 1)
            pool.tensor_tensor(xdd.rearrange("p (e n) -> p e n", e=HEADS),
                               xdt[:, 0, :].rearrange("p (e n) -> p e n", e=HEADS),
                               spread(decay_out, 2, HDIM), ALU.mult).then_inc(xdd_ready, 1)
            pool.wait_ge(moe_params, 64)
            pool.wait_ge(chan_ready, 1)
            pool.tensor_tensor(wr, wr, spread(chan[:, R_N2:R_N2 + KD], 2, E), ALU.mult).then_inc(wr_ready, 1)
            pool.wait_ge(ms_ready, 1)
            pool.tensor_tensor(mix_rstd[:, 0:TT], mix_ms[:, 0:TT], power[:, 0:TT], ALU.pow)\
                .then_inc(mix_rstd_ready, 1)
            pool.wait_ge(ms_ready, 2)
            pool.tensor_tensor(mix_rstd[:, TT:3 * TT], mix_ms[:, TT:3 * TT], power[:, 0:2 * TT], ALU.pow)\
                .then_inc(mix_rstd_ready, 1)
            for n, t in enumerate((1, 0)):
                pool.wait_ge(sumsq2_ready, 2 * n + 2)
                chain.step(pool.tensor_tensor(rstd[:, t:t + 1], sumsq2[:, 2 * t:2 * t + 1],
                                              sumsq2[:, 2 * t + 1:2 * t + 2], ALU.add))
                root(rstd[:, t:t + 1], rstd[:, t:t + 1], 1, 1.0 / D).then_inc(rstd2_ready, 1)
            pool.dma_start(final_row, final_norm_w.partition_broadcast(P)).then_inc(final_row_loaded, 16)
            for t in range(TT):
                pool.wait_ge(last_sq, t + 1)
                root(rstd[:, t:t + 1], sumsq[:, t:t + 1], 1, 1.0 / D).then_inc(last_rstd, 1)

        @block.scalar
        def _(act):
            chain = Chain(act, act_step)

            for t in range(TT):
                act.wait_ge(x_loaded[t], 16)
                act.activation(xn[:, t, :], h[:, t, :], ACT.Square, accum_out=sumsq[:, t:t + 1])\
                    .then_inc(sumsq_ready, 1)
            act.dma_start(wdt, w_in[:, C_DT:C_DT + HEADS].rearrange("(k p) n -> p k n", p=P))\
                .then_inc(wdt_loaded, 16)
            act.wait_ge(rstd_ready, 2)
            act.activation(xn[:, 1, :], h[:, 1, :], ACT.Copy, scale=rstd[:, 1:2]).then_inc(xn_ready, 1)
            act.dma_start(dtb_row, dt_bias.partition_broadcast(P)).then_inc(dt_rows_loaded, 16)
            act.dma_start(a_row, a_log.partition_broadcast(P)).then_inc(dt_rows_loaded, 16)

            act.wait_ge(chan_ready, 1)
            for k in range(KD // 2, KD):
                act.wait_ge(xT_ps, k // 2 + 1)
                act.activation(xnT[:, k, :], ps[:, 4 + k // 2, (k % 2) * T:(k % 2) * T + T], ACT.Copy,
                               scale=chan[:, R_N1 + k:R_N1 + k + 1]).then_inc(xT_act, 1)

            act.dma_start(wr, w_router.rearrange("(k p) n -> p k n", p=P)).then_inc(moe_params, 16)
            act.dma_start(br_row, b_router.partition_broadcast(P)).then_inc(moe_params, 16)
            act.dma_start(bdn[0:E, :], b_down).then_inc(moe_params, 16)
            act.dma_start(bgu[0:E, :], b_gate_up).then_inc(moe_params, 16)
            act.wait_ge(dt_rows_loaded, 32)
            chain.step(act.activation(a_row, a_row, ACT.Exp))
            act.wait_ge(dtx_ready, 1)
            act.activation(dt_s, dt_x, ACT.Exp, scale=-1.0).then_inc(dt_exp, 1)

            def conv_block(b):
                for s in range(2):
                    n = 2 * b + s
                    dst = xs[:, n, :] if n < KD else bcT[:, n - KD, :]
                    act.wait_ge(blk_done, b + 1)
                    act.activation(dst, ps[:, b % 4, s * T:s * T + T], ACT.Identity,
                                   scale=chan[:, R_CW + 3 * XT + n:R_CW + 3 * XT + n + 1],
                                   bias=chan[:, R_CB + n:R_CB + n + 1]).then_inc(conv_tap, 1)
                act.wait_ge(conv_sum, b + 1)
                src = xs[:, 2 * b:2 * b + 2, :] if b < 4 else bcT[:, 2 * b - KD:2 * b - KD + 2, :]
                if b > 0:
                    act.wait_ge(xbc_ready, b)
                act.activation(sig.rearrange("p (n t) -> p n t", n=2), src, ACT.Sigmoid).then_inc(conv_sig, 1)

            for b in range(A_BLOCKS):
                conv_block(b)
            act.wait_ge(acumT_ready, 1)
            act.activation(decay_out, ps[:, 5, 32:48], ACT.Exp).then_inc(decay_ready, 1)

            def b_turn(q, bank0):
                act.wait_ge(blk_done, q * 4 + (A_BLOCKS + 1))
                act.wait_ge(zs_ready, q)
                act.activation(sig, ps[:, bank0 % 4, :], ACT.Sigmoid).then_inc(z_sig, 1)
                act.wait_ge(blk_done, q * 4 + (A_BLOCKS + 2))
                act.wait_ge(prod_ready, q)
                act.activation(gcs, ps[:, (bank0 + 1) % 4, :], ACT.Copy).then_inc(gc_ready, 1)
                act.wait_ge(sc_ready, q + 1)
                for s in range(2):
                    act.activation(sq_sc[:, ds(q * 2 + s, 1), :], gsc[:, ds(q * 2 + s, 1), :],
                                   ACT.Square).then_inc(sc_scaled, 1)
                act.wait_ge(sc_scaled, q * 4 + 2)
                for s in range(2):
                    act.activation(gsc[:, ds(q * 2 + s, 1), :], gsc[:, ds(q * 2 + s, 1), :], ACT.Copy,
                                   scale=chan[:, ds(q * 2 + (R_SCN + s), 1)]).then_inc(sc_scaled, 1)

            act.wait_ge(xbc_ready, A_BLOCKS)
            b_turn(0, A_BLOCKS)
            act.wait_ge(cb_ps, 2)
            act.activation(btok, ps[:, 5, 0:GROUPS * NSTATE], ACT.Copy).then_inc(btok_ready, 1)
            for c in range(TT):
                act.wait_ge(seg_ready, c + 1)
                act.activation(mt[:, c], mt[:, c], ACT.Exp).then_inc(seg_exp, 1)
            act.wait_ge(acum_spread[1], 16)
            act.activation(cs, cs, ACT.Exp).then_inc(cs_exp, 1)
            with act.Fori(1, B_TURNS) as q:
                b_turn(q, A_BLOCKS)
            act.wait_ge(state_ps, 1)
            act.activation(state, ps[:, 6:8, :].rearrange("p b n -> p (b n)"), ACT.Copy)\
                .then_inc(state_ready, 1)

            for q in range(KD):
                act.wait_ge(g_ready, q // 2 + 1)
                chain.step(act.activation(sq_ssd[:, q, :], xs[:, q, :], ACT.Square))
                act.activation(xs[:, q, :], xs[:, q, :], ACT.Copy,
                               scale=chan[:, R_SN + q:R_SN + q + 1]).then_inc(g_scaled, 1)

            for n, t in enumerate((1, 0)):
                for m in range(2):
                    act.wait_ge(mix_taken, 8 + 2 * n + m + 1)
                    cols = slice((1 - m) * 512, (1 - m) * 512 + 512)
                    act.activation(x2[:, t, cols], h[:, t, cols], ACT.Square,
                                   accum_out=sumsq2[:, 2 * t + m:2 * t + m + 1]).then_inc(sumsq2_ready, 1)
                if n == 1:
                    act.wait_ge(hT_ps, 4)
                    act.activation(hT[:, 0, 0:4, :], ps[:, 7, :].rearrange("p (k j) -> p k j", k=4), ACT.Copy)\
                        .then_inc(hT_act, 1)
                act.wait_ge(rstd2_ready, n + 1)
                act.activation(x2[:, t, :], h[:, t, :], ACT.Copy, scale=rstd[:, t:t + 1]).then_inc(x2_ready, 1)
            for n, t in enumerate((1, 0)):
                act.wait_ge(max_ready, n + 1)
                act.activation(gates3[:, t, 0:E], logit[:, t, :], ACT.Exp, bias=negmax[:, t:t + 1])\
                    .then_inc(exp_ready, 1)

            def item(i, g):
                for n in range(2):
                    half = slice(n * 512, n * 512 + 512)
                    act.wait_ge(gate_ready, i * 2 + (n + 1))
                    act.activation(hid[:, half], gate[:, half], ACT.Sigmoid, scale=SW_ALPHA)\
                        .then_inc(gate_sig, 1)
                for n in range(2):
                    act.wait_ge(hidT_ps, i * 2 + (n + 1))
                    act.activation(hidT[:, n * 4:n * 4 + 4, :], ps[:, n, :].rearrange("p (f j) -> p f j", j=P),
                                   ACT.Copy).then_inc(hidT_ready, 1)
                act.wait_ge(gT_ps, i + 1)
                act.activation(gT, ps[:, 2, 0:T].rearrange("p (t j) -> p t j", t=TT), ACT.Copy)\
                    .then_inc(gT_ready, 1)
                act.wait_ge(chunk_done, i * CHUNKS + CHUNKS)
                for n in range(2):
                    act.activation(oute[:, n * 512:n * 512 + 512], ps[:, 6 + n, :], ACT.Copy)\
                        .then_inc(oute_ready, 1)

            def expert_pass(rnd):
                with act.Fori(0, PAIRS) as p:
                    item(rnd * PAIRS + p, rnd * (PAIRS + 1) + p)

            expert_pass(0)
            act.wait_ge(route_ready, 1)
            with act.If(flag_set(act)):
                with act.Fori(1, ROUNDS) as rnd:
                    expert_pass(rnd)

            for t in range(TT):
                act.wait_ge(moe_added, t + 1)
                act.activation(x2[:, t, :], h[:, t, :], ACT.Square, accum_out=sumsq[:, t:t + 1])\
                    .then_inc(last_sq, 1)

        @block.vector
        def _(dve):
            chain = Chain(dve, dve_step)

            def sent(ins, sem_, value):
                ins.then_inc(sem_, 1)
                dve.wait_ge(sem_, value)

            dve.wait_ge(rows_loaded, 16 * ROW_LOADS)
            sent(dve.tensor_copy(rows[R_DS:R_DS + KD, :].rearrange("q (a n) -> q a n", a=2),
                                 spread(skip2[0:KD, :], 2, HDIM)), skip_ready, 1)
            dve.wait_ge(rstd_ready, 1)
            dve.tensor_scalar(xn[:, 0, :], h[:, 0, :], rstd[:, 0:1], None, ALU.mult).then_inc(xn_ready, 1)
            dve.wait_ge(chan_ps, 1)
            sent(dve.tensor_copy(chan[:, :], ps[:, 0, 0:ROWS]), chan_ready, 1)
            for b in range(2):
                dve.wait_ge(xT_ps, b + 1)
                dve.tensor_tensor(xnT[:, 2 * b:2 * b + 2, :], ps[:, 4 + b, :].rearrange("p (k t) -> p k t", k=2),
                                  spread(chan[:, R_N1 + 2 * b:R_N1 + 2 * b + 2], 2, T), ALU.mult)\
                    .then_inc(xT_dve, 1)

            dve.wait_ge(dt_ps, 1)
            dve.wait_ge(dt_rows_loaded, 32)
            chain.step(dve.tensor_tensor(dt_y.rearrange("p (c e) -> p c e", c=TT),
                                         ps[:, 4, 0:TT * HEADS].rearrange("p (c e) -> p c e", c=TT),
                                         spread(dtb_row, 1, TT), ALU.add))
            chain.step(dve.tensor_scalar(dt_x, dt_y, -1.0, None, ALU.mult))
            sent(dve.tensor_tensor(dt_x, dt_x, dt_y, ALU.max), dtx_ready, 1)
            chain.step(dve.tensor_scalar(dt_y, dt_y, 0.0, None, ALU.max))
            dve.wait_ge(dt_exp, 1)
            chain.step(dve.tensor_scalar(dt_x, dt_s, 2.0, None, ALU.add))
            chain.step(dve.reciprocal(dt_x, dt_x))
            chain.step(dve.tensor_tensor(dt_s, dt_s, dt_x, ALU.mult))
            chain.step(dve.tensor_tensor(dt_x, dt_s, dt_s, ALU.mult))
            terms = list(range(15, 1, -2))
            chain.step(dve.tensor_scalar(dtv, dt_x, 2.0 / 17, None, ALU.mult))
            for n in terms:
                chain.step(dve.scalar_tensor_tensor(out=dtv, in0=dtv, scalar=2.0 / n, in1=dt_x,
                                                    op0=ALU.add, op1=ALU.mult))
            chain.step(dve.scalar_tensor_tensor(out=dtv, in0=dtv, scalar=2.0, in1=dt_s,
                                                op0=ALU.add, op1=ALU.mult))
            chain.step(dve.tensor_tensor(dtv, dtv, dt_y, ALU.add))
            dve.wait_ge(act_step, 1)
            sent(dve.scalar_tensor_tensor(out=adt.rearrange("p (c e) -> p c e", c=TT),
                                          in0=dtv.rearrange("p (c e) -> p c e", c=TT), scalar=-1.0,
                                          in1=spread(a_row, 1, TT), op0=ALU.mult, op1=ALU.mult), adt_ready, 1)

            def conv_block(b):
                for s in range(2):
                    n = 2 * b + s
                    dst = xs[:, n, :] if n < KD else bcT[:, n - KD, :]
                    src = ps[:, b % 4, s * T:s * T + T]
                    dve.wait_ge(conv_tap, 2 * b + 2)
                    for back in range(1, SSD_TAPS):
                        tap = SSD_TAPS - 1 - back
                        ins = dve.scalar_tensor_tensor(
                            out=dst[:, back:], in0=src[:, :T - back],
                            scalar=chan[:, R_CW + tap * XT + n:R_CW + tap * XT + n + 1],
                            in1=dst[:, back:], op0=ALU.mult, op1=ALU.add)
                        if s == 1 and back == SSD_TAPS - 1:
                            sent(ins, conv_sum, b + 1)
                        else:
                            chain.step(ins)
                dst = xs[:, 2 * b:2 * b + 2, :] if b < 4 else bcT[:, 2 * b - KD:2 * b - KD + 2, :]
                dve.wait_ge(conv_sig, b + 1)
                sent(dve.tensor_tensor(dst, dst, sig.rearrange("p (n t) -> p n t", n=2), ALU.mult),
                     xbc_ready, b + 1)

            for b in range(3):
                conv_block(b)
            dve.wait_ge(acum_ps, 1)
            chain.step(dve.tensor_copy(acum_j, ps[:, 5, 0:TT * HEADS]))
            sent(dve.tensor_copy(acumT[0:HEADS, :], ps[0:HEADS, 5, 64:64 + T]), acumT_ready, 1)
            for b in range(3, A_BLOCKS):
                conv_block(b)

            def b_turn(q, bank0):
                two = ds(q * 2, 2)
                dve.wait_ge(z_sig, q + 1)
                sent(dve.tensor_tensor(zs[:, two, :], ps[:, bank0 % 4, :].rearrange("p (n t) -> p n t", n=2),
                                       sig.rearrange("p (n t) -> p n t", n=2), ALU.mult), zs_ready, q + 1)
                dve.wait_ge(gc_ready, q + 1)
                dve.wait_ge(blk_done, q * 4 + (A_BLOCKS + 3))
                sent(dve.tensor_tensor(prod, ps[:, (bank0 + 2) % 4, :], gcs, ALU.mult), prod_ready, q + 1)
                for s in range(2):
                    src, dst = prod[:, s * T:s * T + T], conv[:, s * T:s * T + T]
                    chain.step(dve.tensor_scalar(dst, src, chan[:, ds(q * 2 + (R_SCW + 2 * KD + s), 1)], None, ALU.mult))
                    for back in range(1, SC_TAPS):
                        tap = SC_TAPS - 1 - back
                        chain.step(dve.scalar_tensor_tensor(
                            out=dst[:, back:], in0=src[:, :T - back],
                            scalar=chan[:, ds(q * 2 + (R_SCW + tap * KD + s), 1)],
                            in1=dst[:, back:], op0=ALU.mult, op1=ALU.add))
                dve.wait_ge(blk_done, q * 4 + (A_BLOCKS + 4))
                sent(dve.tensor_tensor(gsc[:, two, :], ps[:, (bank0 + 3) % 4, :].rearrange("p (n t) -> p n t", n=2),
                                       conv.rearrange("p (n t) -> p n t", n=2), ALU.mult), sc_ready, q + 1)

            b_turn(0, A_BLOCKS)
            for c in range(TT):
                for n in range(2):
                    dve.wait_ge(xs_tok_ps, 2 * c + n + 1)
                    heads = slice(c * HEADS + 8 * n, c * HEADS + 8 * n + 8)
                    sent(dve.tensor_tensor(xdt[:, c, n * 512:n * 512 + 512].rearrange("p (e d) -> p e d", e=8),
                                           ps[:, 4 + 2 * c + n, :].rearrange("p (e d) -> p e d", e=8),
                                           spread(dtv[:, heads], 2, HDIM), ALU.mult), xdt_ready, 2 * c + n + 1)
            for c in range(TT):
                dve.wait_ge(acum_spread[0], 16)
                chain.step(dve.tensor_tensor(mt[:, c], mt[:, c],
                                             spread(acum_j[:, c * HEADS:c * HEADS + HEADS], 2, P), ALU.subtract))
                sent(dve.tensor_scalar(mt[:, c], mt[:, c], 0.0, None, ALU.min), seg_ready, c + 1)
            dve.wait_ge(cb_ps, 1)
            sent(dve.tensor_tensor(cbt.rearrange("p c g i -> p (c g) i"),
                                   ps[:, 4, :].rearrange("p (n i) -> p n i", i=P),
                                   spread(upto[:, :], 1, TT * GROUPS), ALU.mult), cb_taken, 1)
            n = 0
            for c in range(TT):
                dve.wait_ge(seg_exp, c + 1)
                for g in range(GROUPS):
                    n += 1
                    sent(dve.tensor_tensor(mt[:, c, 8 * g:8 * g + 8, :], mt[:, c, 8 * g:8 * g + 8, :],
                                           spread(cbt[:, c, g, :], 1, 8), ALU.mult), mt_ready, n)
            dve.wait_ge(cs_exp, 1)
            for g in range(GROUPS):
                n += 1
                sent(dve.tensor_tensor(cs[:, 8 * g:8 * g + 8, :], cs[:, 8 * g:8 * g + 8, :],
                                       spread(bcT[:, 2 + g, P:2 * P], 1, 8), ALU.mult), mt_ready, n)
            before_loop = chain.n
            TURN_STEPS = 2 * SC_TAPS
            with dve.Fori(1, B_TURNS) as q:
                chain.turn(q, TURN_STEPS)
                chain.base = chain.base + (before_loop - TURN_STEPS)
                b_turn(q, A_BLOCKS)
                assert chain.n == TURN_STEPS
            chain.base, chain.n = before_loop + TURN_STEPS * (B_TURNS - 1), 0

            dve.wait_ge(ms_ps, 1)
            sent(dve.tensor_scalar(mix_ms[:, 0:TT], ps[:, 0, 0:TT], 1.0 / D, EPS, ALU.mult, ALU.add), ms_ready, 1)
            for b in range(4):
                dve.wait_ge(y_ps, b + 1)
                for s in range(2):
                    n = 2 * b + s
                    chain.step(dve.scalar_tensor_tensor(
                        out=xs[:, n, :], in0=xs[:, n, :], scalar=chan[:, R_DS + n:R_DS + n + 1],
                        in1=ps[:, 4 + b, s * T:s * T + T], op0=ALU.mult, op1=ALU.add))
                sent(dve.tensor_tensor(xs[:, 2 * b:2 * b + 2, :], xs[:, 2 * b:2 * b + 2, :],
                                       zs[:, 2 * b:2 * b + 2, :], ALU.mult), g_ready, b + 1)

            def add_group(g, bank0, quarters=range(4)):
                for n in quarters:
                    t, half = divmod(3 - n, 2)
                    dve.wait_ge(mix_ps, 4 * g + n + 1)
                    cols = slice(half * 512, half * 512 + 512)
                    sent(dve.scalar_tensor_tensor(out=h[:, t, cols], in0=ps[:, bank0 + 3 - n, :],
                                                  scalar=mix_rstd[:, 2 * g + t:2 * g + t + 1],
                                                  in1=h[:, t, cols], op0=ALU.mult, op1=ALU.add),
                         mix_taken, 4 * g + n + 1)

            dve.wait_ge(ms_ps, 2)
            sent(dve.tensor_scalar(mix_ms[:, TT:3 * TT], ps[:, 4, 0:2 * TT], 1.0 / 512, EPS, ALU.mult, ALU.add),
                 ms_ready, 2)
            dve.wait_ge(mix_rstd_ready, 1)
            add_group(0, 0)
            dve.wait_ge(mix_rstd_ready, 2)
            add_group(1, 4)

            dve.wait_ge(moe_params, 64)
            def copy_hT(n, m):
                dve.wait_ge(hT_ps, 2 * n + m + 1)
                dve.tensor_copy(hT[:, 1 - n, 4 * (1 - m):4 * (1 - m) + 4, :],
                                ps[:, 4 + 2 * n + m, :].rearrange("p (k j) -> p k j", k=4))\
                    .then_inc(hT_dve, 1)

            add_group(2, 0, range(3))
            copy_hT(0, 0)
            copy_hT(0, 1)
            add_group(2, 0, (3,))
            copy_hT(1, 0)
            for n, t in enumerate((1, 0)):
                dve.wait_ge(rstd2_ready, n + 1)
                dve.wait_ge(logit_ps, n + 1)
                chain.step(dve.scalar_tensor_tensor(out=logit[:, t, :], in0=ps[:, 4 + 2 * n, 0:E],
                                                    scalar=rstd[:, t:t + 1], in1=br_row,
                                                    op0=ALU.mult, op1=ALU.add))
                chain.step(dve.max(top8[:, 8 * t:8 * t + 8], logit[:, t, :]))
                chain.step(dve.max_index(topi[:, t, :], top8[:, 8 * t:8 * t + 8], logit[:, t, :]))
                chain.step(dve.tensor_copy(topi_f[:, 8 * t:8 * t + 8], topi[:, t, :]))
                chain.step(dve.tensor_tensor(hot, spread(iota[:, 0:E], 1, TOPK),
                                             spread(topi_f[:, 8 * t:8 * t + TOPK], 2, E), ALU.is_equal))
                sent(dve.tensor_reduce(mask[:, t, :], hot.rearrange("p n e -> p e n"), AX.X, ALU.add),
                     mask_ready, n + 1)
                sent(dve.tensor_scalar(negmax[:, t:t + 1], top8[:, 8 * t:8 * t + 1], -1.0, None, ALU.mult),
                     max_ready, n + 1)
                if n == 0:
                    chain.step(dve.memset(gates3[:, :, E:EPAD], 0.0))
                    chain.step(dve.memset(posm3[:, :, E:EPAD], -1.0))
            dve.wait_ge(pos_ps, 1)
            chain.step(dve.scalar_tensor_tensor(out=posm3[:, :, 0:E],
                                                in0=ps[:, 6, 0:TT * E].rearrange("p (t e) -> p t e", t=TT),
                                                scalar=1.0, in1=mask, op0=ALU.add, op1=ALU.mult))
            sent(dve.tensor_scalar(posm3[:, :, 0:E], posm3[:, :, 0:E], -1.0, None, ALU.add), slots_ready, 1)

            def finish_routing():
                dve.wait_ge(exp_ready, 2)
                chain.step(dve.tensor_tensor(gates3[:, :, 0:E], gates3[:, :, 0:E], mask, ALU.mult))
                chain.step(dve.tensor_reduce(gsum, gates3[:, :, 0:E], AX.X, ALU.add))
                chain.step(dve.reciprocal(gsum, gsum))
                chain.step(dve.tensor_tensor(gates3[:, :, 0:E], gates3[:, :, 0:E], spread(gsum, 2, E), ALU.mult))
                chain.step(dve.tensor_reduce(cnt[:, 1:2], ps[:, 6, TT * E:TT * E + E], AX.X, ALU.max))
                sent(dve.tensor_scalar(overflow[:, :], cnt[:, 1:2], float(SLOTS), None, ALU.is_gt),
                     route_ready, 1)

            moe = Chain(dve, dve_moe)
            ITEM_STEPS = 8
            quad = "p t (a j) -> p t a j"

            def build_sel(g, p, rnd):
                if not isinstance(g, int):
                    dve.wait_ge(gather_ps, g)
                slots = iota[:, ds(rnd * SLOTS, SLOTS)]
                sent(dve.tensor_tensor(sel.rearrange(quad, a=2), spread(spread(slots, 1, 2), 1, TT),
                                       spread(posm3[:, :, ds(p * 2, 2)], 3, SLOTS), ALU.is_equal),
                     sel_ready, g + 1)

            def build_sele(g, p):
                dve.tensor_copy(sele[0:E, :].rearrange("p (a j) -> p a j", a=2),
                                spread(ident[0:E, ds(p * 2, 2)], 2, SLOTS)).then_inc(sele_ready, 1)

            def take_gathered(g):
                dve.wait_ge(gather_ps, g + 1)
                dve.tensor_tensor(xsel, ps[:, 4:6, :].rearrange("p b (k j) -> p (b k) j", j=P),
                                  spread(chan[:, R_N2:R_N2 + KD], 2, P), ALU.mult).then_inc(xsel_ready, 1)

            def item(i, g, p, rnd):
                moe.turn(i, ITEM_STEPS)
                build_sel(g + 1, p + 1, rnd)
                slots = iota[:, ds(rnd * SLOTS, SLOTS)]
                moe.step(dve.tensor_tensor(selg.rearrange(quad, a=2), spread(spread(slots, 1, 2), 1, TT),
                                           spread(posm3[:, :, ds(p * 2, 2)], 3, SLOTS), ALU.is_equal))
                sent(dve.tensor_tensor(selg.rearrange(quad, a=2), selg.rearrange(quad, a=2),
                                       spread(gates3[:, :, ds(p * 2, 2)], 3, SLOTS), ALU.mult),
                     selg_ready, i + 1)
                dve.wait_ge(chunk_done, i * CHUNKS + 8)
                for n in range(2):
                    sent(dve.tensor_scalar(gate[:, n * 512:n * 512 + 512], ps[:, n, :], LIMIT, None, ALU.min),
                         gate_ready, i * 2 + (n + 1))
                moe.step(dve.tensor_scalar(up, ps[:, 2:4, :].rearrange("p b n -> p (b n)"), LIMIT, -LIMIT,
                                           ALU.min, ALU.max))
                for n in range(2):
                    half = slice(n * 512, n * 512 + 512)
                    dve.wait_ge(gate_sig, i * 2 + (n + 1))
                    moe.step(dve.tensor_tensor(gate[:, half], gate[:, half], hid[:, half], ALU.mult))
                    sent(dve.scalar_tensor_tensor(out=hid[:, half], in0=up[:, half], scalar=1.0,
                                                  in1=gate[:, half], op0=ALU.add, op1=ALU.mult),
                         hid_ready, i * 2 + (n + 1))
                take_gathered(g + 1)
                dve.wait_ge(hidT_ps, i * 2 + 1)
                build_sele(g + 1, p + 1)
                for n in range(4):
                    half, t = divmod(n, 2)
                    cols = slice(half * 512, half * 512 + 512)
                    dve.wait_ge(add_ps, i * 4 + (n + 1))
                    moe.step(dve.tensor_tensor(h[:, t, cols], h[:, t, cols], ps[:, [6, 7, 4, 5][n], :], ALU.add))
                assert moe.n == ITEM_STEPS

            def expert_pass(rnd):
                g = rnd * (PAIRS + 1)
                build_sel(g, 0, rnd)
                build_sele(g, 0)
                take_gathered(g)
                if isinstance(rnd, int):
                    finish_routing()
                with dve.Fori(0, PAIRS) as p:
                    item(rnd * PAIRS + p, g + p, p, rnd)

            expert_pass(0)
            with dve.If(flag_set(dve)):
                with dve.Fori(1, ROUNDS) as rnd:
                    expert_pass(rnd)

            for t in range(TT):
                sent(dve.memset(cnt[:, 3 + t:4 + t], 0.0), moe_added, t + 1)
            dve.wait_ge(final_row_loaded, 16)
            for t in range(TT):
                dve.wait_ge(last_rstd, t + 1)
                dve.scalar_tensor_tensor(out=h[:, t, :], in0=h[:, t, :], scalar=rstd[:, t:t + 1],
                                         in1=final_row, op0=ALU.mult, op1=ALU.mult).then_inc(out_ready, 1)

        @block.tensor
        def _(pe):
            pe.wait_ge(consts_made, CONSTS)
            pe.wait_ge(rows_loaded, 16 * ROW_LOADS)
            pe.wait_ge(skip_ready, 1)
            pe.transpose(ps[:, 0, 0:ROWS], rows[0:ROWS, :], ident[0:ROWS, 0:ROWS]).then_inc(chan_ps, 1)
            pe.wait_ge(xn_ready, 2)
            for k in range(KD):
                for t in range(TT):
                    mm = pe.transpose(ps[:, 4 + k // 2, (k % 2) * T + t * P:(k % 2) * T + t * P + P],
                                      xn[:, t, k * P:k * P + P], ident[:, :])
                if k % 2:
                    mm.then_inc(xT_ps, 1)
            pe.wait_ge(xT_dve, 2)
            pe.wait_ge(xT_act, 4)
            pe.wait_ge(wdt_loaded, 16)
            for t in range(TT):
                for k in range(KD):
                    mm = pe.matmul(ps[:, 4, t * HEADS:t * HEADS + HEADS], xnT[:, k, t * P:t * P + P],
                                   wdt[:, k, :], start=(k == 0), stop=(k == KD - 1))
            mm.then_inc(dt_ps, 1)

            def w_in_block(slot, use, bank):
                pe.wait_ge(wblk_full[slot], use * 16 + 16)
                w = wblk[:, slot, :].rearrange("p (k n) -> p k n", k=KD)
                for s in range(2):
                    for k in range(KD):
                        mm = pe.matmul(ps[:, bank, s * T:s * T + T], w[:, k, s * P:s * P + P], xnT[:, k, :],
                                       start=(k == 0), stop=(k == KD - 1))
                mm.then_inc(blk_done, 1)

            for b in range(A_BLOCKS):
                if b >= 4:
                    pe.wait_ge(conv_sum, b - 3)
                w_in_block(b % WSLOTS, b // WSLOTS, b % 4)
                if b == 1:
                    pe.wait_ge(adt_ready, 1)
                    pe.matmul(ps[:, 5, 0:TT * HEADS], upto[:, :], adt, start=True, stop=True)
                    pe.matmul(ps[:, 5, 32:48], after[:, :], adt[:, 0:HEADS], start=True, stop=True)
                    for c in range(TT):
                        mm = pe.matmul(ps[0:HEADS, 5, 64 + c * P:64 + c * P + P],
                                       adt[:, c * HEADS:c * HEADS + HEADS], upto[:, :], start=True, stop=True)
                    mm.then_inc(acum_ps, 1)

            def b_turn(q):
                for j in range(4):
                    b = A_BLOCKS + j
                    if isinstance(q, int):
                        pe.wait_ge(conv_sum, b - 3)
                    else:
                        pe.wait_ge((zs_ready, gc_ready, prod_ready, sc_ready)[j], q)
                    w_in_block(b % WSLOTS, q + b // WSLOTS, b % 4)

            b_turn(0)
            pe.wait_ge(acumT_ready, 1)
            pe.wait_ge(decay_ready, 1)
            pe.wait_ge(xbc_ready, A_BLOCKS)
            for c in range(TT):
                for k in range(KD):
                    mm = pe.transpose(ps[:, 4 + 2 * c + k // 4, (k % 4) * P:(k % 4) * P + P],
                                      xs[:, k, c * P:c * P + P], ident[:, :])
                    if k % 4 == 3:
                        mm.then_inc(xs_tok_ps, 1)
            pe.wait_ge(xdt_ready, 1)
            for c in range(TT):
                for g in range(GROUPS):
                    mm = pe.matmul(ps[:, 4, (c * GROUPS + g) * P:(c * GROUPS + g) * P + P],
                                   bcT[:, g, c * P:c * P + P], bcT[:, 2 + g, c * P:c * P + P],
                                   start=True, stop=True)
            mm.then_inc(cb_ps, 1)
            pe.wait_ge(xdt_ready, 2)
            for g in range(GROUPS):
                mm = pe.transpose(ps[:, 5, g * NSTATE:g * NSTATE + NSTATE], bcT[:, g, 0:P], ident[:, :])
            mm.then_inc(cb_ps, 1)
            with pe.Fori(1, B_TURNS) as q:
                b_turn(q)

            pe.wait_ge(xdd_ready, 1)
            pe.wait_ge(btok_ready, 1)
            pe.wait_ge(xdt_ready, 4)
            for g in range(GROUPS):
                mm = pe.matmul(ps[:, 6 + g, :], btok[:, g * NSTATE:g * NSTATE + NSTATE],
                               xdd[:, g * 512:g * 512 + 512], start=True, stop=True)
            mm.then_inc(state_ps, 1)
            pe.wait_ge(sc_scaled, 4 * B_TURNS)
            for t in range(TT):
                for k in range(KD):
                    mm = pe.matmul(ps[:, 0, t:t + 1], sq_sc[:, k, t * P:t * P + P], ones[:, 0:1],
                                   start=(k == 0), stop=(k == KD - 1))
            mm.then_inc(ms_ps, 1)
            pe.wait_ge(cb_taken, 1)
            pe.wait_ge(mt_ready, 6)
            for q in range(KD):
                if q == 0:
                    pe.wait_ge(state_ready, 1)
                for s in range(2):
                    e = 2 * q + s
                    cols = slice(e * HDIM, e * HDIM + HDIM)
                    bank, at_col = 4 + q // 2, (q % 2) * T
                    rows_ = slice(s * HDIM, s * HDIM + HDIM)
                    pe.matmul(ps[rows_, bank, at_col:at_col + P], xdt[:, 0, cols], mt[:, 0, e, :],
                              start=True, stop=True)
                    pe.matmul(ps[rows_, bank, at_col + P:at_col + T], xdt[:, 1, cols], mt[:, 1, e, :],
                              start=True, stop=False)
                    mm = pe.matmul(ps[rows_, bank, at_col + P:at_col + T], state[:, cols], cs[:, e, :],
                                   start=False, stop=True)
                if q % 2:
                    mm.then_inc(y_ps, 1)

            def hT_half(n, m):
                t, half = 1 - n, 1 - m
                pe.wait_ge(mix_taken, 8 + 2 * n + m + 1)
                for k in range(4):
                    c = (4 * half + k) * P
                    mm = pe.transpose(ps[:, 4 + 2 * n + m, k * P:k * P + P], h[:, t, c:c + P], ident[:, :])
                mm.then_inc(hT_ps, 1)

            def logits(n, halves_):
                t = 1 - n
                for m in halves_:
                    if n == 1 and m == 1:
                        pe.wait_ge(hT_act, 1)
                    else:
                        pe.wait_ge(hT_dve, 2 * n + m + 1)
                    for kk in range(4):
                        k = 4 * (1 - m) + kk
                        mm = pe.matmul(ps[:, 4 + 2 * n, 0:E], hT[:, t, k, :], wr[:, k, :],
                                       start=(m == 0 and kk == 0), stop=(m == 1 and kk == 3))
                return mm

            def out_group(g, blocks, src, tile0, bank0):
                for n, i in enumerate(blocks):
                    b = LAST + i
                    pe.wait_ge(wblk_full[b % WSLOTS], 16 * (b // WSLOTS + 1))
                    w = wblk[:, b % WSLOTS, :].rearrange("p (k n) -> p k n", k=2)
                    for kk in range(2):
                        k = tile0 + 2 * n + kk
                        final = n == len(blocks) - 1 and kk == 1
                        for r in range(4):
                            t, half = divmod(3 - r, 2)
                            mm = pe.matmul(ps[:, bank0 + 3 - r, :], src[:, k, t * P:t * P + P],
                                           w[:, kk, half * 512:half * 512 + 512],
                                           start=(n == 0 and kk == 0), stop=final)
                            if final and r < 3:
                                mm.then_inc(mix_ps, 1)
                    if final:
                        mm.then_inc(mix_ps, 1)
                    else:
                        mm.then_inc(blk_done, 1)

            pe.wait_ge(sc_ready, B_TURNS)
            pe.wait_ge(ms_ready, 1)
            out_group(0, range(0, 4), gsc, 0, 0)
            pe.wait_ge(g_scaled, KD)
            for g in range(2):
                for t in range(TT):
                    for k in range(4):
                        mm = pe.matmul(ps[:, 4, 2 * g + t:2 * g + t + 1], sq_ssd[:, 4 * g + k, t * P:t * P + P],
                                       ones[:, 0:1], start=(k == 0), stop=(k == 3))
            mm.then_inc(ms_ps, 1)
            pe.wait_ge(ms_ready, 2)
            out_group(1, range(4, 6), xs, 0, 4)
            pe.wait_ge(mix_taken, 4)
            w = []
            for i in (6, 7):
                b = LAST + i
                pe.wait_ge(wblk_full[b % WSLOTS], 16 * (b // WSLOTS + 1))
                w.append(wblk[:, b % WSLOTS, :].rearrange("p (k n) -> p k n", k=2))
            for r in range(4):
                t, half = divmod(3 - r, 2)
                if r == 3:
                    hT_half(0, 0)
                    hT_half(0, 1)
                for k in range(4):
                    mm = pe.matmul(ps[:, 3 - r, :], xs[:, 4 + k, t * P:t * P + P],
                                   w[k // 2][:, k % 2, half * 512:half * 512 + 512],
                                   start=(k == 0), stop=(k == 3))
                mm.then_inc(mix_ps, 1)
            pe.wait_ge(moe_params, 64)
            pe.wait_ge(wr_ready, 1)
            hT_half(1, 0)
            logits(0, (0, 1)).then_inc(logit_ps, 1)
            hT_half(1, 1)
            logits(1, (0, 1)).then_inc(logit_ps, 1)
            pe.wait_ge(mask_ready, 2)
            pe.matmul(ps[:, 6, 0:E], before[:, :], mask[:, 0, :], start=True, stop=True)
            pe.matmul(ps[:, 6, E:2 * E], before[:, :], mask[:, 1, :], start=True, stop=False)
            pe.matmul(ps[:, 6, E:2 * E], ones[:, :], mask[:, 0, :], start=False, stop=True)
            pe.matmul(ps[:, 6, 2 * E:3 * E], ones[:, :], mask[:, 0, :], start=True, stop=False)
            pe.matmul(ps[:, 6, 2 * E:3 * E], ones[:, :], mask[:, 1, :], start=False, stop=True)\
                .then_inc(pos_ps, 1)

            def gather(g):
                pe.wait_ge(sel_ready, g + 1)
                if isinstance(g, int):
                    pe.wait_ge(x2_ready, 2)
                for k in range(KD):
                    for t in range(TT):
                        mm = pe.matmul(ps[:, 4 + k // 4, (k % 4) * P:(k % 4) * P + P],
                                       x2[:, t, k * P:k * P + P], sel[:, t, :], start=(t == 0), stop=(t == TT - 1))
                mm.then_inc(gather_ps, 1)

            def halves(bank, lhs, w, first, last):
                for a in range(2):
                    mm = pe.matmul(ps[a * 64:a * 64 + 64, bank, :], lhs[:, a * 64:a * 64 + 64], w[a],
                                   start=first, stop=last, skip_group_check=True)
                    yield mm

            def item(i, g, t, u):
                pe.wait_ge(sele_ready, g + 1)
                for n in range(4):
                    pe.matmul(ps[:, n, :], sele[0:E, :], bgu[0:E, n * 512:n * 512 + 512], start=True,
                              stop=False, skip_group_check=True)
                pe.wait_ge(xsel_ready, g + 1)

                def chunk_pair(step):
                    c = u * CHUNKS + 2 * step
                    slots_ = []
                    for a in range(2):
                        pe.wait_ge(ring_full[(c + a) % RING], t * 48 + 16 * ((c + a) // RING + 1))
                        slots_.append(ring[:, (c + a) % RING, :])
                    return slots_

                for step in range(4):
                    w = [s.rearrange("p (k n) -> p k n", k=2) for s in chunk_pair(step)]
                    for kk in range(2):
                        k = 2 * step + kk
                        for n in range(4):
                            for mm in halves(n, xsel[:, k, :], [v[:, kk, n * 512:n * 512 + 512] for v in w],
                                             False, k == KD - 1):
                                if kk == 1 and n == 3:
                                    mm.then_inc(chunk_done, 1)
                gather(g + 1)
                for n in range(2):
                    pe.matmul(ps[:, 6 + n, :], sele[0:E, :], bdn[0:E, n * 512:n * 512 + 512], start=True,
                              stop=False, skip_group_check=True)
                for n in range(2):
                    pe.wait_ge(hid_ready, i * 2 + (n + 1))
                    for f in range(4):
                        mm = pe.transpose(ps[:, n, f * P:f * P + P], hid[:, (4 * n + f) * P:(4 * n + f) * P + P],
                                          ident[:, :])
                    mm.then_inc(hidT_ps, 1)
                pe.wait_ge(selg_ready, i + 1)
                for tt in range(TT):
                    mm = pe.transpose(ps[:, 2, tt * P:tt * P + P], selg[:, tt, :], ident[:, :])
                mm.then_inc(gT_ps, 1)
                for step in range(2):
                    w = [s.rearrange("p (k n) -> p k n", k=4) for s in chunk_pair(4 + step)]
                    pe.wait_ge(hidT_ready, i * 2 + (step + 1))
                    for kk in range(4):
                        f = 4 * step + kk
                        for n in range(2):
                            for mm in halves(6 + n, hidT[:, f, :], [v[:, kk, n * 512:n * 512 + 512] for v in w],
                                             False, f == KD - 1):
                                if kk == 3 and n == 1:
                                    mm.then_inc(chunk_done, 1)
                pe.wait_ge(gT_ready, i + 1)
                for n in range(4):
                    half, tt = divmod(n, 2)
                    if tt == 0:
                        pe.wait_ge(oute_ready, i * 2 + 2)
                        if half:
                            pe.wait_ge(xsel_ready, g + 2)
                    pe.matmul(ps[:, [6, 7, 4, 5][n], :], gT[:, tt, :], oute[:, half * 512:half * 512 + 512],
                              start=True, stop=True).then_inc(add_ps, 1)

            def expert_pass(rnd):
                g0, i0, t0 = rnd * (PAIRS + 1), rnd * PAIRS, rnd * (PAIRS // 2)
                gather(g0)
                with pe.Fori(0, PAIRS // 2) as t:
                    for u in range(2):
                        item(i0 + t * 2 + u, g0 + t * 2 + u, t0 + t, u)

            pe.wait_ge(moe_params, 64)
            expert_pass(0)
            with pe.If(flag_set(pe)):
                with pe.Fori(1, ROUNDS) as rnd:
                    expert_pass(rnd)


_INS = ['x', 'norm1_w', 'w_in', 'ssd_conv_w', 'ssd_conv_b', 'dt_bias', 'a_log', 'd_skip', 'ssd_norm_w',
        'sc_conv_w', 'sc_norm_w', 'w_out', 'norm2_w', 'w_router', 'b_router', 'w_gate_up', 'b_gate_up',
        'w_down', 'b_down', 'final_norm_w']


def kernel(**inputs):
    import numpy as _np
    import concourse.bacc as _bacc
    from concourse import mybir as _mybir
    from concourse.bass_utils import run_bass_kernel_spmd as _run

    nc = _bacc.Bacc("TRN2", target_bir_lowering=False, num_devices=1)
    arrays, args = {}, []
    for name in _INS:
        a = _np.ascontiguousarray(inputs[name])
        if name != 'final_norm_w':
            a = a.reshape(a.shape[1:])
        arrays[f"in_{name}"] = a
        args.append(nc.dram_tensor(f"in_{name}", a.shape, _mybir.dt.from_np(a.dtype), kind="ExternalInput").ap())
    out = nc.dram_tensor("out", (256, 1024), _mybir.dt.float32, kind="ExternalOutput").ap()
    hybrid_layer(nc, *args, out)
    r = _run(nc, [arrays], core_ids=[0])
    return r.results[0]["out"].reshape(1, 256, 1024)
```

```python
import concourse.bass as bass
from concourse import mybir
from contextlib import ExitStack

F32 = mybir.dt.float32
F32R = mybir.dt.float32r
I32 = mybir.dt.int32
U32 = mybir.dt.uint32
ALU = mybir.AluOpType
ACT = mybir.ActivationFunctionType
AX = mybir.AxisListType
ds = bass.ds

P = 128
D = 1024
T = 256
TT = T // P
KD = D // P
HEADS = 16
HDIM = D // HEADS
GROUPS = 2
NSTATE = 128
XBC = D + 2 * GROUPS * NSTATE
XT = XBC // P
SSD_TAPS = 4
SC_TAPS = 3
E = 32
TOPK = 4
FF = 1024
EPS = 1e-5
LIMIT = 7.0
SW_ALPHA = 1.702

C_Z, C_XBC = 0, D
C_DT = C_XBC + XBC
C_GB = C_DT + HEADS
C_GC = C_GB + D
C_U = C_GC + D

BLK = 256
A_BLOCKS = XBC // BLK
B_TURNS = D // BLK
WSLOTS = 4

SLOTS = 64
ROUNDS = T // SLOTS
PAIRS = E // 2
RING = 8
CHUNKS = 12
EPAD = E + 2

R_DS = 0
R_N1 = R_DS + KD
R_CW = R_N1 + KD
R_CB = R_CW + SSD_TAPS * XT
R_SCW = R_CB + XT
R_SN = R_SCW + SC_TAPS * KD
R_SCN = R_SN + KD
R_N2 = R_SCN + KD
ROWS = R_N2 + KD


def spread(ap, axis, n):
    shape = list(ap.shape)
    index = [slice(None)] * len(shape)
    index.insert(axis, None)
    shape.insert(axis, n)
    return ap[tuple(index)].broadcast_to(shape)


class Chain:

    def __init__(self, eng, sem):
        self.eng, self.sem, self.n, self.base = eng, sem, 0, 0

    def turn(self, turn, steps):
        self.base, self.n = turn * steps, 0

    def add(self, ins):
        self.n += 1
        ins.then_inc(self.sem, 1)

    def step(self, ins):
        self.add(ins)
        self.eng.wait_ge(self.sem, self.base + self.n)


def hybrid_layer(nc, x, norm1_w, w_in, ssd_conv_w, ssd_conv_b, dt_bias, a_log, d_skip, ssd_norm_w,
                 sc_conv_w, sc_norm_w, w_out, norm2_w, w_router, b_router, w_gate_up, b_gate_up,
                 w_down, b_down, final_norm_w, out):
    acum_dram = nc.dram_tensor("acum_scratch", (TT, HEADS, P), F32).ap()

    with ExitStack() as ctx:
        def sb(name, shape, dt=F32):
            return ctx.enter_context(nc.sbuf_tensor(name, shape, dt))

        def sem(name):
            return ctx.enter_context(nc.semaphore(name))

        base = -(-nc.sbuf_base // 32) * 32
        ring = sb("ring", [P, RING, 4096])
        work = sb("work", [P, 17664])

        def over(name, shape, at_float):
            return nc.alloc_sbuf_tensor_at(name, shape, F32R, offset=base + 4 * at_float)

        xg_hi = over("xg_hi", [P, KD, T], 5 * 4096)
        xg_lo = over("xg_lo", [P, KD, T], 5 * 4096 + 2048)
        whi = over("whi", [P, 2, 2048], 6 * 4096)
        wlo = over("wlo", [P, 2, 2048], 7 * 4096)
        gsc_hi = over("gsc_hi", [P, KD, T], RING * 4096 + 12288)
        gsc_lo = over("gsc_lo", [P, KD, T], RING * 4096 + 14336)
        bgu_parts = over("bgu_parts", [P, 2 * FF], RING * 4096 + 10240)
        bdn_parts = over("bdn_parts", [P, D], RING * 4096 + 16384)
        bias_hi = sb("bias_hi", [P, 512], F32R)
        sele = sb("sele", [P, P], F32R)
        ident = sb("ident", [P, P])
        upto = sb("upto", [P, P])
        after = sb("after", [P, P])
        before = sb("before", [P, P])
        ones = sb("ones", [P, P])
        iota = sb("iota", [P, T])
        chan = sb("chan", [P, ROWS])
        small = sb("small", [P, 640])

        used = [0]

        def part(n):
            a = small[:, used[0]:used[0] + n]
            used[0] += n
            return a

        dtb_row = part(HEADS)
        a_row = part(HEADS)
        dt_x = part(TT * HEADS)
        dt_s = part(TT * HEADS)
        dt_y = part(TT * HEADS)
        dtv = part(TT * HEADS)
        adt = part(TT * HEADS)
        acum_at = used[0]
        acum_j = part(TT * HEADS)
        decay_sum = part(HEADS)
        decay_out = part(HEADS)
        sumsq = part(TT)
        sumsq2 = part(2 * TT)
        rstd = part(TT)
        power = part(3 * TT)
        mix_ms = part(3 * TT)
        mix_rstd = part(3 * TT)
        br_row = part(E)
        top8 = part(TT * 8)
        negmax = part(TT)
        topi_f = part(TT * 8)
        gsum = part(TT)
        cnt = part(8)
        skip2 = part(2)
        posm = part(TT * EPAD)
        gates = part(TT * EPAD)
        route = sb("route", [P, 256])
        topi = sb("topi", [P, TT, 8], U32)
        overflow = sb("overflow", [P, 1], I32)

        flat = ring[:, :, :].rearrange("p s n -> p (s n)")
        at = [0]

        def scratch(n):
            a = flat[:, at[0]:at[0] + n]
            at[0] += n
            return a

        zs = scratch(KD * T).rearrange("p (n t) -> p n t", n=KD)
        xn = zs.rearrange("p n t -> p (n t)").rearrange("p (t d) -> p t d", t=TT)
        bcT = scratch(4 * T).rearrange("p (n t) -> p n t", n=4)
        xdt = scratch(TT * D).rearrange("p (c d) -> p c d", c=TT)
        mt = scratch(TT * HEADS * P).rearrange("p (c e i) -> p c e i", c=TT, e=HEADS)
        cs = scratch(HEADS * P).rearrange("p (e i) -> p e i", e=HEADS)
        xdd = scratch(D)
        state = xdd
        btok = scratch(GROUPS * NSTATE)
        cbt = scratch(TT * GROUPS * P).rearrange("p (c g i) -> p c g i", c=TT, g=GROUPS)
        sig = scratch(2 * T)
        gcs = scratch(2 * T)
        prod = scratch(2 * T)
        conv = scratch(2 * T)
        sq_turn = scratch(2 * T)
        wdt = scratch(KD * HEADS).rearrange("p (k n) -> p k n", k=KD)
        rows = scratch(P)
        acumT = scratch(TT * P)
        dtT = acumT
        FREE_AFTER_SCAN = 4
        assert at[0] <= FREE_AFTER_SCAN * 4096
        at[0] = FREE_AFTER_SCAN * 4096
        sq_ssd = scratch(KD * T).rearrange("p (n t) -> p n t", n=KD)
        xnT = sq_ssd
        sq_sc = scratch(2 * T)
        FREE_AFTER_SUMS = 5
        assert at[0] <= FREE_AFTER_SUMS * 4096

        wblk = work[:, 0:8192].rearrange("p (s n) -> p s n", s=WSLOTS)
        h = work[:, 8192:10240].rearrange("p (t d) -> p t d", t=TT)
        xs = work[:, 10240:12288].rearrange("p (n t) -> p n t", n=KD)
        bgu = work[:, 10240:12288]
        bdn = work[:, 16384:17408]
        wr = work[:, 17408:17664].rearrange("p (k n) -> p k n", k=KD)
        xsel = work[:, 0:1024].rearrange("p (k j) -> p k j", k=KD)
        gate = work[:, 1024:2048]
        up = work[:, 2048:3072]
        hid = work[:, 3072:4096]
        x2 = work[:, 4096:6144].rearrange("p (t d) -> p t d", t=TT)
        hidT = gate.rearrange("p (f j) -> p f j", f=KD)
        oute = up
        hT = work[:, 6144:8192].rearrange("p (t k j) -> p t k j", t=TT, k=KD)
        weighted = (work[:, 0:1024], hid)
        final_row = work[:, 6144:7168]
        sel = work[:, 7168:7424].rearrange("p (t j) -> p t j", t=TT)
        selg = work[:, 7424:7680].rearrange("p (t j) -> p t j", t=TT)
        gT = work[:, 7680:7936].rearrange("p (t j) -> p t j", t=TT)
        chunk0 = work[:, 12288:16384]
        masks = route[:, 0:TT * E]
        mask = masks.rearrange("p (t e) -> p t e", t=TT)
        logit = route[:, 64:64 + TT * E].rearrange("p (t e) -> p t e", t=TT)
        hot = route[:, 128:128 + TOPK * E].rearrange("p (n e) -> p n e", n=TOPK)

        posm3 = posm.rearrange("p (t e) -> p t e", t=TT)
        gates3 = gates.rearrange("p (t e) -> p t e", t=TT)

        ps = ctx.enter_context(nc.psum_tensor("ps", [P, 8, 512], F32))

        consts_made = sem("consts_made")
        x_loaded = [sem(f"x_loaded{t}") for t in range(TT)]
        rows_loaded = sem("rows_loaded")
        wdt_loaded = sem("wdt_loaded")
        dt_rows_loaded = sem("dt_rows_loaded")
        wblk_full = [sem(f"wblk_full{s}") for s in range(WSLOTS)]
        acum_stored = sem("acum_stored")
        acum_spread = [sem("acum_spread_mt"), sem("acum_spread_cs")]
        moe_params = sem("moe_params")
        bgu_loaded = sem("bgu_loaded")
        bias_hi_ready = sem("bias_hi_ready")
        bias_parts_ready = sem("bias_parts_ready")
        final_row_loaded = sem("final_row_loaded")
        chunk0_full = sem("chunk0_full")
        last_half = sem("last_half")
        ring_full = [sem(f"ring_full{s}") for s in range(RING)]
        out_stored = sem("out_stored")
        act_step = sem("act_step")
        dve_step = sem("dve_step")
        pool_step = sem("pool_step")
        sumsq_ready = sem("sumsq_ready")
        rstd_ready = sem("rstd_ready")
        xn_ready = sem("xn_ready")
        skip_ready = sem("skip_ready")
        chan_ps = sem("chan_ps")
        chan_ready = sem("chan_ready")
        xT_ps = sem("xT_ps")
        xT_dve = sem("xT_dve")
        xT_act = sem("xT_act")
        dt_ps = sem("dt_ps")
        dtT_ready = sem("dtT_ready")
        dtx_ready = sem("dtx_ready")
        dt_exp = sem("dt_exp")
        adt_ready = sem("adt_ready")
        acum_ps = sem("acum_ps")
        acumT_ready = sem("acumT_ready")
        decay_ready = sem("decay_ready")
        xhi_ready = sem("xhi_ready")
        xlo_ready = sem("xlo_ready")
        hi_ready = sem("hi_ready")
        lo_dve = sem("lo_dve")
        lo_pool = sem("lo_pool")
        sc_lo_ready = sem("sc_lo_ready")
        g_lo_ready = sem("g_lo_ready")
        blk_done = sem("blk_done")
        zs_ready = sem("zs_ready")
        prod_ready = sem("prod_ready")
        conv_tap = sem("conv_tap")
        conv_sum = sem("conv_sum")
        conv_sig = sem("conv_sig")
        xbc_ready = sem("xbc_ready")
        xs_tok_ps = sem("xs_tok_ps")
        xdt_ready = sem("xdt_ready")
        cb_ps = sem("cb_ps")
        cb_taken = sem("cb_taken")
        seg_ready = sem("seg_ready")
        seg_exp = sem("seg_exp")
        cs_exp = sem("cs_exp")
        mt_ready = sem("mt_ready")
        xdd_ready = sem("xdd_ready")
        btok_ready = sem("btok_ready")
        state_ps = sem("state_ps")
        state_ready = sem("state_ready")
        z_sig = sem("z_sig")
        gc_ready = sem("gc_ready")
        sc_ready = sem("sc_ready")
        sc_scaled = sem("sc_scaled")
        sc_squared = sem("sc_squared")
        sc_summed = sem("sc_summed")
        g_summed = sem("g_summed")
        y_ps = sem("y_ps")
        g_ready = sem("g_ready")
        g_scaled = sem("g_scaled")
        ms_ps = sem("ms_ps")
        ms_ready = sem("ms_ready")
        mix_rstd_ready = sem("mix_rstd_ready")
        mix_ps = sem("mix_ps")
        mix_taken = sem("mix_taken")
        wr_ready = sem("wr_ready")
        sumsq2_ready = sem("sumsq2_ready")
        rstd2_ready = sem("rstd2_ready")
        x2_ready = sem("x2_ready")
        hT_ps = sem("hT_ps")
        hT_dve = sem("hT_dve")
        hT_act = sem("hT_act")
        logit_ps = sem("logit_ps")
        max_ready = sem("max_ready")
        exp_ready = sem("exp_ready")
        mask_ready = sem("mask_ready")
        pos_ps = sem("pos_ps")
        slots_ready = sem("slots_ready")
        bias_made = sem("bias_made")
        add_taken = sem("add_taken")
        route_ready = sem("route_ready")
        dve_moe = sem("dve_moe")
        sel_ready = sem("sel_ready")
        sele_ready = sem("sele_ready")
        selg_ready = sem("selg_ready")
        gather_ps = sem("gather_ps")
        xsel_ready = sem("xsel_ready")
        chunk_done = sem("chunk_done")
        gate_ps = sem("gate_ps")
        up_ready = sem("up_ready")
        down_ps = sem("down_ps")
        gate_ready = sem("gate_ready")
        gate_sig = sem("gate_sig")
        hid_ready = sem("hid_ready")
        hidT_ps = sem("hidT_ps")
        hidT_ready = sem("hidT_ready")
        gT_ps = sem("gT_ps")
        gT_ready = sem("gT_ready")
        oute_ready = sem("oute_ready")
        add_ps = sem("add_ps")
        moe_added = sem("moe_added")
        last_sq = sem("last_sq")
        last_rstd = sem("last_rstd")
        weighted_ready = sem("weighted_ready")
        out_ready = sem("out_ready")

        CONSTS = 7
        GATHER_PARTS = (slice(0, 2), slice(2, 4), slice(4, KD))
        ADD_BANKS = (2, 3, 6, 7)
        ROW_LOADS = 8
        LAST = A_BLOCKS + 4 * B_TURNS
        OUT_BLOCKS = 8
        OUT_ROWS = [D + 256 * i for i in range(4)] + [256 * i for i in range(4)]

        BLOCKS = LAST + OUT_BLOCKS

        def wait_block(eng, b):
            if b == LAST + 3:
                eng.wait_ge(mix_ps, 4)
            elif b == LAST + 4:
                eng.wait_ge(blk_done, LAST + 4)
            elif b == LAST + 5:
                eng.wait_ge(mix_ps, 8)
            else:
                eng.wait_ge(blk_done, b + 1)

        BIAS_PIECES = [(raw, parts_, slice(c, c + 512)) for raw, parts_, n in
                       ((bdn, bdn_parts, D), (bgu, bgu_parts, 2 * FF)) for c in range(0, n, 512)]

        block = ctx.enter_context(nc.Block())

        def flag_set(eng):
            return eng.value_load(overflow[0:1, 0:1], min_val=0, max_val=1) > 0

        @block.sync
        def _(sp):
            def w_in_block(slot, col):
                return sp.dma_start(wblk[:, slot, :].rearrange("p (k n) -> p k n", k=KD),
                                    w_in[:, ds(col, BLK)].rearrange("(k p) n -> p k n", p=P))

            for t in range(TT):
                sp.dma_start(h[:, t, :], x[t * P:(t + 1) * P, :]).then_inc(x_loaded[t], 16)
            for at_row, src in ((R_N1, norm1_w.rearrange("(n p) -> n p", p=P)),
                                (R_CW, ssd_conv_w.rearrange("w (n p) -> (w n) p", p=P)),
                                (R_CB, ssd_conv_b.rearrange("(n p) -> n p", p=P)),
                                (R_SCW, sc_conv_w.rearrange("w (n p) -> (w n) p", p=P)),
                                (R_SN, ssd_norm_w.rearrange("(n p) -> n p", p=P)),
                                (R_SCN, sc_norm_w.rearrange("(n p) -> n p", p=P)),
                                (R_N2, norm2_w.rearrange("(n p) -> n p", p=P))):
                sp.dma_start(rows[at_row:at_row + src.shape[0], :], src).then_inc(rows_loaded, 16)
            sp.dma_start(skip2[0:KD, :], d_skip.rearrange("(q a) -> q a", a=2)).then_inc(rows_loaded, 16)
            for b in range(A_BLOCKS):
                if b >= WSLOTS:
                    sp.wait_ge(lo_dve, b - WSLOTS + 1)
                    sp.wait_ge(lo_pool, b - WSLOTS + 1)
                w_in_block(b % WSLOTS, C_XBC + BLK * b).then_inc(wblk_full[b % WSLOTS], 16)
            with sp.Fori(0, B_TURNS) as q:
                for j, col in enumerate((C_Z, C_GC, C_U, C_GB)):
                    b = A_BLOCKS + j
                    sp.wait_ge(lo_dve, q * 4 + (b - WSLOTS + 1))
                    sp.wait_ge(lo_pool, q * 4 + (b - WSLOTS + 1))
                    w_in_block(b % WSLOTS, q * BLK + col).then_inc(wblk_full[b % WSLOTS], 16)
            def w_out_block(i):
                b = LAST + i
                sp.wait_ge(lo_dve, b - WSLOTS + 1)
                sp.wait_ge(lo_pool, b - WSLOTS + 1)
                sp.dma_start(wblk[:, b % WSLOTS, :].rearrange("p (k n) -> p k n", k=2),
                             w_out[OUT_ROWS[i]:OUT_ROWS[i] + 2 * P, :].rearrange("(k p) n -> p k n", p=P))\
                    .then_inc(wblk_full[b % WSLOTS], 16)

            def load_chunk(pair, c, first=False):
                e = (pair + c // CHUNKS) * 2 + c % 2
                step = c % CHUNKS // 2
                slot = (c - 1) % RING
                dst, full = ring[:, slot, :], ring_full[slot]
                if first and c == 0:
                    dst, full = chunk0, chunk0_full
                if step < 4:
                    src = w_gate_up[ds(e, 1), step * 256:step * 256 + 256, :]
                    sp.dma_start(dst.rearrange("p (k n) -> p k n", k=2),
                                 src.rearrange("o (k p) n -> p (o k) n", p=P)).then_inc(full, 16)
                else:
                    step -= 4
                    src = w_down[ds(e, 1), step * 512:step * 512 + 512, :]
                    sp.dma_start(dst.rearrange("p (k n) -> p k n", k=4),
                                 src.rearrange("o (k p) n -> p (o k) n", p=P)).then_inc(full, 16)

            def load_pass(rnd, first):
                done = rnd * (PAIRS * CHUNKS)
                if not first:
                    for c in range(RING + 1):
                        sp.wait_ge(chunk_done, done + (c - RING + 1))
                        load_chunk(0, c)
                with sp.Fori(0, PAIRS // 2 - 1) as t:
                    for c in range(RING + 1, RING + 1 + 2 * CHUNKS):
                        sp.wait_ge(chunk_done, done + t * (2 * CHUNKS) + (c - RING + 1))
                        load_chunk(t * 2, c)
                t = PAIRS // 2 - 1
                for c in range(RING + 1, 2 * CHUNKS - 2):
                    sp.wait_ge(chunk_done, done + (t * 2 * CHUNKS + c - RING + 1))
                    load_chunk(t * 2, c)
                for half in range(2):
                    for c in range(2 * CHUNKS - 2, 2 * CHUNKS):
                        slot = (c - 1) % RING
                        sp.wait_ge(chunk_done, done + (t * 2 * CHUNKS + c - RING + 1))
                        src = w_down[PAIRS * 2 - 2 + c % 2, 512 + half * 256:512 + half * 256 + 256, :]
                        sp.dma_start(ring[:, slot, half * 2048:half * 2048 + 2048].rearrange("p (k n) -> p k n", k=2),
                                     src.rearrange("(k p) n -> p k n", p=P))\
                            .then_inc(ring_full[slot] if half else last_half, 16)

            for i in range(6):
                w_out_block(i)
            sp.wait_ge(y_ps, 4)
            sp.wait_ge(sc_scaled, 2 * B_TURNS)
            sp.wait_ge(sc_summed, B_TURNS)
            sp.wait_ge(g_ready, 4)
            load_chunk(0, 1)
            sp.wait_ge(g_lo_ready, 4)
            sp.wait_ge(g_scaled, 2 * KD)
            for n in range(2):
                sp.dma_start(bgu[n * E:n * E + E, :], b_gate_up).then_inc(bgu_loaded, 16)
            load_chunk(0, 2)
            w_out_block(6)
            load_chunk(0, 3)
            w_out_block(7)
            load_chunk(0, 4)
            sp.wait_ge(ms_ps, 1)
            load_chunk(0, FREE_AFTER_SUMS)
            sp.wait_ge(mix_ps, 4)
            load_chunk(0, 0, first=True)
            sp.wait_ge(mix_ps, 12)
            for c in range(FREE_AFTER_SUMS + 1, RING + 1):
                load_chunk(0, c)
            load_pass(0, True)
            sp.wait_ge(route_ready, 1)
            with sp.If(flag_set(sp)):
                with sp.Fori(1, ROUNDS) as rnd:
                    load_pass(rnd, False)
            for t in range(TT):
                sp.wait_ge(out_ready, t + 1)
                sp.dma_start(out[t * P:(t + 1) * P, :], weighted[t]).then_inc(out_stored, 16)
            sp.wait_ge(out_stored, 16 * TT)

        @block.gpsimd
        def _(pool):
            chain = Chain(pool, pool_step)
            for tile, value in ((ident, 0.0), (upto, 1.0), (after, 1.0), (before, 1.0), (ones, 1.0)):
                chain.step(pool.memset(tile[:, :], value))
            pool.memset(power, -0.5).then_inc(consts_made, 1)
            for tile, how, fill, sign in ((ident, ALU.not_equal, 1.0, 1), (upto, ALU.is_ge, 0.0, 1),
                                          (after, ALU.is_gt, 0.0, -1), (before, ALU.is_gt, 0.0, 1)):
                pool.affine_select(out=tile[:, :], in_=tile[:, :], compare_op=how, fill=fill, base=0,
                                   pattern=[[sign, P]], channel_multiplier=-sign).then_inc(consts_made, 1)
            pool.iota(iota[:, :], pattern=[[1, T]], base=0, channel_multiplier=0,
                      allow_small_or_imprecise_dtypes=True).then_inc(consts_made, 1)
            pool.memset(cnt[:, 0:1], 0.0).then_inc(consts_made, 1)

            def root(dst, sums, n, scale):
                chain.step(pool.tensor_scalar(dst, sums, scale, EPS, ALU.mult, ALU.add))
                return pool.tensor_tensor(dst, dst, power[:, 0:n], ALU.pow)

            pool.wait_ge(consts_made, CONSTS)
            for t in range(TT):
                pool.wait_ge(sumsq_ready, t + 1)
                root(rstd[:, t:t + 1], sumsq[:, t:t + 1], 1, 1.0 / D).then_inc(rstd_ready, 1)
            def split_lo(slot, ready):
                pool.wait_ge(hi_ready, ready)
                pool.tensor_tensor(wlo[:, slot % 2, 1024:2048], wblk[:, slot, 1024:2048],
                                   whi[:, slot % 2, 1024:2048].bitcast(F32), ALU.subtract).then_inc(lo_pool, 1)

            for b in range(4):
                split_lo(b % WSLOTS, 2 * b + 2)
            pool.wait_ge(acumT_ready, 1)
            pool.dma_start(acum_dram.rearrange("c e i -> e c i"),
                           acumT[0:HEADS, :].rearrange("e (c i) -> e c i", c=TT)).then_inc(acum_stored, 16)
            for b in range(4, 6):
                split_lo(b % WSLOTS, 2 * b + 2)
            pool.wait_ge(acum_stored, 16)
            pool.dma_start(mt.rearrange("p c e i -> p (c e i)"),
                           acum_dram.rearrange("c e i -> (c e i)").partition_broadcast(P))\
                .then_inc(acum_spread[0], 16)
            pool.dma_start(cs.rearrange("p e i -> p (e i)"),
                           acum_dram[1].rearrange("e i -> (e i)").partition_broadcast(P))\
                .then_inc(acum_spread[1], 16)
            for b in range(6, 12):
                split_lo(b % WSLOTS, 2 * b + 2)

            def sc_squares(q):
                pool.wait_ge(sc_ready, q + 1)
                dst = sq_sc if isinstance(q, int) and q == 0 else sq_turn
                pool.tensor_tensor(dst, conv, conv, ALU.mult).then_inc(sc_squared, 1)
                if dst is sq_turn:
                    pool.wait_ge(sc_squared, q + 1)
                    pool.tensor_tensor(sq_sc, sq_sc, sq_turn, ALU.add).then_inc(sc_summed, 1)
                    pool.wait_ge(sc_summed, q)

            sc_squares(0)
            for b in range(12, 16):
                split_lo(b % WSLOTS, 2 * b + 2)
            sc_squares(1)
            pool.wait_ge(xdt_ready, 2)
            pool.wait_ge(decay_ready, 1)
            pool.tensor_tensor(xdd.rearrange("p (e n) -> p e n", e=HEADS),
                               xdt[:, 0, :].rearrange("p (e n) -> p e n", e=HEADS),
                               spread(decay_out, 2, HDIM), ALU.mult).then_inc(xdd_ready, 1)
            with pool.Fori(2, B_TURNS) as q:
                for b in range(8, 12):
                    split_lo(b % WSLOTS, q * 8 + (2 * b + 2))
                sc_squares(q)
            pool.tensor_tensor(sq_sc[:, 0:T], sq_sc[:, 0:T], sq_sc[:, T:2 * T], ALU.add).then_inc(sc_summed, 1)
            pool.wait_ge(moe_params, 64)
            pool.wait_ge(chan_ready, 1)
            pool.tensor_tensor(wr, wr, spread(chan[:, R_N2:R_N2 + KD], 2, E), ALU.mult).then_inc(wr_ready, 1)
            for g in range(GROUPS):
                pool.wait_ge(g_scaled, 8 * (g + 1))
                chain.step(pool.tensor_tensor(sq_ssd[:, 4 * g:4 * g + 2, :], sq_ssd[:, 4 * g:4 * g + 2, :],
                                              sq_ssd[:, 4 * g + 2:4 * g + 4, :], ALU.add))
                pool.tensor_tensor(sq_ssd[:, 4 * g, :], sq_ssd[:, 4 * g, :], sq_ssd[:, 4 * g + 1, :], ALU.add)\
                    .then_inc(g_summed, 1)
            def bias_lo(n):
                raw, parts_, cols = BIAS_PIECES[n]
                pool.wait_ge(bias_hi_ready, 2 * n + 2)
                pool.wait_ge(lo_pool, LAST + 3 + n)
                if n == 2:
                    pool.wait_ge(mix_rstd_ready, 1)
                pool.tensor_tensor(parts_[E:2 * E, cols], raw[E:2 * E, cols], bias_hi[E:2 * E, :].bitcast(F32),
                                   ALU.subtract).then_inc(bias_parts_ready, 1)
                pool.wait_ge(bias_parts_ready, n + 1)

            for n, b in enumerate(range(LAST + 2, LAST + 5)):
                split_lo(b % WSLOTS, 2 * b + 2)
                if n < 2:
                    bias_lo(n)
            pool.wait_ge(ms_ready, 2)
            pool.tensor_tensor(mix_rstd, mix_ms, power, ALU.pow).then_inc(mix_rstd_ready, 1)
            bias_lo(2)
            for b in range(LAST + 5, BLOCKS):
                split_lo(b % WSLOTS, 2 * b + 2)
                bias_lo(b - LAST - 2)
            for n, t in enumerate((1, 0)):
                pool.wait_ge(sumsq2_ready, 2 * n + 2)
                chain.step(pool.tensor_tensor(rstd[:, t:t + 1], sumsq2[:, 2 * t:2 * t + 1],
                                              sumsq2[:, 2 * t + 1:2 * t + 2], ALU.add))
                root(rstd[:, t:t + 1], rstd[:, t:t + 1], 1, 1.0 / D).then_inc(rstd2_ready, 1)
            pool.wait_ge(logit_ps, 2)
            pool.dma_start(final_row, final_norm_w.partition_broadcast(P)).then_inc(final_row_loaded, 16)
            for t in range(TT):
                pool.wait_ge(last_sq, t + 1)
                root(rstd[:, t:t + 1], sumsq[:, t:t + 1], 1, 1.0 / D).then_inc(last_rstd, 1)

        @block.scalar
        def _(act):
            chain = Chain(act, act_step)

            for t in range(TT):
                act.wait_ge(x_loaded[t], 16)
                act.activation(xn[:, t, :], h[:, t, :], ACT.Square, accum_out=sumsq[:, t:t + 1])\
                    .then_inc(sumsq_ready, 1)
            act.dma_start(wdt, w_in[:, C_DT:C_DT + HEADS].rearrange("(k p) n -> p k n", p=P))\
                .then_inc(wdt_loaded, 16)
            def split_hi(b):
                act.wait_ge(wblk_full[b % WSLOTS], 16 * (b // WSLOTS + 1))
                if b >= 2:
                    wait_block(act, b - 2)
                for n in range(2):
                    cols = slice(n * 1024, n * 1024 + 1024)
                    act.activation(whi[:, b % 2, cols], wblk[:, b % WSLOTS, cols], ACT.Copy)\
                        .then_inc(hi_ready, 1)

            act.wait_ge(rstd_ready, 2)
            act.activation(xn[:, 1, :], h[:, 1, :], ACT.Copy, scale=rstd[:, 1:2]).then_inc(xn_ready, 1)
            act.dma_start(dtb_row, dt_bias.partition_broadcast(P)).then_inc(dt_rows_loaded, 16)
            act.dma_start(a_row, a_log.partition_broadcast(P)).then_inc(dt_rows_loaded, 16)

            split_hi(0)
            act.wait_ge(chan_ready, 1)
            for k in range(KD - 2, KD):
                act.wait_ge(xT_ps, k // 2 + 1)
                act.activation(xnT[:, k, :], ps[:, 4 + k // 2, (k % 2) * T:(k % 2) * T + T], ACT.Copy,
                               scale=chan[:, R_N1 + k:R_N1 + k + 1]).then_inc(xT_act, 1)

            for n in range(2):
                act.wait_ge(xT_dve, 2 + n)
                if n == 1:
                    act.wait_ge(xT_act, 2)
                act.activation(xg_hi[:, 4 * n:4 * n + 4, :], xnT[:, 4 * n:4 * n + 4, :], ACT.Copy)\
                    .then_inc(xhi_ready, 1)
            split_hi(1)
            act.dma_start(wr, w_router.rearrange("(k p) n -> p k n", p=P)).then_inc(moe_params, 16)
            act.dma_start(br_row, b_router.partition_broadcast(P)).then_inc(moe_params, 16)
            for n in range(2):
                act.dma_start(bdn[n * E:n * E + E, :], b_down).then_inc(moe_params, 16)
            act.wait_ge(dt_rows_loaded, 32)
            chain.step(act.activation(a_row, a_row, ACT.Exp))
            act.wait_ge(dtx_ready, 1)
            act.activation(dt_s, dt_x, ACT.Exp, scale=-1.0).then_inc(dt_exp, 1)

            def conv_tap_block(b):
                for s in range(2):
                    n = 2 * b + s
                    dst = xs[:, n, :] if n < KD else bcT[:, n - KD, :]
                    act.activation(dst, ps[:, b % 4, s * T:s * T + T], ACT.Identity,
                                   scale=chan[:, R_CW + 3 * XT + n:R_CW + 3 * XT + n + 1],
                                   bias=chan[:, R_CB + n:R_CB + n + 1]).then_inc(conv_tap, 1)

            def conv_sigmoid(b):
                act.wait_ge(conv_sum, b + 1)
                src = xs[:, 2 * b:2 * b + 2, :] if b < 4 else bcT[:, 2 * b - KD:2 * b - KD + 2, :]
                if b > 0:
                    act.wait_ge(xbc_ready, b)
                act.activation(sig.rearrange("p (n t) -> p n t", n=2), src, ACT.Sigmoid).then_inc(conv_sig, 1)

            for b in range(A_BLOCKS):
                split_hi(b + 2)
                if b > 0:
                    conv_sigmoid(b - 1)
                act.wait_ge(blk_done, b + 1)
                conv_tap_block(b)
            conv_sigmoid(A_BLOCKS - 1)

            for q in range(B_TURNS):
                b = A_BLOCKS + 4 * q
                split_hi(b + 2)
                if q == 2:
                    act.wait_ge(acum_spread[1], 16)
                    act.activation(cs, cs, ACT.Exp).then_inc(cs_exp, 1)
                act.wait_ge(blk_done, b + 1)
                if q == 0:
                    act.wait_ge(xbc_ready, A_BLOCKS)
                else:
                    act.wait_ge(zs_ready, q)
                act.activation(sig, ps[:, b % 4, :], ACT.Sigmoid).then_inc(z_sig, 1)
                split_hi(b + 3)
                act.wait_ge(blk_done, b + 2)
                if q > 0:
                    act.wait_ge(prod_ready, q)
                act.activation(gcs, ps[:, (b + 1) % 4, :], ACT.Copy).then_inc(gc_ready, 1)
                if q == 2:
                    act.wait_ge(cb_ps, 2)
                    act.activation(btok, ps[:, 5, 0:GROUPS * NSTATE], ACT.Copy).then_inc(btok_ready, 1)
                if q == 3:
                    act.wait_ge(state_ps, 1)
                    act.activation(state, ps[:, 6:8, :].rearrange("p b n -> p (b n)"), ACT.Copy)\
                        .then_inc(state_ready, 1)
                split_hi(b + 4)
                if q == 1:
                    act.wait_ge(acumT_ready, 1)
                    act.activation(decay_out, decay_sum, ACT.Exp).then_inc(decay_ready, 1)
                    act.wait_ge(seg_ready, 1)
                    act.activation(mt[:, 0], mt[:, 0], ACT.Exp).then_inc(seg_exp, 1)
                split_hi(b + 5)
                if q == 1:
                    act.wait_ge(seg_ready, 2)
                    act.activation(mt[:, 1], mt[:, 1], ACT.Exp).then_inc(seg_exp, 1)
                act.wait_ge(sc_ready, q + 1)
                for s in range(2):
                    n = 2 * q + s
                    act.activation(gsc_hi[:, n, :], conv[:, s * T:s * T + T], ACT.Copy,
                                   scale=chan[:, R_SCN + n:R_SCN + n + 1]).then_inc(sc_scaled, 1)

            for q in range(KD):
                act.wait_ge(g_ready, q // 2 + 1)
                act.activation(xg_hi[:, q, :], xs[:, q, :], ACT.Copy,
                               scale=chan[:, R_SN + q:R_SN + q + 1]).then_inc(g_scaled, 1)
                act.activation(sq_ssd[:, q, :], xs[:, q, :], ACT.Square).then_inc(g_scaled, 1)
            for n, b in enumerate(range(LAST + 2, BLOCKS)):
                split_hi(b)
                raw, parts_, cols = BIAS_PIECES[n]
                if n == 0:
                    act.wait_ge(moe_params, 64)
                elif n == 2:
                    act.wait_ge(bgu_loaded, 32)
                if n > 0:
                    act.wait_ge(bias_parts_ready, n)
                act.activation(parts_[0:E, cols], raw[0:E, cols], ACT.Copy).then_inc(bias_hi_ready, 1)
                act.activation(bias_hi[E:2 * E, :], raw[E:2 * E, cols], ACT.Copy).then_inc(bias_hi_ready, 1)

            for n, t in enumerate((1, 0)):
                for m in range(2):
                    act.wait_ge(mix_taken, 8 + 2 * n + m + 1)
                    cols = slice((1 - m) * 512, (1 - m) * 512 + 512)
                    act.activation(x2[:, t, cols], h[:, t, cols], ACT.Square,
                                   accum_out=sumsq2[:, 2 * t + m:2 * t + m + 1]).then_inc(sumsq2_ready, 1)
                if n == 1:
                    act.wait_ge(hT_ps, 4)
                    act.activation(hT[:, 0, 0:4, :], ps[:, 7, :].rearrange("p (k j) -> p k j", k=4), ACT.Copy)\
                        .then_inc(hT_act, 1)
                act.wait_ge(rstd2_ready, n + 1)
                act.activation(x2[:, t, :], h[:, t, :], ACT.Copy, scale=rstd[:, t:t + 1]).then_inc(x2_ready, 1)
            for n, t in enumerate((1, 0)):
                act.wait_ge(max_ready, n + 1)
                act.activation(gates3[:, t, 0:E], logit[:, t, :], ACT.Exp, bias=negmax[:, t:t + 1])\
                    .then_inc(exp_ready, 1)

            def item(i, g):
                for n in range(2):
                    half = slice(n * 512, n * 512 + 512)
                    act.wait_ge(gate_ready, i * 2 + (n + 1))
                    act.activation(hid[:, half], gate[:, half], ACT.Sigmoid, scale=SW_ALPHA)\
                        .then_inc(gate_sig, 1)
                for n in range(2):
                    act.wait_ge(hidT_ps, i * 2 + (n + 1))
                    act.activation(hidT[:, n * 4:n * 4 + 4, :], ps[:, n, :].rearrange("p (f j) -> p f j", j=P),
                                   ACT.Copy).then_inc(hidT_ready, 1)
                act.wait_ge(gT_ps, i + 1)
                act.activation(gT, ps[:, 2, 0:T].rearrange("p (t j) -> p t j", t=TT), ACT.Copy)\
                    .then_inc(gT_ready, 1)
                for n in range(2):
                    if n == 0:
                        act.wait_ge(down_ps, i + 1)
                    else:
                        act.wait_ge(chunk_done, i * CHUNKS + CHUNKS)
                    act.activation(oute[:, n * 512:n * 512 + 512], ps[:, 6 + n, :], ACT.Copy)\
                        .then_inc(oute_ready, 1)

            def expert_pass(rnd):
                with act.Fori(0, PAIRS) as p:
                    item(rnd * PAIRS + p, rnd * (PAIRS + 1) + p)

            expert_pass(0)
            act.wait_ge(route_ready, 1)
            with act.If(flag_set(act)):
                with act.Fori(1, ROUNDS) as rnd:
                    expert_pass(rnd)

            for t in range(TT):
                act.wait_ge(moe_added, 1)
                act.activation((gate, up)[t], h[:, t, :], ACT.Square, accum_out=sumsq[:, t:t + 1])\
                    .then_inc(last_sq, 1)

        @block.vector
        def _(dve):
            chain = Chain(dve, dve_step)

            def sent(ins, sem_, value):
                ins.then_inc(sem_, 1)
                dve.wait_ge(sem_, value)

            dve.wait_ge(rows_loaded, 16 * ROW_LOADS)
            sent(dve.tensor_copy(rows[R_DS:R_DS + KD, :].rearrange("q (a n) -> q a n", a=2),
                                 spread(skip2[0:KD, :], 2, HDIM)), skip_ready, 1)
            dve.wait_ge(rstd_ready, 1)
            dve.tensor_scalar(xn[:, 0, :], h[:, 0, :], rstd[:, 0:1], None, ALU.mult).then_inc(xn_ready, 1)
            dve.wait_ge(chan_ps, 1)
            sent(dve.tensor_copy(chan[:, :], ps[:, 0, 0:ROWS]), chan_ready, 1)
            for b in range(3):
                dve.wait_ge(xT_ps, b + 1)
                dve.tensor_tensor(xnT[:, 2 * b:2 * b + 2, :], ps[:, 4 + b, :].rearrange("p (k t) -> p k t", k=2),
                                  spread(chan[:, R_N1 + 2 * b:R_N1 + 2 * b + 2], 2, T), ALU.mult)\
                    .then_inc(xT_dve, 1)

            def build_sele(g, p):
                for n in range(2):
                    ins = dve.tensor_copy(sele[n * E:n * E + E, :].rearrange("p (a j) -> p a j", a=2),
                                          spread(ident[n * E:n * E + E, ds(p * 2 + n * E, 2)], 2, SLOTS))
                ins.then_inc(sele_ready, 1)

            def split_lo(b):
                dve.wait_ge(hi_ready, 2 * b + 1)
                dve.tensor_tensor(wlo[:, b % 2, 0:1024], wblk[:, b % WSLOTS, 0:1024],
                                  whi[:, b % 2, 0:1024].bitcast(F32), ALU.subtract).then_inc(lo_dve, 1)

            split_lo(0)
            dve.wait_ge(xT_dve, 3)
            dve.wait_ge(xT_act, 2)
            for n in range(2):
                half = slice(4 * n, 4 * n + 4)
                dve.wait_ge(xhi_ready, n + 1)
                dve.tensor_tensor(xg_lo[:, half, :], xnT[:, half, :], xg_hi[:, half, :].bitcast(F32),
                                  ALU.subtract).then_inc(xlo_ready, 1)
            dve.wait_ge(dt_ps, 1)
            dve.tensor_copy(dtT[0:HEADS, :], ps[0:HEADS, 4, 0:T]).then_inc(dtT_ready, 1)
            split_lo(1)

            dve.wait_ge(dt_ps, 2)
            dve.wait_ge(dt_rows_loaded, 32)
            chain.step(dve.tensor_tensor(dt_y.rearrange("p (c e) -> p c e", c=TT),
                                         ps[:, 4, T:T + TT * HEADS].rearrange("p (c e) -> p c e", c=TT),
                                         spread(dtb_row, 1, TT), ALU.add))
            chain.step(dve.tensor_scalar(dt_x, dt_y, -1.0, None, ALU.mult))
            sent(dve.tensor_tensor(dt_x, dt_x, dt_y, ALU.max), dtx_ready, 1)
            chain.step(dve.tensor_scalar(dt_y, dt_y, 0.0, None, ALU.max))
            dve.wait_ge(dt_exp, 1)
            chain.step(dve.tensor_scalar(dt_x, dt_s, 2.0, None, ALU.add))
            chain.step(dve.reciprocal(dt_x, dt_x))
            chain.step(dve.tensor_tensor(dt_s, dt_s, dt_x, ALU.mult))
            chain.step(dve.tensor_tensor(dt_x, dt_s, dt_s, ALU.mult))
            terms = list(range(15, 1, -2))
            chain.step(dve.tensor_scalar(dtv, dt_x, 2.0 / 17, None, ALU.mult))
            for n in terms:
                chain.step(dve.scalar_tensor_tensor(out=dtv, in0=dtv, scalar=2.0 / n, in1=dt_x,
                                                    op0=ALU.add, op1=ALU.mult))
            chain.step(dve.scalar_tensor_tensor(out=dtv, in0=dtv, scalar=2.0, in1=dt_s,
                                                op0=ALU.add, op1=ALU.mult))
            chain.step(dve.tensor_tensor(dtv, dtv, dt_y, ALU.add))
            dve.wait_ge(act_step, 1)
            sent(dve.scalar_tensor_tensor(out=adt.rearrange("p (c e) -> p c e", c=TT),
                                          in0=dtv.rearrange("p (c e) -> p c e", c=TT), scalar=-1.0,
                                          in1=spread(a_row, 1, TT), op0=ALU.mult, op1=ALU.mult), adt_ready, 1)

            def conv_block(b):
                dve.wait_ge(conv_tap, 2 * b + 2)
                for back in range(1, SSD_TAPS):
                    tap = SSD_TAPS - 1 - back
                    for s in range(2):
                        n = 2 * b + s
                        dst = xs[:, n, :] if n < KD else bcT[:, n - KD, :]
                        ins = dve.scalar_tensor_tensor(
                            out=dst[:, back:], in0=ps[:, b % 4, s * T:s * T + T - back],
                            scalar=chan[:, R_CW + tap * XT + n:R_CW + tap * XT + n + 1],
                            in1=dst[:, back:], op0=ALU.mult, op1=ALU.add)
                        if s == 0:
                            chain.add(ins)
                        elif back < SSD_TAPS - 1:
                            chain.step(ins)
                        else:
                            sent(ins, conv_sum, b + 1)

            def conv_silu(b):
                dst = xs[:, 2 * b:2 * b + 2, :] if b < 4 else bcT[:, 2 * b - KD:2 * b - KD + 2, :]
                dve.wait_ge(conv_sig, b + 1)
                sent(dve.tensor_tensor(dst, dst, sig.rearrange("p (n t) -> p n t", n=2), ALU.mult),
                     xbc_ready, b + 1)

            for b in range(A_BLOCKS):
                split_lo(b + 2)
                if b > 0:
                    conv_silu(b - 1)
                conv_block(b)
                if b == 1:
                    dve.wait_ge(acum_ps, 1)
                    chain.step(dve.tensor_copy(small[:, acum_at:acum_at + 3 * HEADS], ps[:, 5, 0:3 * HEADS]))
                    sent(dve.tensor_copy(acumT[0:HEADS, :], ps[0:HEADS, 5, 64:64 + T]), acumT_ready, 1)
            conv_silu(A_BLOCKS - 1)

            def take_xdt(m):
                c, n = divmod(m, 2)
                dve.wait_ge(xs_tok_ps, m + 1)
                heads = slice(c * HEADS + 8 * n, c * HEADS + 8 * n + 8)
                sent(dve.tensor_tensor(xdt[:, c, n * 512:n * 512 + 512].rearrange("p (e d) -> p e d", e=8),
                                       ps[:, 4 + m, :].rearrange("p (e d) -> p e d", e=8),
                                       spread(dtv[:, heads], 2, HDIM), ALU.mult), xdt_ready, m + 1)

            def difference(c):
                dve.wait_ge(acum_spread[0], 16)
                chain.step(dve.tensor_tensor(mt[:, c], mt[:, c],
                                             spread(acum_j[:, c * HEADS:c * HEADS + HEADS], 2, P), ALU.subtract))

            def cap(c):
                sent(dve.tensor_scalar(mt[:, c], mt[:, c], 0.0, None, ALU.min), seg_ready, c + 1)

            def mask_scores():
                dve.wait_ge(cb_ps, 1)
                sent(dve.tensor_tensor(cbt.rearrange("p c g i -> p (c g) i"),
                                       ps[:, 4, :].rearrange("p (n i) -> p n i", i=P),
                                       spread(upto[:, :], 1, TT * GROUPS), ALU.mult), cb_taken, 1)

            def decayed_scores(m):
                c, g = divmod(m, GROUPS)
                dve.wait_ge(seg_exp, c + 1)
                sent(dve.tensor_tensor(mt[:, c, 8 * g:8 * g + 8, :], mt[:, c, 8 * g:8 * g + 8, :],
                                       spread(cbt[:, c, g, :], 1, 8), ALU.mult), mt_ready, m + 1)

            def decayed_c(g):
                dve.wait_ge(cs_exp, 1)
                sent(dve.tensor_tensor(cs[:, 8 * g:8 * g + 8, :], cs[:, 8 * g:8 * g + 8, :],
                                       spread(bcT[:, 2 + g, P:2 * P], 1, 8), ALU.mult), mt_ready, 5 + g)

            beside = {(0, 0): [lambda: difference(0)],
                      (0, 1): [lambda: cap(0), lambda: difference(1)],
                      (1, 0): [lambda: take_xdt(0), lambda: take_xdt(1), lambda: cap(1)],
                      (1, 1): [lambda: take_xdt(2), lambda: take_xdt(3)],
                      (2, 0): [mask_scores, lambda: decayed_scores(0)],
                      (2, 1): [lambda: decayed_scores(1), lambda: decayed_scores(2)],
                      (3, 0): [lambda: decayed_scores(3), lambda: decayed_c(0)],
                      (3, 1): [lambda: decayed_c(1)]}
            for q in range(B_TURNS):
                b = A_BLOCKS + 4 * q
                for step in range(4):
                    split_lo(b + step + 2)
                    if step == 0:
                        dve.wait_ge(z_sig, q + 1)
                        sent(dve.tensor_tensor(zs[:, 2 * q:2 * q + 2, :],
                                               ps[:, b % 4, :].rearrange("p (n t) -> p n t", n=2),
                                               sig.rearrange("p (n t) -> p n t", n=2), ALU.mult),
                             zs_ready, q + 1)
                    elif step == 2:
                        dve.wait_ge(gc_ready, q + 1)
                        dve.wait_ge(blk_done, b + 3)
                        sent(dve.tensor_tensor(prod, ps[:, (b + 2) % 4, :], gcs, ALU.mult), prod_ready, q + 1)
                        if q > 0:
                            dve.wait_ge(sc_squared, q)
                        for s in range(2):
                            tap = R_SCW + 2 * KD + 2 * q + s
                            ins = dve.tensor_scalar(conv[:, s * T:s * T + T], prod[:, s * T:s * T + T],
                                                    chan[:, tap:tap + 1], None, ALU.mult)
                            (chain.step if s else chain.add)(ins)
                        for back in range(1, SC_TAPS):
                            for s in range(2):
                                tap = R_SCW + (SC_TAPS - 1 - back) * KD + 2 * q + s
                                dst = conv[:, s * T + back:s * T + T]
                                ins = dve.scalar_tensor_tensor(
                                    out=dst, in0=prod[:, s * T:s * T + T - back], scalar=chan[:, tap:tap + 1],
                                    in1=dst, op0=ALU.mult, op1=ALU.add)
                                (chain.step if s else chain.add)(ins)
                    elif step == 3:
                        dve.wait_ge(blk_done, b + 4)
                        sent(dve.tensor_tensor(conv, ps[:, (b + 3) % 4, :], conv, ALU.mult), sc_ready, q + 1)
                        dve.wait_ge(sc_scaled, 2 * q + 2)
                        for s in range(2):
                            n = 2 * q + s
                            dve.scalar_tensor_tensor(
                                out=gsc_lo[:, n, :], in0=conv[:, s * T:s * T + T],
                                scalar=chan[:, R_SCN + n:R_SCN + n + 1], in1=gsc_hi[:, n, :].bitcast(F32),
                                op0=ALU.mult, op1=ALU.subtract).then_inc(sc_lo_ready, 1)
                    for piece in beside.get((q, step), ()):
                        piece()

            for b in range(4):
                dve.wait_ge(y_ps, b + 1)
                for s in range(2):
                    n = 2 * b + s
                    chain.step(dve.scalar_tensor_tensor(
                        out=xs[:, n, :], in0=xs[:, n, :], scalar=chan[:, R_DS + n:R_DS + n + 1],
                        in1=ps[:, 4 + b, s * T:s * T + T], op0=ALU.mult, op1=ALU.add))
                sent(dve.tensor_tensor(xs[:, 2 * b:2 * b + 2, :], xs[:, 2 * b:2 * b + 2, :],
                                       zs[:, 2 * b:2 * b + 2, :], ALU.mult), g_ready, b + 1)

            for n in range(KD):
                dve.wait_ge(g_scaled, 2 * n + 1)
                ins = dve.scalar_tensor_tensor(out=xg_lo[:, n, :], in0=xs[:, n, :],
                                               scalar=chan[:, R_SN + n:R_SN + n + 1],
                                               in1=xg_hi[:, n, :].bitcast(F32), op0=ALU.mult, op1=ALU.subtract)
                if n % 2:
                    ins.then_inc(g_lo_ready, 1)
            split_lo(LAST + 2)
            split_lo(LAST + 3)

            def add_group(g, bank0, quarters=range(4)):
                for n in quarters:
                    t, half = divmod(3 - n, 2)
                    dve.wait_ge(mix_ps, 4 * g + n + 1)
                    cols = slice(half * 512, half * 512 + 512)
                    sent(dve.scalar_tensor_tensor(out=h[:, t, cols], in0=ps[:, bank0 + 3 - n, :],
                                                  scalar=mix_rstd[:, 2 * g + t:2 * g + t + 1],
                                                  in1=h[:, t, cols], op0=ALU.mult, op1=ALU.add),
                         mix_taken, 4 * g + n + 1)

            split_lo(LAST + 4)
            dve.wait_ge(ms_ps, 1)
            dve.tensor_scalar(mix_ms[:, 0:TT], ps[:, 4, 0:TT], 1.0 / D, EPS, ALU.mult, ALU.add)\
                .then_inc(ms_ready, 1)
            dve.tensor_scalar(mix_ms[:, TT:3 * TT], ps[:, 4, TT:3 * TT], 1.0 / 512, EPS, ALU.mult, ALU.add)\
                .then_inc(ms_ready, 1)
            dve.wait_ge(mix_rstd_ready, 1)
            add_group(0, 0)
            split_lo(LAST + 5)
            split_lo(LAST + 6)
            add_group(1, 4)
            split_lo(LAST + 7)
            build_sele(0, 0)

            dve.wait_ge(moe_params, 64)
            def copy_hT(n, m):
                dve.wait_ge(hT_ps, 2 * n + m + 1)
                dve.tensor_copy(hT[:, 1 - n, 4 * (1 - m):4 * (1 - m) + 4, :],
                                ps[:, 4 + 2 * n + m, :].rearrange("p (k j) -> p k j", k=4))\
                    .then_inc(hT_dve, 1)

            add_group(2, 0, range(3))
            copy_hT(0, 0)
            copy_hT(0, 1)
            copy_hT(1, 0)
            for n, t in enumerate((1, 0)):
                if n == 1:
                    add_group(2, 0, (3,))
                dve.wait_ge(rstd2_ready, n + 1)
                dve.wait_ge(logit_ps, n + 1)
                chain.step(dve.scalar_tensor_tensor(out=logit[:, t, :], in0=ps[:, 4 + 2 * n, 0:E],
                                                    scalar=rstd[:, t:t + 1], in1=br_row,
                                                    op0=ALU.mult, op1=ALU.add))
                chain.step(dve.max(top8[:, 8 * t:8 * t + 8], logit[:, t, :]))
                chain.step(dve.max_index(topi[:, t, :], top8[:, 8 * t:8 * t + 8], logit[:, t, :]))
                chain.step(dve.tensor_copy(topi_f[:, 8 * t:8 * t + 8], topi[:, t, :]))
                chain.step(dve.tensor_tensor(hot, spread(iota[:, 0:E], 1, TOPK),
                                             spread(topi_f[:, 8 * t:8 * t + TOPK], 2, E), ALU.is_equal))
                sent(dve.tensor_reduce(mask[:, t, :], hot.rearrange("p n e -> p e n"), AX.X, ALU.add),
                     mask_ready, n + 1)
                sent(dve.tensor_scalar(negmax[:, t:t + 1], top8[:, 8 * t:8 * t + 1], -1.0, None, ALU.mult),
                     max_ready, n + 1)
                if n == 0:
                    chain.step(dve.memset(gates3[:, :, E:EPAD], 0.0))
                    chain.step(dve.memset(posm3[:, :, E:EPAD], -1.0))
            dve.wait_ge(pos_ps, 1)
            chain.step(dve.scalar_tensor_tensor(out=posm3[:, :, 0:E],
                                                in0=ps[:, 6, 0:TT * E].rearrange("p (t e) -> p t e", t=TT),
                                                scalar=1.0, in1=mask, op0=ALU.add, op1=ALU.mult))
            sent(dve.tensor_scalar(posm3[:, :, 0:E], posm3[:, :, 0:E], -1.0, None, ALU.add), slots_ready, 1)

            def finish_routing():
                dve.wait_ge(exp_ready, 2)
                chain.step(dve.tensor_tensor(gates3[:, :, 0:E], gates3[:, :, 0:E], mask, ALU.mult))
                chain.step(dve.tensor_reduce(gsum, gates3[:, :, 0:E], AX.X, ALU.add))
                chain.step(dve.reciprocal(gsum, gsum))
                chain.step(dve.tensor_tensor(gates3[:, :, 0:E], gates3[:, :, 0:E], spread(gsum, 2, E), ALU.mult))
                dve.wait_ge(pos_ps, 2)
                chain.step(dve.tensor_copy(hot[:, 0, :], ps[:, 7, 0:E]))
                chain.step(dve.tensor_tensor(hot[:, 0, :], hot[:, 0, :], ps[:, 7, E:2 * E], ALU.add))
                chain.step(dve.tensor_reduce(cnt[:, 1:2], hot[:, 0, :], AX.X, ALU.max))
                sent(dve.tensor_scalar(overflow[:, :], cnt[:, 1:2], float(SLOTS), None, ALU.is_gt),
                     route_ready, 1)

            moe = Chain(dve, dve_moe)
            ITEM_STEPS = 6
            quad = "p t (a j) -> p t a j"

            def build_sel(g, p, rnd):
                slots = iota[:, ds(rnd * SLOTS, SLOTS)]
                sent(dve.tensor_tensor(sel.rearrange(quad, a=2), spread(spread(slots, 1, 2), 1, TT),
                                       spread(posm3[:, :, ds(p * 2, 2)], 3, SLOTS), ALU.is_equal),
                     sel_ready, g + 1)

            def take_gathered(tiles, n, ks):
                dve.wait_ge(gather_ps, tiles + (n + 1))
                dve.tensor_tensor(xsel[:, ks, :],
                                  ps[:, 4:6, :].rearrange("p b (k j) -> p (b k) j", j=P)[:, ks, :],
                                  spread(chan[:, R_N2 + ks.start:R_N2 + ks.stop], 2, P), ALU.mult)\
                    .then_inc(xsel_ready, 1)

            def item(i, g, p, rnd):
                moe.turn(i, ITEM_STEPS)
                for n, ks in enumerate(GATHER_PARTS):
                    take_gathered(i * 2 + g, n, ks)
                build_sel(g + 1, p + 1, rnd)
                slots = iota[:, ds(rnd * SLOTS, SLOTS)]
                moe.step(dve.tensor_tensor(selg.rearrange(quad, a=2), spread(spread(slots, 1, 2), 1, TT),
                                           spread(posm3[:, :, ds(p * 2, 2)], 3, SLOTS), ALU.is_equal))
                sent(dve.tensor_tensor(selg.rearrange(quad, a=2), selg.rearrange(quad, a=2),
                                       spread(gates3[:, :, ds(p * 2, 2)], 3, SLOTS), ALU.mult),
                     selg_ready, i + 1)
                dve.wait_ge(gate_ps, i + 1)
                for n in range(2):
                    sent(dve.tensor_scalar(gate[:, n * 512:n * 512 + 512], ps[:, n, :], LIMIT, None, ALU.min),
                         gate_ready, i * 2 + (n + 1))
                for n in range(2):
                    half = slice(n * 512, n * 512 + 512)
                    dve.wait_ge(gate_sig, i * 2 + (n + 1))
                    moe.step(dve.tensor_tensor(gate[:, half], gate[:, half], hid[:, half], ALU.mult))
                dve.wait_ge(chunk_done, i * CHUNKS + 8)
                for n in range(2):
                    half = slice(n * 512, n * 512 + 512)
                    sent(dve.tensor_scalar(up[:, half], ps[:, 2 + n, :], LIMIT, -LIMIT, ALU.min, ALU.max),
                         up_ready, i * 2 + (n + 1))
                    sent(dve.scalar_tensor_tensor(out=hid[:, half], in0=up[:, half], scalar=1.0,
                                                  in1=gate[:, half], op0=ALU.add, op1=ALU.mult),
                         hid_ready, i * 2 + (n + 1))
                dve.wait_ge(hidT_ps, i * 2 + 1)
                build_sele(g + 1, p + 1)
                for n in range(4):
                    half, t = divmod(n, 2)
                    cols = slice(half * 512, half * 512 + 512)
                    dve.wait_ge(add_ps, i * 4 + (n + 1))
                    ins = dve.tensor_tensor(h[:, t, cols], h[:, t, cols], ps[:, ADD_BANKS[n], :], ALU.add)
                    if n == 1:
                        sent(ins, add_taken, i + 1)
                    else:
                        moe.step(ins)
                assert moe.n == ITEM_STEPS

            def expert_pass(rnd, many=None):
                g = rnd * (PAIRS + 1)
                if isinstance(rnd, int):
                    build_sel(g, 0, rnd)
                    finish_routing()
                    many.append(flag_set(dve))
                else:
                    take_gathered(rnd * (PAIRS * 3 + 1) - 1, 0, GATHER_PARTS[0])
                    build_sel(g, 0, rnd)
                    dve.wait_ge(bias_made, g)
                    build_sele(g, 0)
                with dve.Fori(0, PAIRS) as p:
                    item(rnd * PAIRS + p, g + p, p, rnd)

            many = []
            expert_pass(0, many)
            with dve.If(many[0]):
                with dve.Fori(1, ROUNDS) as rnd:
                    expert_pass(rnd)

            sent(dve.memset(cnt[:, 3:4], 0.0), moe_added, 1)
            dve.wait_ge(final_row_loaded, 16)
            for t in range(TT):
                dve.tensor_tensor(weighted[t], h[:, t, :], final_row, ALU.mult).then_inc(weighted_ready, 1)
            for t in range(TT):
                dve.wait_ge(weighted_ready, t + 1)
                dve.wait_ge(last_rstd, t + 1)
                dve.tensor_scalar(weighted[t], weighted[t], rstd[:, t:t + 1], None, ALU.mult)\
                    .then_inc(out_ready, 1)

        @block.tensor
        def _(pe):
            pe.wait_ge(consts_made, CONSTS)
            pe.wait_ge(rows_loaded, 16 * ROW_LOADS)
            pe.wait_ge(skip_ready, 1)
            pe.transpose(ps[:, 0, 0:ROWS], rows[0:ROWS, :], ident[0:ROWS, 0:ROWS]).then_inc(chan_ps, 1)
            pe.wait_ge(xn_ready, 2)
            for k in range(KD):
                for t in range(TT):
                    mm = pe.transpose(ps[:, 4 + k // 2, (k % 2) * T + t * P:(k % 2) * T + t * P + P],
                                      xn[:, t, k * P:k * P + P], ident[:, :])
                if k % 2:
                    mm.then_inc(xT_ps, 1)
            pe.wait_ge(xT_dve, 3)
            pe.wait_ge(xT_act, 2)
            pe.wait_ge(wdt_loaded, 16)
            for k in range(KD):
                mm = pe.matmul(ps[0:HEADS, 4, 0:T], wdt[:, k, :], xnT[:, k, :],
                               start=(k == 0), stop=(k == KD - 1))
            mm.then_inc(dt_ps, 1)

            def w_in_block(b, bank):
                slot, ready = b % 2, b + 1
                pe.wait_ge(hi_ready, ready * 2)
                for s in range(2):
                    dst = ps[:, bank, s * T:s * T + T]
                    for k in range(KD):
                        w = whi[:, slot, k * BLK + s * P:k * BLK + s * P + P]
                        pe.matmul(dst, w, xg_hi[:, k, :], start=(k == 0), stop=False)
                        pe.matmul(dst, w, xg_lo[:, k, :], start=False, stop=False)
                    if s == 0:
                        pe.wait_ge(lo_dve, ready)
                        pe.wait_ge(lo_pool, ready)
                    for k in range(KD):
                        w = wlo[:, slot, k * BLK + s * P:k * BLK + s * P + P]
                        mm = pe.matmul(dst, w, xg_hi[:, k, :], start=False, stop=(k == KD - 1))
                mm.then_inc(blk_done, 1)

            pe.wait_ge(xhi_ready, 2)
            pe.wait_ge(xlo_ready, 2)
            for b in range(A_BLOCKS):
                if b >= 4:
                    pe.wait_ge(conv_sum, b - 3)
                w_in_block(b, b % 4)
                if b == 0:
                    pe.wait_ge(dtT_ready, 1)
                    for t in range(TT):
                        mm = pe.transpose(ps[:, 4, T + t * HEADS:T + t * HEADS + HEADS],
                                          dtT[0:HEADS, t * P:t * P + P], ident[0:HEADS, 0:HEADS])
                    mm.then_inc(dt_ps, 1)
                if b == 1:
                    pe.wait_ge(adt_ready, 1)
                    pe.matmul(ps[:, 5, 0:TT * HEADS], upto[:, :], adt, start=True, stop=True)
                    pe.matmul(ps[:, 5, 32:48], after[:, :], adt[:, 0:HEADS], start=True, stop=True)
                    for c in range(TT):
                        mm = pe.matmul(ps[0:HEADS, 5, 64 + c * P:64 + c * P + P],
                                       adt[:, c * HEADS:c * HEADS + HEADS], upto[:, :], start=True, stop=True)
                    mm.then_inc(acum_ps, 1)

            def b_turn(q):
                for j in range(4):
                    b = A_BLOCKS + 4 * q + j
                    if q == 0:
                        pe.wait_ge(conv_sum, b - 3)
                    else:
                        pe.wait_ge((zs_ready, gc_ready, prod_ready, sc_ready)[j], q)
                    w_in_block(b, b % 4)

            b_turn(0)
            pe.wait_ge(acumT_ready, 1)
            pe.wait_ge(xbc_ready, A_BLOCKS)
            for c in range(TT):
                for k in range(KD):
                    mm = pe.transpose(ps[:, 4 + 2 * c + k // 4, (k % 4) * P:(k % 4) * P + P],
                                      xs[:, k, c * P:c * P + P], ident[:, :])
                    if k % 4 == 3:
                        mm.then_inc(xs_tok_ps, 1)
            b_turn(1)
            pe.wait_ge(xdt_ready, 1)
            for c in range(TT):
                for g in range(GROUPS):
                    mm = pe.matmul(ps[:, 4, (c * GROUPS + g) * P:(c * GROUPS + g) * P + P],
                                   bcT[:, g, c * P:c * P + P], bcT[:, 2 + g, c * P:c * P + P],
                                   start=True, stop=True)
            mm.then_inc(cb_ps, 1)
            pe.wait_ge(xdt_ready, 2)
            for g in range(GROUPS):
                mm = pe.transpose(ps[:, 5, g * NSTATE:g * NSTATE + NSTATE], bcT[:, g, 0:P], ident[:, :])
            mm.then_inc(cb_ps, 1)
            b_turn(2)

            pe.wait_ge(xdd_ready, 1)
            pe.wait_ge(btok_ready, 1)
            pe.wait_ge(xdt_ready, 4)
            for g in range(GROUPS):
                mm = pe.matmul(ps[:, 6 + g, :], btok[:, g * NSTATE:g * NSTATE + NSTATE],
                               xdd[:, g * 512:g * 512 + 512], start=True, stop=True)
            mm.then_inc(state_ps, 1)
            b_turn(3)
            pe.wait_ge(cb_taken, 1)
            pe.wait_ge(mt_ready, 6)
            def heads(q):
                for s in range(2):
                    e = 2 * q + s
                    yield e, slice(e * HDIM, e * HDIM + HDIM), slice(s * HDIM, s * HDIM + HDIM)

            pe.wait_ge(state_ready, 1)
            for q in range(KD):
                bank, at_col = 4 + q // 2, (q % 2) * T
                for e, cols, rows_ in heads(q):
                    pe.matmul(ps[rows_, bank, at_col:at_col + P], xdt[:, 0, cols], mt[:, 0, e, :],
                              start=True, stop=True)
                for e, cols, rows_ in heads(q):
                    pe.matmul(ps[rows_, bank, at_col + P:at_col + T], xdt[:, 1, cols], mt[:, 1, e, :],
                              start=True, stop=False)
                for e, cols, rows_ in heads(q):
                    mm = pe.matmul(ps[rows_, bank, at_col + P:at_col + T], state[:, cols], cs[:, e, :],
                                   start=False, stop=True)
                if q % 2:
                    mm.then_inc(y_ps, 1)

            def bias(g, banks, last_bank=3):
                pe.wait_ge(sele_ready, g + 1)
                for n in banks:
                    mm = pe.matmul(ps[:, n, :], sele[0:2 * E, :], bgu_parts[0:2 * E, n * 512:n * 512 + 512], start=True,
                                   stop=False, skip_group_check=True)
                if banks[-1] == last_bank:
                    mm.then_inc(bias_made, 1)

            def hT_half(n, m):
                t, half = 1 - n, 1 - m
                pe.wait_ge(mix_taken, 8 + 2 * n + m + 1)
                for k in range(4):
                    c = (4 * half + k) * P
                    mm = pe.transpose(ps[:, 4 + 2 * n + m, k * P:k * P + P], h[:, t, c:c + P], ident[:, :])
                mm.then_inc(hT_ps, 1)

            def logits(n, halves_):
                t = 1 - n
                for m in halves_:
                    if n == 1 and m == 1:
                        pe.wait_ge(hT_act, 1)
                    else:
                        pe.wait_ge(hT_dve, 2 * n + m + 1)
                    for kk in range(4):
                        k = 4 * (1 - m) + kk
                        mm = pe.matmul(ps[:, 4 + 2 * n, 0:E], hT[:, t, k, :], wr[:, k, :],
                                       start=(m == 0 and kk == 0), stop=(m == 1 and kk == 3))
                return mm

            def out_products(b, src_hi, src_lo, tile, t, half, bank, first, last):
                dst = ps[:, bank, :]
                cols = [kk * 1024 + half * 512 for kk in range(2)]
                tok = slice(t * P, t * P + P)
                for kk in range(2):
                    w = whi[:, b % 2, cols[kk]:cols[kk] + 512]
                    pe.matmul(dst, src_hi[:, tile + kk, tok], w, start=(first and kk == 0), stop=False)
                    pe.matmul(dst, src_lo[:, tile + kk, tok], w, start=False, stop=False)
                for kk in range(2):
                    w = wlo[:, b % 2, cols[kk]:cols[kk] + 512]
                    mm = pe.matmul(dst, src_hi[:, tile + kk, tok], w, start=False, stop=(last and kk == 1))
                return mm

            def wait_parts(b):
                pe.wait_ge(hi_ready, 2 * b + 2)
                pe.wait_ge(lo_dve, b + 1)
                pe.wait_ge(lo_pool, b + 1)

            def square_sums():
                pe.wait_ge(sc_summed, B_TURNS)
                pe.wait_ge(g_summed, GROUPS)
                pe.wait_ge(g_ready, 4)
                for n, src in enumerate((sq_sc, sq_ssd[:, 0, :], sq_ssd[:, 4, :])):
                    for t in range(TT):
                        mm = pe.matmul(ps[:, 4, TT * n + t:TT * n + t + 1], src[:, t * P:t * P + P],
                                       ones[:, 0:1], start=True, stop=True)
                mm.then_inc(ms_ps, 1)

            def out_group(blocks, src_hi, src_lo, tile0, bank0):
                for n, i in enumerate(blocks):
                    final = n == len(blocks) - 1
                    wait_parts(LAST + i)
                    for r in range(4):
                        t, half = divmod(3 - r, 2)
                        mm = out_products(LAST + i, src_hi, src_lo, tile0 + 2 * n, t, half, bank0 + 3 - r,
                                          n == 0, final)
                        if final:
                            mm.then_inc(mix_ps, 1)
                    if not final:
                        mm.then_inc(blk_done, 1)
                    if blocks[0] == 0 and n == 1:
                        square_sums()

            pe.wait_ge(sc_lo_ready, 2 * B_TURNS)
            out_group(range(0, 4), gsc_hi, gsc_lo, 0, 0)
            pe.wait_ge(g_lo_ready, 4)
            pe.wait_ge(ms_ready, 2)
            out_group(range(4, 6), xg_hi, xg_lo, 0, 4)
            pe.wait_ge(mix_taken, 4)
            pe.wait_ge(moe_params, 64)
            pe.wait_ge(wr_ready, 1)
            last = [LAST + 6, LAST + 7]
            for n, r in ((0, 0), (0, 1), (0, 2), (1, 0), (1, 1), (1, 2), (0, 3), (1, 3)):
                t, half = divmod(3 - r, 2)
                if r == 0:
                    wait_parts(last[n])
                mm = out_products(last[n], xg_hi, xg_lo, 4 + 2 * n, t, half, 3 - r, n == 0, n == 1)
                if n == 1:
                    mm.then_inc(mix_ps, 1)
                if (n, r) == (0, 3):
                    hT_half(0, 0)
                    hT_half(0, 1)
                    hT_half(1, 0)
                    logits(0, (0, 1)).then_inc(logit_ps, 1)
                    logits(1, (0,))
            pe.wait_ge(bias_parts_ready, len(BIAS_PIECES))
            bias(0, (2,))
            hT_half(1, 1)
            bias(0, (3,), None)
            logits(1, (1,)).then_inc(logit_ps, 1)
            bias(0, (0,))
            pe.wait_ge(mask_ready, 2)
            pe.matmul(ps[:, 6, 0:TT * E], before[:, :], masks, start=True, stop=False)
            pe.matmul(ps[:, 6, E:2 * E], ones[:, :], mask[:, 0, :], start=False, stop=True).then_inc(pos_ps, 1)
            pe.matmul(ps[:, 7, 0:TT * E], ones[:, :], masks, start=True, stop=True).then_inc(pos_ps, 1)
            def gather(g, n, tiles=None):
                if n == 0:
                    pe.wait_ge(sel_ready, g + 1)
                elif n == 1:
                    pe.wait_ge(xsel_ready, tiles + 1)
                for k in range(KD)[GATHER_PARTS[n]]:
                    for t in range(TT):
                        mm = pe.matmul(ps[:, 4 + k // 4, (k % 4) * P:(k % 4) * P + P],
                                       x2[:, t, k * P:k * P + P], sel[:, t, :], start=(t == 0), stop=(t == TT - 1))
                mm.then_inc(gather_ps, 1)

            def halves(bank, lhs, w, first, last):
                for a in range(2):
                    mm = pe.matmul(ps[a * 64:a * 64 + 64, bank, :], lhs[:, a * 64:a * 64 + 64], w[a],
                                   start=first, stop=last, skip_group_check=True)
                    yield mm

            def item(i, g, t, u, last_of=None):
                def chunk_pair(step):
                    c = u * CHUNKS + 2 * step
                    slots_ = []
                    for a in range(2):
                        if c + a == 0 and isinstance(t, int) and t == 0:
                            pe.wait_ge(chunk0_full, 16)
                            slots_.append(chunk0)
                            continue
                        slot = (c + a - 1) % RING
                        pe.wait_ge(ring_full[slot], t * 48 + 16 * ((c + a - 1) // RING + 1))
                        slots_.append(ring[:, slot, :])
                    return slots_

                for step in range(4):
                    w = [s.rearrange("p (k n) -> p k n", k=2) for s in chunk_pair(step)]
                    if step < 3:
                        pe.wait_ge(xsel_ready, i * 2 + g + (step + 1))
                    for n in range(4):
                        for kk in range(2):
                            k = 2 * step + kk
                            for mm in halves(n, xsel[:, k, :], [v[:, kk, n * 512:n * 512 + 512] for v in w],
                                             False, k == KD - 1):
                                if kk == 1 and n == 3:
                                    mm.then_inc(chunk_done, 1)
                        if step == 3 and n == 1:
                            mm.then_inc(gate_ps, 1)
                    if step == 0:
                        gather(g, 1, i * 2 + g)
                    elif step == 1:
                        gather(g, 2)
                for n in range(2):
                    pe.matmul(ps[:, 6 + n, :], sele[0:2 * E, :], bdn_parts[0:2 * E, n * 512:n * 512 + 512], start=True,
                              stop=False, skip_group_check=True)
                for n in range(2):
                    pe.wait_ge(hid_ready, i * 2 + (n + 1))
                    for f in range(4):
                        mm = pe.transpose(ps[:, n, f * P:f * P + P], hid[:, (4 * n + f) * P:(4 * n + f) * P + P],
                                          ident[:, :])
                    mm.then_inc(hidT_ps, 1)
                pe.wait_ge(selg_ready, i + 1)
                for tt in range(TT):
                    mm = pe.transpose(ps[:, 2, tt * P:tt * P + P], selg[:, tt, :], ident[:, :])
                mm.then_inc(gT_ps, 1)
                for step in range(2):
                    c = u * CHUNKS + 8 + 2 * step
                    parts = 2 if step == 1 and last_of is not None else 1
                    if parts == 1:
                        w = chunk_pair(4 + step)
                    pe.wait_ge(hidT_ready, i * 2 + (step + 1))
                    for part_ in range(parts):
                        if parts == 2:
                            if part_ == 0:
                                pe.wait_ge(last_half, last_of * 32 + 32)
                                w = [ring[:, (c + a - 1) % RING, :] for a in range(2)]
                            else:
                                w = chunk_pair(4 + step)
                        v = [x_.rearrange("p (k n) -> p k n", k=4) for x_ in w]
                        kks = range(4 * part_ // parts, 4 * (part_ + 1) // parts)
                        for n in range(2):
                            for kk in kks:
                                f = 4 * step + kk
                                for mm in halves(6 + n, hidT[:, f, :], [x_[:, kk, n * 512:n * 512 + 512] for x_ in v],
                                                 False, f == KD - 1):
                                    if kk == 3 and n == 1:
                                        mm.then_inc(chunk_done, 1)
                            if step == 1 and n == 0 and part_ == parts - 1:
                                mm.then_inc(down_ps, 1)
                pe.wait_ge(gT_ready, i + 1)
                for n in range(4):
                    half, tt = divmod(n, 2)
                    if tt == 0:
                        pe.wait_ge(oute_ready, i * 2 + (half + 1))
                    pe.matmul(ps[:, ADD_BANKS[n], :], gT[:, tt, :], oute[:, half * 512:half * 512 + 512],
                              start=True, stop=True).then_inc(add_ps, 1)
                bias(g + 1, (0, 1))
                gather(g + 1, 0)
                pe.wait_ge(add_taken, i + 1)
                bias(g + 1, (2, 3))

            def expert_pass(rnd):
                g0, i0, t0 = rnd * (PAIRS + 1), rnd * PAIRS, rnd * (PAIRS // 2)
                if not isinstance(rnd, int):
                    bias(g0, range(4))
                gather(g0, 0)
                if isinstance(rnd, int):
                    bias(g0, (1,), 1)
                if isinstance(rnd, int):
                    for u in range(2):
                        item(u, u, 0, u)
                with pe.Fori(1 if isinstance(rnd, int) else 0, PAIRS // 2 - 1) as t:
                    for u in range(2):
                        item(i0 + t * 2 + u, g0 + t * 2 + u, t0 + t, u)
                t = PAIRS // 2 - 1
                for u in range(2):
                    item(i0 + (t * 2 + u), g0 + (t * 2 + u), t0 + t, u, last_of=rnd if u else None)

            pe.wait_ge(x2_ready, 2)
            expert_pass(0)
            with pe.If(flag_set(pe)):
                with pe.Fori(1, ROUNDS) as rnd:
                    expert_pass(rnd)


_INS = ['x', 'norm1_w', 'w_in', 'ssd_conv_w', 'ssd_conv_b', 'dt_bias', 'a_log', 'd_skip', 'ssd_norm_w',
        'sc_conv_w', 'sc_norm_w', 'w_out', 'norm2_w', 'w_router', 'b_router', 'w_gate_up', 'b_gate_up',
        'w_down', 'b_down', 'final_norm_w']


def kernel(**inputs):
    import numpy as _np
    import concourse.bacc as _bacc
    from concourse import mybir as _mybir
    from concourse.bass_utils import run_bass_kernel_spmd as _run

    nc = _bacc.Bacc("TRN2", target_bir_lowering=False, num_devices=1)
    arrays, args = {}, []
    for name in _INS:
        a = _np.ascontiguousarray(inputs[name])
        if name != 'final_norm_w':
            a = a.reshape(a.shape[1:])
        arrays[f"in_{name}"] = a
        args.append(nc.dram_tensor(f"in_{name}", a.shape, _mybir.dt.from_np(a.dtype), kind="ExternalInput").ap())
    out = nc.dram_tensor("out", (256, 1024), _mybir.dt.float32, kind="ExternalOutput").ap()
    hybrid_layer(nc, *args, out)
    r = _run(nc, [arrays], core_ids=[0])
    return r.results[0]["out"].reshape(1, 256, 1024)
```
